# Optimizing a Trainium2 kernel written in Bass

```python
import math
import jax, jax.numpy as jnp
from jax import lax
import numpy as np

D_MODEL = 1024
BATCH = 1
SEQ = 256
DEPTH = 2

GRID_W = 64
N_Q_HEADS = 8
N_KV_HEADS = 2
HEAD_DIM = 64
Q_BLOCK = 128
ROPE_THETA = 10000.0
ATTN_WIDTH = N_Q_HEADS * HEAD_DIM
KV_WIDTH = N_KV_HEADS * HEAD_DIM
SGU_GROUPS = 8
SGU_WIDTH = 512
SGU_GROUP_DIM = SGU_WIDTH // SGU_GROUPS
SGU_CHUNK = 128
Q_END = ATTN_WIDTH
K_END = Q_END + KV_WIDTH
V_END = K_END + KV_WIDTH
Z_END = V_END + 2 * SGU_WIDTH
GA_END = Z_END + D_MODEL
IN_COLS = GA_END + D_MODEL
N_EXPERTS = 64
TOP_K = 8
N_GROUPS = 8
TOPK_GROUPS = 4
EXPERT_FF = 256
SHARED_FF = 256
ROUTED_SCALE = 2.5
MOE_BLOCK = 128
ALPHA = (2 * DEPTH) ** 0.25
BETA = (8 * DEPTH) ** -0.25


def layer_norm(x, g, b, eps=1e-5):
    xf = x.astype(jnp.float32)
    mu = jnp.mean(xf, -1, keepdims=True)
    var = jnp.mean(jnp.square(xf - mu), -1, keepdims=True)
    return ((xf - mu) * lax.rsqrt(var + eps)).astype(x.dtype) * g + b

def rms_norm(x, g, eps=1e-6):
    xf = x.astype(jnp.float32)
    return (xf * lax.rsqrt(jnp.mean(jnp.square(xf), -1, keepdims=True) + eps)).astype(x.dtype) * g

def axial_rope_tables(seq_len, rows):
    t = jnp.arange(seq_len)
    row = (t // GRID_W - rows // 2).astype(jnp.float32)
    col = (t % GRID_W - GRID_W // 2).astype(jnp.float32)
    n_pairs = HEAD_DIM // 4
    inv_freq = ROPE_THETA ** (-jnp.arange(n_pairs, dtype=jnp.float32) / n_pairs)
    ang = jnp.concatenate([row[:, None] * inv_freq, col[:, None] * inv_freq], -1)
    return jnp.cos(ang), jnp.sin(ang)

def apply_rope(x, cos, sin):
    xf = x.astype(jnp.float32).reshape(*x.shape[:-1], HEAD_DIM // 2, 2)
    x0, x1 = xf[..., 0], xf[..., 1]
    c = cos[None, :, None, :]
    s = sin[None, :, None, :]
    out = jnp.stack([x0 * c - x1 * s, x0 * s + x1 * c], -1)
    return out.reshape(x.shape).astype(x.dtype)

def attention_branch(q, k, v, q_scale, k_scale, cos, sin):
    B, S = q.shape[:2]
    grp = N_Q_HEADS // N_KV_HEADS
    q = apply_rope(rms_norm(q, q_scale), cos, sin)
    k = apply_rope(rms_norm(k, k_scale), cos, sin)
    nqb = S // Q_BLOCK
    qb = q.reshape(B, nqb, Q_BLOCK, N_KV_HEADS, grp, HEAD_DIM).transpose(1, 0, 3, 4, 2, 5)
    kt = k.transpose(0, 2, 1, 3)
    vt = v.transpose(0, 2, 1, 3)
    scale = HEAD_DIM ** -0.5

    def attend(q_blk):
        s = jnp.einsum('bkgqd,bksd->bkgqs', q_blk, kt).astype(jnp.float32) * scale
        p = jax.nn.softmax(s, axis=-1).astype(vt.dtype)
        return jnp.einsum('bkgqs,bksd->bkgqd', p, vt)

    o = lax.map(attend, qb)
    return o.transpose(1, 0, 4, 2, 3, 5).reshape(B, S, ATTN_WIDTH)

def spatial_gating_branch(z, ln_g, ln_b, w_s, b_s):
    B, S, _ = z.shape
    z = jax.nn.gelu(z, approximate=False)
    u, v = z[..., :SGU_WIDTH], z[..., SGU_WIDTH:]
    v = layer_norm(v, ln_g, ln_b)
    vc = v.reshape(B, S // SGU_CHUNK, SGU_CHUNK, SGU_GROUPS, SGU_GROUP_DIM)
    sv = jnp.einsum('gij,bnjgd->bnigd', w_s, vc) + b_s.T[:, :, None]
    return u * sv.reshape(B, S, SGU_WIDTH)

def token_mixer(h, w_in, q_scale, k_scale, sgu_ln_g, sgu_ln_b, w_s, b_s, w_branch_a, w_branch_b, w_out, cos, sin):
    B, S, _ = h.shape
    p = h @ w_in
    q = p[..., :Q_END].reshape(B, S, N_Q_HEADS, HEAD_DIM)
    k = p[..., Q_END:K_END].reshape(B, S, N_KV_HEADS, HEAD_DIM)
    v = p[..., K_END:V_END].reshape(B, S, N_KV_HEADS, HEAD_DIM)
    z = p[..., V_END:Z_END]
    gate_a = p[..., Z_END:GA_END]
    gate_b = p[..., GA_END:]
    o_a = attention_branch(q, k, v, q_scale, k_scale, cos, sin)
    o_b = spatial_gating_branch(z, sgu_ln_g, sgu_ln_b, w_s, b_s)
    y = jax.nn.sigmoid(gate_a) * (o_a @ w_branch_a) + jax.nn.sigmoid(gate_b) * (o_b @ w_branch_b)
    return y @ w_out

def moe_ffn(h, router_w, router_bias, w_gate, w_up, w_down, ws_gate, ws_up, ws_down):
    B, S, D = h.shape
    T = B * S
    xt = h.reshape(T, D)
    scores = jax.nn.sigmoid((xt @ router_w).astype(jnp.float32))
    sel = scores + router_bias.astype(jnp.float32)
    per_group = N_EXPERTS // N_GROUPS
    group_score = lax.top_k(sel.reshape(T, N_GROUPS, per_group), 2)[0].sum(-1)
    _, gidx = lax.top_k(group_score, TOPK_GROUPS)
    gmask = jnp.any(gidx[..., None] == jnp.arange(N_GROUPS), axis=-2)
    emask = jnp.repeat(gmask, per_group, axis=-1)
    _, eidx = lax.top_k(jnp.where(emask, sel, -jnp.inf), TOP_K)
    wts = jnp.take_along_axis(scores, eidx, -1)
    wts = wts / jnp.sum(wts, -1, keepdims=True) * ROUTED_SCALE
    A = T * TOP_K
    e_flat = eidx.reshape(A)
    t_flat = jnp.repeat(jnp.arange(T, dtype=jnp.int32), TOP_K)
    w_flat = wts.reshape(A)
    order = jnp.argsort(e_flat)
    e_s, t_s, w_s = e_flat[order], t_flat[order], w_flat[order]
    counts = jnp.bincount(e_flat, length=N_EXPERTS)
    starts = jnp.cumsum(counts) - counts
    padded = (counts + MOE_BLOCK - 1) // MOE_BLOCK * MOE_BLOCK
    pends = jnp.cumsum(padded)
    pstarts = pends - padded
    dest = pstarts[e_s] + (jnp.arange(A) - starts[e_s])
    n_blocks = A // MOE_BLOCK + N_EXPERTS
    P = n_blocks * MOE_BLOCK
    tok_buf = jnp.full((P,), T, jnp.int32).at[dest].set(t_s.astype(jnp.int32))
    w_buf = jnp.zeros((P,), xt.dtype).at[dest].set(w_s.astype(xt.dtype))
    blk_expert = jnp.minimum(jnp.searchsorted(pends, jnp.arange(n_blocks) * MOE_BLOCK, side='right'), N_EXPERTS - 1)
    x_pad = jnp.concatenate([xt, jnp.zeros((1, D), xt.dtype)], 0)

    def run_block(args):
        e, toks, ws = args
        xb = x_pad[toks]
        hb = jax.nn.silu(xb @ w_gate[e]) * (xb @ w_up[e])
        return (hb @ w_down[e]) * ws[:, None]

    yb = lax.map(run_block, (blk_expert, tok_buf.reshape(n_blocks, MOE_BLOCK), w_buf.reshape(n_blocks, MOE_BLOCK)))
    routed = jax.ops.segment_sum(yb.reshape(P, D), tok_buf, num_segments=T + 1)[:T]
    shared = (jax.nn.silu(xt @ ws_gate) * (xt @ ws_up)) @ ws_down
    return (routed + shared).reshape(B, S, D)

def first_inputs(seed: int = 0) -> dict:
    key = jax.random.key(seed)
    ks = jax.random.split(key, 26)
    L, D, E = DEPTH, D_MODEL, N_EXPERTS
    f32 = jnp.float32

    def nrm(k, shape, s):
        return jax.random.normal(k, shape, f32) * s

    def gain(k, shape):
        return 1.0 + 0.02 * jax.random.normal(k, shape, f32)

    w_in = nrm(ks[4], (L, D, IN_COLS), D ** -0.5)
    w_in = w_in.at[:, :, K_END:V_END].multiply(BETA)
    return {
        'x': nrm(ks[0], (BATCH, SEQ, D), 1.0),
        'c': nrm(ks[1], (BATCH, D), 1.0),
        'w_ada': nrm(ks[2], (L, D, 6 * D), 0.5 * D ** -0.5),
        'b_ada': nrm(ks[3], (L, 6 * D), 0.02),
        'w_in': w_in,
        'q_scale': gain(ks[5], (L, HEAD_DIM)),
        'k_scale': gain(ks[6], (L, HEAD_DIM)),
        'sgu_ln_g': gain(ks[7], (L, SGU_WIDTH)),
        'sgu_ln_b': nrm(ks[8], (L, SGU_WIDTH), 0.02),
        'w_spatial': nrm(ks[9], (L, SGU_GROUPS, SGU_CHUNK, SGU_CHUNK), SGU_CHUNK ** -0.5),
        'b_spatial': nrm(ks[10], (L, SGU_GROUPS, SGU_CHUNK), 0.02),
        'w_branch_a': nrm(ks[11], (L, ATTN_WIDTH, D), ATTN_WIDTH ** -0.5),
        'w_branch_b': nrm(ks[12], (L, SGU_WIDTH, D), SGU_WIDTH ** -0.5),
        'w_out': nrm(ks[13], (L, D, D), BETA * D ** -0.5),
        'ln1_g': gain(ks[14], (L, D)),
        'ln1_b': nrm(ks[15], (L, D), 0.02),
        'router_w': nrm(ks[16], (L, D, E), D ** -0.5),
        'router_bias': nrm(ks[17], (L, E), 0.01),
        'w_gate': nrm(ks[18], (L, E, D, EXPERT_FF), D ** -0.5),
        'w_up': nrm(ks[19], (L, E, D, EXPERT_FF), D ** -0.5),
        'w_down': nrm(ks[20], (L, E, EXPERT_FF, D), BETA * EXPERT_FF ** -0.5),
        'ws_gate': nrm(ks[21], (L, D, SHARED_FF), D ** -0.5),
        'ws_up': nrm(ks[22], (L, D, SHARED_FF), D ** -0.5),
        'ws_down': nrm(ks[23], (L, SHARED_FF, D), BETA * SHARED_FF ** -0.5),
        'ln2_g': gain(ks[24], (L, D)),
        'ln2_b': nrm(ks[25], (L, D), 0.02),
    }

def first_block(x, c, w_ada, b_ada, w_in, q_scale, k_scale, sgu_ln_g, sgu_ln_b, w_spatial, b_spatial,
              w_branch_a, w_branch_b, w_out, ln1_g, ln1_b, router_w, router_bias, w_gate, w_up, w_down,
              ws_gate, ws_up, ws_down, ln2_g, ln2_b):
    B, S, D = x.shape
    rows = S // GRID_W
    cos, sin = axial_rope_tables(S, rows)
    cond = jax.nn.silu(c)
    for l in range(DEPTH):
        mod = cond @ w_ada[l] + b_ada[l]
        shift1, scale1, gate1, shift2, scale2, gate2 = jnp.split(mod[:, None, :], 6, axis=-1)
        h = x * (1 + scale1) + shift1
        y = token_mixer(h, w_in[l], q_scale[l], k_scale[l], sgu_ln_g[l], sgu_ln_b[l], w_spatial[l], b_spatial[l],
                        w_branch_a[l], w_branch_b[l], w_out[l], cos, sin)
        x = layer_norm(ALPHA * x + gate1 * y, ln1_g[l], ln1_b[l])
        h = x * (1 + scale2) + shift2
        y = moe_ffn(h, router_w[l], router_bias[l], w_gate[l], w_up[l], w_down[l], ws_gate[l], ws_up[l], ws_down[l])
        x = layer_norm(ALPHA * x + gate2 * y, ln2_g[l], ln2_b[l])
    return x


D_A = D_MODEL // 2
HEAD_A = 64
N_HEADS_A = D_A // HEAD_A
LORA_DECAY = 64
LORA_ICLR = 64
LORA_GATE = 128
N_DIR = 2
C_RWKV = 3 * D_A + N_DIR * LORA_DECAY + N_DIR * LORA_ICLR + LORA_GATE
RWKV_SPLITS = [D_A, 2 * D_A, 3 * D_A, 3 * D_A + N_DIR * LORA_DECAY,
               3 * D_A + N_DIR * LORA_DECAY + N_DIR * LORA_ICLR]
DECAY_SCALE = math.exp(-0.5)
GN_EPS = 64e-5
HEAD_B = 64
D_B = D_MODEL // 2
N_HEADS_B = D_B // (2 * HEAD_B)
C_ATTN = 3 * D_B
ALIBI_MAX_EXP = 8.0
N_BRANCH = 2
C_IN = C_RWKV + C_ATTN + N_BRANCH * D_MODEL
D_FF = ((8 * D_MODEL // 3 + 127) // 128) * 128
NORM_EPS = 1e-6


def rms_norm_2(x, g, eps=NORM_EPS):
    xf = x.astype(jnp.float32)
    y = xf * lax.rsqrt(jnp.mean(xf * xf, axis=-1, keepdims=True) + eps)
    return (y * g.astype(jnp.float32)).astype(x.dtype)

def swiglu(h, w_in, w_out):
    gate, up = jnp.split(h @ w_in, 2, axis=-1)
    return (jax.nn.silu(gate) * up) @ w_out

def centred_shift(p):
    prev = jnp.pad(p[:, :-1], ((0, 0), (1, 0), (0, 0)))
    nxt = jnp.pad(p[:, 1:], ((0, 0), (0, 1), (0, 0)))
    return 0.5 * (prev + nxt)

def to_heads(t, n_heads):
    return t.reshape(t.shape[:-1] + (n_heads, t.shape[-1] // n_heads))

def rwkv7_scan(r, w, k, v, kk, a, reverse):
    b, s, h, n = r.shape
    xs = tuple(jnp.moveaxis(t.astype(jnp.float32), 1, 0) for t in (r, w, k, v, kk, a))

    def step(state, inp):
        r_t, w_t, k_t, v_t, kk_t, a_t = inp
        sa = jnp.einsum('bhvk,bhk->bhv', state, -kk_t)
        state = (state * w_t[:, :, None, :]
                 + sa[..., None] * (kk_t * a_t)[:, :, None, :]
                 + v_t[..., None] * k_t[:, :, None, :])
        y_t = jnp.einsum('bhvk,bhk->bhv', state, r_t)
        return state, y_t

    s0 = jnp.zeros((b, h, n, n), jnp.float32)
    _, ys = lax.scan(step, s0, xs, reverse=reverse)
    return jnp.moveaxis(ys, 0, 1)

def rwkv7_mixer(p, mu, w0, w2, a0, a2, g2, k_k, k_a, r_k, ln_g, ln_b):
    p = p + mu * (centred_shift(p) - p)
    r, k, v, dw, da, dg = jnp.split(p, RWKV_SPLITS, axis=-1)
    b, s, _ = r.shape
    dw = dw.reshape(b, s, N_DIR, LORA_DECAY)
    da = da.reshape(b, s, N_DIR, LORA_ICLR)
    decay = jnp.exp(-DECAY_SCALE * jax.nn.sigmoid(
        w0 + jnp.einsum('bsgr,grc->bsgc', jnp.tanh(dw), w2)))
    iclr = jax.nn.sigmoid(a0 + jnp.einsum('bsgr,grc->bsgc', da, a2))
    gate = jax.nn.sigmoid(dg) @ g2
    kk = to_heads(k * k_k, N_HEADS_A).astype(jnp.float32)
    kk = kk / jnp.maximum(jnp.sqrt(jnp.sum(kk * kk, axis=-1, keepdims=True)), 1e-12)
    k_dir = k[:, :, None, :] * (1.0 + (iclr - 1.0) * k_a)
    r_h = to_heads(r, N_HEADS_A)
    v_h = to_heads(v, N_HEADS_A)
    k_h = to_heads(k_dir, N_HEADS_A)
    w_h = to_heads(decay, N_HEADS_A)
    a_h = to_heads(iclr, N_HEADS_A)
    y = (rwkv7_scan(r_h, w_h[:, :, 0], k_h[:, :, 0], v_h, kk, a_h[:, :, 0], False)
         + rwkv7_scan(r_h, w_h[:, :, 1], k_h[:, :, 1], v_h, kk, a_h[:, :, 1], True))
    mean = jnp.mean(y, axis=-1, keepdims=True)
    var = jnp.mean(jnp.square(y - mean), axis=-1, keepdims=True)
    y = ((y - mean) * lax.rsqrt(var + GN_EPS)).reshape(b, s, D_A) * ln_g + ln_b
    bonus = jnp.einsum('bshn,bsghn,hn->bsh', r_h.astype(jnp.float32),
                       k_h.astype(jnp.float32), r_k.astype(jnp.float32))[..., None] * v_h
    return (y + bonus.reshape(b, s, D_A)) * gate

def diff_attention(p, q_gain, k_gain, lam_vecs, sub_g, lam_init):
    b, s, _ = p.shape
    q, k, v = jnp.split(p, 3, axis=-1)
    q = rms_norm_2(q.reshape(b, s, N_HEADS_B, 2, HEAD_B), q_gain)
    k = rms_norm_2(k.reshape(b, s, N_HEADS_B, 2, HEAD_B), k_gain)
    v = v.reshape(b, s, N_HEADS_B, 2 * HEAD_B)
    lv = lam_vecs.astype(jnp.float32)
    lam = jnp.exp(jnp.sum(lv[0] * lv[1])) - jnp.exp(jnp.sum(lv[2] * lv[3])) + lam_init
    n_blk = s // Q_BLOCK
    q_blk = q.reshape(b, n_blk, Q_BLOCK, N_HEADS_B, 2, HEAD_B).transpose(1, 0, 3, 4, 2, 5)
    k_t = k.transpose(0, 2, 3, 1, 4)
    v_t = v.transpose(0, 2, 1, 3)
    slopes = 2.0 ** (-ALIBI_MAX_EXP * jnp.arange(1, N_HEADS_B + 1, dtype=jnp.float32) / N_HEADS_B)
    k_pos = jnp.arange(s, dtype=jnp.float32)
    q_pos = k_pos.reshape(n_blk, Q_BLOCK)
    scale = HEAD_B ** -0.5

    def attend_block(args):
        qb, qp = args
        logits = jnp.einsum('bhmqd,bhmkd->bhmqk', qb, k_t,
                            preferred_element_type=jnp.float32) * scale
        bias = -slopes[:, None, None] * jnp.abs(qp[:, None] - k_pos[None, :])
        prob = jax.nn.softmax(logits + bias[None, :, None], axis=-1)
        attn = prob[:, :, 0] - lam * prob[:, :, 1]
        return jnp.einsum('bhqk,bhkc->bhqc', attn.astype(v_t.dtype), v_t)

    o = lax.map(attend_block, (q_blk, q_pos))
    o = o.transpose(1, 0, 3, 2, 4).reshape(b, s, N_HEADS_B, 2 * HEAD_B)
    o = rms_norm_2(o, sub_g) * (1.0 - lam_init)
    return o.reshape(b, s, D_B)

def second_inputs(seed: int = 0) -> dict:
    key = jax.random.key(seed)
    ks = iter(jax.random.split(key, 32))
    L = DEPTH

    def nrm(shape, scale):
        return jax.random.normal(next(ks), shape, jnp.float32) * scale

    def gain(shape):
        return 1.0 + nrm(shape, 0.02)

    return {
        'x': nrm((BATCH, SEQ, D_MODEL), 1.0),
        'norm_ffn1': gain((L, D_MODEL)),
        'ffn1_in': nrm((L, D_MODEL, 2 * D_FF), D_MODEL ** -0.5),
        'ffn1_out': nrm((L, D_FF, D_MODEL), D_FF ** -0.5),
        'norm_mix': gain((L, D_MODEL)),
        'w_in': nrm((L, D_MODEL, C_IN), D_MODEL ** -0.5),
        'rwkv_mu': jax.random.uniform(next(ks), (L, C_RWKV), jnp.float32),
        'decay_w0': nrm((L, N_DIR, D_A), 1.0),
        'decay_w2': nrm((L, N_DIR, LORA_DECAY, D_A), 0.5 * LORA_DECAY ** -0.5),
        'iclr_a0': nrm((L, N_DIR, D_A), 0.5),
        'iclr_a2': nrm((L, N_DIR, LORA_ICLR, D_A), 0.5 * LORA_ICLR ** -0.5),
        'gate_g2': nrm((L, LORA_GATE, D_A), LORA_GATE ** -0.5),
        'k_k': 0.85 + nrm((L, D_A), 0.05),
        'k_a': 1.0 + nrm((L, D_A), 0.05),
        'r_k': nrm((L, N_HEADS_A, HEAD_A), 0.1),
        'ln_x_g': gain((L, D_A)),
        'ln_x_b': nrm((L, D_A), 0.02),
        'q_gain': gain((L, HEAD_B)),
        'k_gain': gain((L, HEAD_B)),
        'diff_lambda': nrm((L, 4, HEAD_B), 0.1),
        'subln_g': gain((L, 2 * HEAD_B)),
        'w_branch': nrm((L, N_BRANCH, D_A, D_MODEL), D_A ** -0.5),
        'w_out': nrm((L, D_MODEL, D_MODEL), D_MODEL ** -0.5),
        'norm_ffn2': gain((L, D_MODEL)),
        'ffn2_in': nrm((L, D_MODEL, 2 * D_FF), D_MODEL ** -0.5),
        'ffn2_out': nrm((L, D_FF, D_MODEL), D_FF ** -0.5),
    }

def second_block(x, norm_ffn1, ffn1_in, ffn1_out, norm_mix, w_in, rwkv_mu, decay_w0, decay_w2,
              iclr_a0, iclr_a2, gate_g2, k_k, k_a, r_k, ln_x_g, ln_x_b, q_gain, k_gain,
              diff_lambda, subln_g, w_branch, w_out, norm_ffn2, ffn2_in, ffn2_out):
    b, s, d = x.shape
    for l in range(DEPTH):
        lam_init = 0.8 - 0.6 * math.exp(-0.3 * l)
        x = x + 0.5 * swiglu(rms_norm_2(x, norm_ffn1[l]), ffn1_in[l], ffn1_out[l])
        h = rms_norm_2(x, norm_mix[l])
        proj = h @ w_in[l]
        p_rwkv, p_attn, p_gate = jnp.split(proj, [C_RWKV, C_RWKV + C_ATTN], axis=-1)
        o_a = rwkv7_mixer(p_rwkv, rwkv_mu[l], decay_w0[l], decay_w2[l], iclr_a0[l],
                          iclr_a2[l], gate_g2[l], k_k[l], k_a[l], r_k[l],
                          ln_x_g[l], ln_x_b[l]).astype(x.dtype)
        o_b = diff_attention(p_attn, q_gain[l], k_gain[l], diff_lambda[l], subln_g[l],
                             lam_init).astype(x.dtype)
        branches = jnp.stack([o_a, o_b], axis=2)
        y = jnp.einsum('bsgc,gcd->bsgd', branches, w_branch[l])
        gates = jax.nn.sigmoid(p_gate.reshape(b, s, N_BRANCH, d))
        merged = jnp.sum(gates * y, axis=2)
        x = x + merged @ w_out[l]
        x = x + 0.5 * swiglu(rms_norm_2(x, norm_ffn2[l]), ffn2_in[l], ffn2_out[l])
    return x


def setup_inputs(seed=0):
    out = dict(first_inputs(seed))
    for name, value in second_inputs(seed + 1).items():
        if name != "x":
            out[name + "_2"] = value
    return out


def reference(
    x, c, w_ada, b_ada, w_in, q_scale, k_scale, sgu_ln_g, sgu_ln_b, w_spatial, b_spatial,
    w_branch_a, w_branch_b, w_out, ln1_g, ln1_b, router_w, router_bias, w_gate, w_up, w_down,
    ws_gate, ws_up, ws_down, ln2_g, ln2_b, norm_ffn1_2, ffn1_in_2, ffn1_out_2, norm_mix_2,
    w_in_2, rwkv_mu_2, decay_w0_2, decay_w2_2, iclr_a0_2, iclr_a2_2, gate_g2_2, k_k_2, k_a_2,
    r_k_2, ln_x_g_2, ln_x_b_2, q_gain_2, k_gain_2, diff_lambda_2, subln_g_2, w_branch_2,
    w_out_2, norm_ffn2_2, ffn2_in_2, ffn2_out_2,
):
    x = first_block(
        x, c, w_ada, b_ada, w_in, q_scale, k_scale, sgu_ln_g, sgu_ln_b, w_spatial, b_spatial,
        w_branch_a, w_branch_b, w_out, ln1_g, ln1_b, router_w, router_bias, w_gate, w_up,
        w_down, ws_gate, ws_up, ws_down, ln2_g, ln2_b,
    )
    return second_block(
        x, norm_ffn1_2, ffn1_in_2, ffn1_out_2, norm_mix_2, w_in_2, rwkv_mu_2, decay_w0_2,
        decay_w2_2, iclr_a0_2, iclr_a2_2, gate_g2_2, k_k_2, k_a_2, r_k_2, ln_x_g_2, ln_x_b_2,
        q_gain_2, k_gain_2, diff_lambda_2, subln_g_2, w_branch_2, w_out_2, norm_ffn2_2,
        ffn2_in_2, ffn2_out_2,
    )


_drawn_inputs = setup_inputs


def setup_inputs(seed=0):
    import zlib

    import numpy as np

    out = dict(_drawn_inputs(seed))
    spreads = {}
    factors = {'q_scale': 8.0,
     'k_scale': 8.0,
     'sgu_ln_g': 7.632,
     'sgu_ln_b': 8.0,
     'b_spatial': 8.0,
     'norm_ffn1_2': 3.84,
     'k_k_2': 27.564,
     'ln_x_g_2': 24.168,
     'ln_x_b_2': 20.463,
     'q_gain_2': 5.321,
     'k_gain_2': 5.486,
     'subln_g_2': 14.353,
     'norm_ffn2_2': 5.274}
    for name, (base, spread) in spreads.items():
        noise = np.random.default_rng([zlib.crc32(name.encode()), seed]).standard_normal(out[name].shape)
        drawn = base * np.exp(spread * noise) if base else spread * noise
        out[name] = __import__('jax').numpy.asarray(drawn.astype(out[name].dtype))
    for name, factor in factors.items():
        out[name] = (out[name] * factor).astype(out[name].dtype)
    return out
```

```python
import math
from contextlib import ExitStack

import numpy as np

import concourse.bass as bass
from concourse import mybir
from concourse.alu_op_type import AluOpType as ALU

ACT = mybir.ActivationFunctionType
F32 = mybir.dt.float32
AX = mybir.AxisListType.X

P = 128
D = 1024
S = 256
DT = D // P
MT = S // P
DEPTH = 2
BANK = 512
HD = 64

QH, KVH = 8, 2
QW, KVW = QH * HD, KVH * HD
QKW = QW + KVW
SGU = 512
SG = 8
SGD = SGU // SG
TOKC = QW + 2 * KVW + 2 * SGU
IN1 = TOKC + 2 * D
E, TOPK, NG, PG, KEEP_G = 64, 8, 8, 8, 4
FF = 256
ROUTED_SCALE = 2.5
ALPHA = (2 * DEPTH) ** 0.25
ADA = 6 * D
MODS = ADA // P
ROWS = MODS + SG + DT

RW = 512
RT = RW // P
LORA = 64
CRW = 3 * RW + 4 * LORA + P
CT = CRW // P
CAT = 3 * RW
IN2 = CRW + CAT + 2 * D
DFF = 2816
STEPS = DFF // FF
CH = 64
NCH = S // CH
DECAY = 0.6065306597126334
BH = 4

A_SLOTS, A_W = 4, 4096
B_SLOTS, B_W = 4, 2048
NEG = -3.0e38
TAKEN = -3.3e38


def spread(ap, axis, n):
    a = ap.unsqueeze(axis)
    shape = list(a.shape)
    shape[axis] = n
    return a.broadcast_to(shape)


class Banks:

    def __init__(self, tensors, filled, freed):
        self.t, self.filled, self.freed = tensors, filled, freed
        self.count = [0] * len(tensors)
        self.claims = [0] * len(tensors)
        self.uses = {}

    def take(self, key, bank):
        assert key not in self.uses, key
        self.uses[key] = (bank, self.count[bank])
        self.count[bank] += 1

    def claim(self, pe, key):
        b, n = self.uses[key]
        assert self.claims[b] == n, key
        self.claims[b] += 1
        if n:
            pe.wait_ge(self.freed[b], n)
        return self.t[b]

    def fill(self, ins, key):
        ins.then_inc(self.filled[self.uses[key][0]], 1)

    def read(self, eng, key):
        b, n = self.uses[key]
        eng.wait_ge(self.filled[b], n + 1)
        return self.t[b]

    def free(self, ins, key):
        ins.then_inc(self.freed[self.uses[key][0]], 1)

    def evacuated(self, eng, key):
        b, n = self.uses[key]
        eng.wait_ge(self.freed[b], n + 1)


class Chain:

    def __init__(self, eng, sem):
        self.eng, self.sem, self.n = eng, sem, 0

    def mark(self, ins):
        self.n += 1
        ins.then_inc(self.sem, 1)

    def __call__(self, ins):
        self.mark(ins)
        self.eng.wait_ge(self.sem, self.n)
        return ins


def first_block(nc, a, x_tok, consts):
    with ExitStack() as ctx:
        def sb(name, shape):
            return ctx.enter_context(nc.sbuf_tensor("f_" + name, shape, F32))

        def sem(name):
            return ctx.enter_context(nc.semaphore("f_" + name))

        ident, cosr, sinr, jlt = consts["ident"], consts["cos"], consts["sin"], consts["jlt"]

        ringA = sb("ringA", [P, A_SLOTS, A_W])
        ringB = sb("ringB", [P, B_SLOTS, B_W])
        hT = sb("hT", [P, DT, S])
        arena = sb("arena", [P, E * S])
        lnp = sb("lnp", [P, 2, D])
        gate_b = sb("gate_b", [P, D])
        silu_g = sb("silu_g", [P, 2, BANK])
        hid = sb("hid", [P, 2, BANK])
        rows = sb("rows", [ROWS, P])
        cols = sb("cols", [P, ROWS])
        mod = sb("mod", [P, MODS])
        modp1 = sb("modp1", [P, MODS])
        cond = sb("cond", [P, DT])
        qks = sb("qks", [P, 2, HD])
        rw = sb("rw", [P, DT, E])
        rbias = sb("rbias", [P, E])
        stats = sb("stats", [P, MT, 2, 6])
        mv = sb("mv", [P, MT, 2])
        small = sb("small", [P, 320])
        wT = sb("wT", [E, S])

        at = [0]

        def part(n):
            at[0] += n
            assert at[0] <= E * S, at
            return arena[:, at[0] - n:at[0]]

        p_tok = part(MT * TOKC).rearrange("p (m c) -> p m c", m=MT)
        gates = part(2 * DT * S).rearrange("p (t s) -> p t s", s=S)
        tmp = part(2560)
        turned = part(2304)
        qT = part(4 * S).rearrange("p (t s) -> p t s", s=S)
        kT = part(KVH * S).rearrange("p (t s) -> p t s", s=S)
        wsT = part(SG * P).rearrange("p (g i) -> p g i", g=SG)
        oaT = part(4 * S).rearrange("p (t s) -> p t s", s=S)
        obT = wsT.rearrange("p g i -> p (g i)").rearrange("p (t s) -> p t s", s=S)
        qkr = turned[:, 0:MT * QKW].rearrange("p (m c) -> p m c", m=MT)
        kdup = turned[:, MT * QKW:MT * QKW + MT * 4 * HD * 2]
        kdup = kdup.rearrange("p (m c) -> p m c", m=MT)
        yT = turned[:, 0:DT * S].rearrange("p (t s) -> p t s", s=S)
        v_ln = p_tok[:, :, 0:SGU]
        u0, v0 = QKW + KVW, QKW + KVW + SGU
        prob = tmp[:, 0:1024].rearrange("p (b m s) -> p b m s", b=2, m=MT)
        probT = tmp[:, 1024:2048].rearrange("p (b t s) -> p b t s", b=2, t=MT)
        router = tmp[:, 0:9 * MT * E].rearrange("p (n c) -> p n c", n=9)
        w_all = arena[:, :].rearrange("p (e s) -> p e s", s=S)
        ws_nat = hid[:, :, :].rearrange("p a b -> p (a b)").rearrange("p (g j) -> p g j", g=SG)
        sgu_ln = silu_g


        s_go = sem("layer_cleared")
        names = ["a_slot0", "a_slot1", "a_slot2", "a_slot3", "b_slot0", "b_slot1", "b_slot2",
                 "b_slot3", "wT_stored", "ada_chunks", "cond_ready", "mod_ready",
                 "rotated", "vln_ready", "gated_ready", "max_ready", "prob_ready", "merged", "var_ready",
                 "std_ready", "x_ready", "weights_ready", "hidden_ready", "down_done", "dve_steps", "arrived"]
        names += [f"bank_filled{i}" for i in range(8)] + [f"bank_freed{i}" for i in range(8)]
        each = {n: sem(n) for n in names}
        nums = [s.num for s in each.values()]
        cleared = range(min(nums), max(nums) + 1)
        assert len(cleared) == len(nums) and s_go.num not in cleared
        params_landed, ln1_landed, ln2_landed = sem("params_landed"), sem("ln1_landed"), sem("ln2_landed")
        w_all_landed = sem("w_all_landed")
        a_landed = [each[f"a_slot{i}"] for i in range(A_SLOTS)]
        b_landed = [each[f"b_slot{i}"] for i in range(B_SLOTS)]
        ada_chunks, mod_ready, rotated = each["ada_chunks"], each["mod_ready"], each["rotated"]
        vln_ready, gated_ready, max_ready = each["vln_ready"], each["gated_ready"], each["max_ready"]
        prob_ready, merged, var_ready = each["prob_ready"], each["merged"], each["var_ready"]
        std_ready, x_ready, weights_ready = each["std_ready"], each["x_ready"], each["weights_ready"]
        hidden_ready, down_done, dve_steps = each["hidden_ready"], each["down_done"], each["dve_steps"]
        wT_stored = each["wT_stored"]
        arrived, cond_ready = each["arrived"], each["cond_ready"]
        filled = [each[f"bank_filled{i}"] for i in range(8)]
        freed = [each[f"bank_freed{i}"] for i in range(8)]

        banks = Banks([ctx.enter_context(nc.psum_tensor(f"f_bank{i}", [P, BANK], F32)) for i in range(8)],
                      filled, freed)

        for b in range(4):
            banks.take(("xT", b), b)
        banks.take("cols", 5)
        banks.take("ada", 4)
        gemm = [("q", 0), ("q", 1), ("kv", 0), ("kv", 1), ("u", 0), ("u", 1), ("v", 0), ("v", 1)]
        gemm += [("gates", g) for g in range(8)]
        for n, key in enumerate(gemm):
            banks.take(key, n % 4)
        for g in range(2):
            banks.take(("wsT", g), 4 + g)
        for g in range(3):
            banks.take(("qkT", g), (6, 7, 4)[g])
        for m in range(MT):
            banks.take(("sv", m), m)
        for h in range(QH + 1):
            if h < QH:
                banks.take(("score", h), 4 + h % 2)
            if h:
                banks.take(("probT", h - 1), 6 + (h - 1) % 2)
                if h % 2:
                    banks.take(("oT", h // 2), 2 + (h // 2) % 2)
        for g in range(2):
            banks.take(("obT", g), g)
        for t in range(DT):
            banks.take(("branch", t), t % 4)
        for g in range(2):
            banks.take(("gate1", g), 4 + g)
        for n in range(2):
            for m in range(MT):
                banks.take(("out", n, m), 2 * n + m)
        for b in range(4):
            banks.take(("x2T", b), b)
        for g in range(2):
            banks.take(("gate2", g), 4 + g)
        banks.take("router", 6)
        banks.take(("g", "shared"), 4)
        banks.take(("u", "shared"), 5)
        for n in range(4):
            banks.take(("y", n), n)
        banks.take("wT", 7)
        first_turn = list(banks.count)

        n_ada, n_in = ADA // 512, 8
        a_in = n_ada
        a_wa, a_wb, a_out, a_shared = a_in + n_in, a_in + n_in + 1, a_in + n_in + 2, a_in + n_in + 4
        a_exp = a_shared + 1
        last_use = {a_in + c: (name, 1) for c, name in enumerate(("q", "kv", "u", "v"))}
        last_use[n_ada - 1] = "ada"
        last_use |= {a_in + 4 + c: ("gates", 2 * c + 1) for c in range(4)}
        last_use |= {a_wa: ("branch", DT - 1), a_wb: ("branch", DT - 1), a_out: ("out", 0, 1),
                     a_out + 1: ("out", 1, 1), a_shared: ("u", "shared")}

        def slotA(n):
            return ringA[:, n % A_SLOTS, :]

        def slotB(n):
            return ringB[:, n % B_SLOTS, :]

        def rows8(ap):
            return ap.rearrange("p (k c) -> p k c", k=DT)

        block = ctx.enter_context(nc.Block())

        def leave(eng, l):
            eng.nop().then_inc(arrived, 1)
            eng.wait_ge(s_go, l + 1)

        @block.sync
        def _(sp):
            with sp.Fori(0, DEPTH) as l:
                def slot_free(n):
                    old = n - A_SLOTS
                    if old in last_use:
                        banks.read(sp, last_use[old])
                    elif old >= 0:
                        sp.wait_ge(ada_chunks, old + 1)

                def load(n, dst, src):
                    slot_free(n)
                    half = dst.shape[1] // 2
                    for h in range(2):
                        sp.dma_start(dst[:, h * half:(h + 1) * half], src[:, h * half:(h + 1) * half]
                                     ).then_inc(a_landed[n % A_SLOTS], 16)

                for c in range(n_ada):
                    load(c, rows8(slotA(c)),
                         a["w_ada"][l, :, c * 512:(c + 1) * 512].rearrange("(k p) c -> p k c", p=P))
                edges = [0, QW, u0, v0, TOKC] + [TOKC + 512 * (i + 1) for i in range(4)]
                for c in range(n_in):
                    n, w = a_in + c, edges[c + 1] - edges[c]
                    load(n, rows8(slotA(n))[:, :, 0:w],
                         a["w_in"][l, :, edges[c]:edges[c + 1]].rearrange("(k p) c -> p k c", p=P))
                for n, name in ((a_wa, "w_branch_a"), (a_wb, "w_branch_b")):
                    load(n, slotA(n).rearrange("p (k c) -> p k c", k=4),
                         a[name][l].rearrange("(k p) c -> p k c", p=P))
                for c in range(2):
                    load(a_out + c, rows8(slotA(a_out + c)),
                         a["w_out"][l, :, c * 512:(c + 1) * 512].rearrange("(k p) c -> p k c", p=P))

                def gate_up_down(nA, nB, srcs):
                    gu = slotA(nA).rearrange("p (h k c) -> p h k c", h=2, k=DT)
                    for half in range(2):
                        sp.dma_start(gu[:, half], srcs[half].rearrange("(k p) c -> p k c", p=P)
                                     ).then_inc(a_landed[nA % A_SLOTS], 16)
                    yield
                    sp.dma_start(slotB(nB).rearrange("p (k c) -> p k c", k=2),
                                 srcs[2].rearrange("(k p) c -> p k c", p=P)
                                 ).then_inc(b_landed[nB % B_SLOTS], 16)
                    yield

                slot_free(a_shared)
                for _ in gate_up_down(a_shared, 0, [a[n][l] for n in ("ws_gate", "ws_up", "ws_down")]):
                    pass
                for j in range(4):
                    steps = gate_up_down(a_exp + j, 1 + j, [a[n][l, j] for n in ("w_gate", "w_up", "w_down")])
                    slot_free(a_exp + j)
                    next(steps)
                    if 1 + j >= B_SLOTS:
                        sp.wait_ge(down_done, 1 + j - B_SLOTS + 1)
                    next(steps)
                with sp.Fori(1, E // 4) as i:
                    for j in range(4):
                        e = i * 4 + j
                        steps = gate_up_down(a_exp + j, 1 + j,
                                             [a[n][l, e] for n in ("w_gate", "w_up", "w_down")])
                        b = 5 + 2 * (j % 2)
                        sp.wait_ge(filled[b], i * 2 + (first_turn[b] + j // 2 - 1))
                        next(steps)
                        sp.wait_ge(down_done, i * 4 + (j - 2))
                        next(steps)
                sp.wait_ge(arrived, 4)
                sp.sem_clear(cleared)
                sp.nop().then_inc(s_go, 1)

        @block.gpsimd
        def _(pool):
            with pool.Fori(0, DEPTH) as l:
                def param(dst, src):
                    pool.dma_start(dst, src).then_inc(params_landed, 16)

                def on_all(src):
                    return src.unsqueeze(0).broadcast_to([P] + list(src.shape))

                param(rows[0:MODS, :], a["b_ada"][l].rearrange("(m p) -> m p", p=P))
                param(rows[MODS:MODS + SG, :], a["b_spatial"][l])
                param(rows[MODS + SG:ROWS, :], a["c"][0].rearrange("(j p) -> j p", p=P))
                param(qks[:, 0, :], on_all(a["q_scale"][l]))
                param(qks[:, 1, :], on_all(a["k_scale"][l]))
                param(sgu_ln[:, 0, :], on_all(a["sgu_ln_g"][l]))
                param(sgu_ln[:, 1, :], on_all(a["sgu_ln_b"][l]))
                param(ws_nat, a["w_spatial"][l].rearrange("g i j -> i g j"))
                param(rw[:, :, :], a["router_w"][l].rearrange("(k p) e -> p k e", p=P))
                param(rbias[:, :], on_all(a["router_bias"][l]))
                for half, name in enumerate(("ln1_g", "ln1_b")):
                    pool.dma_start(lnp[:, half, :], on_all(a[name][l])).then_inc(ln1_landed, 16)
                pool.wait_ge(x_ready, 1)
                for half, name in enumerate(("ln2_g", "ln2_b")):
                    pool.dma_start(lnp[:, half, :], on_all(a[name][l])).then_inc(ln2_landed, 16)
                pool.wait_ge(wT_stored, 16)
                with pool.Fori(0, E // 4) as i:
                    pool.dma_start(w_all[:, bass.ds(i * 4, 4), :], on_all(a["w_scratch"][bass.ds(i * 4, 4), :])
                                   ).then_inc(w_all_landed, 16)
                    pool.wait_ge(w_all_landed, l * (4 * E) + i * 16 + 16)
                leave(pool, l)
        n_params = 16 * 10

        @block.tensor
        def _(pe):
            mm = nc.tensor.matmul
            turn = nc.tensor.transpose

            def landed(n):
                pe.wait_ge(a_landed[n % A_SLOTS], 32 * (n // A_SLOTS + 1))

            def to_features(name, src, n_banks):
                for b in range(n_banks):
                    ps = banks.claim(pe, (name, b))
                    for t in range(2):
                        for m in range(MT):
                            o = t * S + m * P
                            last = turn(ps[:, o:o + P], src[:, m, (2 * b + t) * P:(2 * b + t + 1) * P],
                                        ident[:, :])
                    banks.fill(last, (name, b))

            def gate_rows(name, first):
                for g in range(2):
                    ps = banks.claim(pe, (name, g))
                    for t in range(4):
                        j = first + 4 * g + t
                        last = mm(ps[:, t * P:(t + 1) * P], mod[:, j:j + 1].broadcast_to([P, P]),
                                  ident[:, :], start=True, stop=True)
                    banks.fill(last, (name, g))

            def hidden(ps, w):
                for t in range(2):
                    for k in range(DT):
                        last = mm(ps[:, t * S:(t + 1) * S], w[:, k, t * P:(t + 1) * P], hT[:, k, :],
                                  start=(k == 0), stop=(k == DT - 1))
                return last

            def down(h, wd, start, stop):
                for m in range(MT):
                    for n in range(2):
                        for k in range(2):
                            last = mm(banks.t[2 * m + n][:, :], h[:, k * S + m * P:k * S + (m + 1) * P],
                                      wd[:, k, n * 512:(n + 1) * 512], start=start and k == 0,
                                      stop=stop and k == 1, skip_group_check=True)
                return last

            pe.wait_ge(consts["landed"], consts["count"])
            pe.wait_ge(consts["x_landed"], 32)
            with pe.Fori(0, DEPTH) as l:
                pe.wait_ge(params_landed, l * n_params + n_params)
                to_features("xT", x_tok, 4)
                ps = banks.claim(pe, "cols")
                banks.fill(turn(ps[:, 0:ROWS], rows[:, :], ident[0:ROWS, 0:ROWS]), "cols")

                pe.wait_ge(cond_ready, 1)
                ps = banks.claim(pe, "ada")
                for c in range(n_ada):
                    w = rows8(slotA(c))
                    landed(c)
                    for t in range(4):
                        for k in range(DT):
                            last = mm(ps[:, 4 * c + t:4 * c + t + 1], w[:, k, t * P:(t + 1) * P],
                                      cond[:, k:k + 1], start=(k == 0), stop=(k == DT - 1))
                    if c < n_ada - 1:
                        last.then_inc(ada_chunks, 1)
                banks.fill(last, "ada")

                for b in range(4):
                    banks.evacuated(pe, ("xT", b))
                for c, name in enumerate(("q", "kv", "u", "v")):
                    width = 2 * KVW if name == "kv" else 512
                    w = rows8(slotA(a_in + c))
                    landed(a_in + c)
                    for m in range(MT):
                        ps = banks.claim(pe, (name, m))
                        for k in range(DT):
                            last = mm(ps[:, 0:width], hT[:, k, m * P:(m + 1) * P], w[:, k, 0:width],
                                      start=(k == 0), stop=(k == DT - 1))
                        banks.fill(last, (name, m))
                for c in range(4):
                    w = rows8(slotA(a_in + 4 + c))
                    landed(a_in + 4 + c)
                    for g in range(2):
                        ps = banks.claim(pe, ("gates", 2 * c + g))
                        banks.fill(hidden(ps, w[:, :, 2 * g * P:(2 * g + 2) * P]), ("gates", 2 * c + g))

                for g in range(2):
                    ps = banks.claim(pe, ("wsT", g))
                    for i in range(4):
                        last = turn(ps[:, i * P:(i + 1) * P], ws_nat[:, 4 * g + i, :], ident[:, :])
                    banks.fill(last, ("wsT", g))
                pe.wait_ge(rotated, 1)
                for g in range(3):
                    ps = banks.claim(pe, ("qkT", g))
                    for t in range(2):
                        for m in range(MT):
                            src = kdup[:, m, t * P:(t + 1) * P] if g == 2 else \
                                qkr[:, m, (2 * g + t) * P:(2 * g + t + 1) * P]
                            last = turn(ps[:, t * S + m * P:t * S + (m + 1) * P], src, ident[:, :])
                    banks.fill(last, ("qkT", g))
                for g in range(2):
                    banks.evacuated(pe, ("wsT", g))
                pe.wait_ge(vln_ready, 1)
                for m in range(MT):
                    ps = banks.claim(pe, ("sv", m))
                    for g in range(SG):
                        last = mm(ps[:, g * SGD:(g + 1) * SGD], wsT[:, g, :],
                                  v_ln[:, m, g * SGD:(g + 1) * SGD], start=True, stop=True)
                    banks.fill(last, ("sv", m))

                for g in range(3):
                    banks.evacuated(pe, ("qkT", g))
                for h in range(QH + 1):
                    if h < QH:
                        o = (h % 2) * HD
                        ps = banks.claim(pe, ("score", h))
                        for m in range(MT):
                            last = mm(ps[:, m * S:(m + 1) * S], qT[o:o + HD, h // 2, m * P:(m + 1) * P],
                                      kT[o:o + HD, h // (QH // KVH), :], start=True, stop=True)
                        banks.fill(last, ("score", h))
                    if h:
                        g = h - 1
                        pe.wait_ge(prob_ready, g + 1)
                        ps = banks.claim(pe, ("probT", g))
                        for t in range(MT):
                            for m in range(MT):
                                last = turn(ps[:, t * S + m * P:t * S + (m + 1) * P],
                                            prob[:, g % 2, m, t * P:(t + 1) * P], ident[:, :])
                        banks.fill(last, ("probT", g))
                        banks.evacuated(pe, ("probT", g))
                        key = ("oT", g // 2)
                        ps = banks.claim(pe, key) if g % 2 == 0 else banks.t[banks.uses[key][0]]
                        o, kv = (g % 2) * HD, QKW + (g // (QH // KVH)) * HD
                        for t in range(MT):
                            last = mm(ps[o:o + HD, 0:S], p_tok[:, t, kv:kv + HD], probT[:, g % 2, t, :],
                                      start=(t == 0), stop=(t == MT - 1))
                        if g % 2:
                            banks.fill(last, key)

                pe.wait_ge(gated_ready, MT)
                to_features("obT", p_tok[:, :, u0:u0 + SGU], 2)

                landed(a_wa)
                landed(a_wb)
                for g in range(4):
                    banks.evacuated(pe, ("oT", g))
                for g in range(2):
                    banks.evacuated(pe, ("obT", g))
                for t in range(DT):
                    ps = banks.claim(pe, ("branch", t))
                    for half, (n, src) in enumerate(((a_wa, oaT), (a_wb, obT))):
                        w = slotA(n).rearrange("p (k c) -> p k c", k=4)
                        for k in range(4):
                            last = mm(ps[:, half * S:(half + 1) * S], w[:, k, t * P:(t + 1) * P], src[:, k, :],
                                      start=(k == 0), stop=(k == 3))
                    banks.fill(last, ("branch", t))
                gate_rows("gate1", 2 * DT)

                pe.wait_ge(merged, DT)
                for n in range(2):
                    w = rows8(slotA(a_out + n))
                    landed(a_out + n)
                    for m in range(MT):
                        ps = banks.claim(pe, ("out", n, m))
                        for k in range(DT):
                            last = mm(ps[:, :], yT[:, k, m * P:(m + 1) * P], w[:, k, :],
                                      start=(k == 0), stop=(k == DT - 1))
                        banks.fill(last, ("out", n, m))

                pe.wait_ge(x_ready, 1)
                to_features("x2T", x_tok, 4)
                gate_rows("gate2", 5 * DT)
                for b in range(4):
                    banks.evacuated(pe, ("x2T", b))
                ps = banks.claim(pe, "router")
                for m in range(MT):
                    for k in range(DT):
                        last = mm(ps[:, m * E:(m + 1) * E], hT[:, k, m * P:(m + 1) * P], rw[:, k, :],
                                  start=(k == 0), stop=(k == DT - 1))
                banks.fill(last, "router")

                landed(a_shared)
                gu = slotA(a_shared).rearrange("p (h k c) -> p h k c", h=2, k=DT)
                for half, name in enumerate("gu"):
                    ps = banks.claim(pe, (name, "shared"))
                    banks.fill(hidden(ps, gu[:, half]), (name, "shared"))
                banks.evacuated(pe, ("u", "shared"))
                pe.wait_ge(b_landed[0], 16)
                for n in range(4):
                    banks.claim(pe, ("y", n))
                down(hid[:, 0, :], slotB(0).rearrange("p (k c) -> p k c", k=2), True, False
                     ).then_inc(down_done, 1)
                pe.wait_ge(weights_ready, 1)
                ps = banks.claim(pe, "wT")
                for m in range(MT):
                    last = turn(ps[0:E, m * P:(m + 1) * P], router[:, 8, m * E:(m + 1) * E], ident[:, :])
                banks.fill(last, "wT")

                with pe.Fori(0, E // 4) as i:
                    def expert_up(j):
                        n, b = a_exp + j, 4 + 2 * (j % 2)
                        pe.wait_ge(a_landed[n % A_SLOTS], i * 32 + 32 * (n // A_SLOTS + 1))
                        gu = slotA(n).rearrange("p (h k c) -> p h k c", h=2, k=DT)
                        for q in range(2):
                            pe.wait_ge(freed[b + q], i * 2 + (first_turn[b + q] + j // 2))
                            hidden(banks.t[b + q], gu[:, q]).then_inc(filled[b + q], 1)

                    def expert_down(j, stop):
                        n = 1 + j
                        pe.wait_ge(b_landed[n % B_SLOTS], i * 16 + 16 * (n // B_SLOTS + 1))
                        pe.wait_ge(hidden_ready, i * 4 + (j + 1))
                        down(hid[:, (j + 1) % 2, :], slotB(n).rearrange("p (k c) -> p k c", k=2), False, stop
                             ).then_inc(down_done, 1)

                    for j in range(5):
                        if j < 4:
                            expert_up(j)
                        if j:
                            expert_down(j - 1, False)
                leave(pe, l)

        @block.scalar
        def _(act):
            f = nc.scalar.activation

            def roots(n, width):
                act.wait_ge(var_ready, n)
                f(small[:, 32:32 + width], small[:, 0:width], ACT.Sqrt).then_inc(std_ready, 1)

            def modulate(name, bank, shift, scale):
                ps = banks.read(act, (name, bank))
                for t in range(2):
                    j = 2 * bank + t
                    last = f(hT[:, j, :], ps[:, t * S:(t + 1) * S], ACT.Identity,
                             bias=mod[:, shift + j:shift + j + 1], scale=modp1[:, scale + j:scale + j + 1])
                banks.free(last, (name, bank))

            def take(key, dst, view, func=ACT.Copy):
                banks.free(f(dst, view(banks.read(act, key)), func), key)

            with act.Fori(0, DEPTH) as l:
                take("cols", cols[:, :], lambda ps: ps[:, 0:ROWS])
                banks.evacuated(act, "cols")
                f(cond[:, :], cols[:, MODS + SG:ROWS], ACT.Silu).then_inc(cond_ready, 1)
                act.wait_ge(mod_ready, 1)
                for b in range(2):
                    modulate("xT", b, 0, DT)
                for m in range(MT):
                    take(("q", m), p_tok[:, m, 0:QW], lambda ps: ps[:, :])
                for m in range(MT):
                    take(("kv", m), p_tok[:, m, QW:u0], lambda ps: ps[:, 0:2 * KVW])
                roots(1, MT * 10)
                for name, c0 in (("u", u0), ("v", v0)):
                    for m in range(MT):
                        take((name, m), p_tok[:, m, c0:c0 + SGU], lambda ps: ps[:, :], ACT.Gelu)
                roots(2, MT)
                for g in range(8):
                    take(("gates", g), gates[:, 2 * g:2 * g + 2, :],
                         lambda ps: ps[:, :].rearrange("p (t s) -> p t s", t=2), ACT.Sigmoid)
                for g in range(3):
                    dst = kT if g == 2 else qT[:, 2 * g:2 * g + 2, :]
                    take(("qkT", g), dst, lambda ps: ps[:, :].rearrange("p (t s) -> p t s", t=2))
                for h in range(QH + 1):
                    if h < QH:
                        act.wait_ge(max_ready, h + 1)
                        if h >= 2:
                            banks.read(act, ("probT", h - 2))
                        ps = banks.t[banks.uses[("score", h)][0]]
                        for m in range(MT):
                            last = f(prob[:, h % 2, m, :], ps[:, m * S:(m + 1) * S], ACT.Exp,
                                     bias=small[:, 104 + 2 * (h % 2) + m:105 + 2 * (h % 2) + m],
                                     scale=HD ** -0.5,
                                     accum_out=small[:, 108 + 2 * (h % 2) + m:109 + 2 * (h % 2) + m])
                        banks.free(last, ("score", h))
                    if h:
                        g = h - 1
                        take(("probT", g), probT[:, g % 2, :, :],
                             lambda ps: ps[:, :].rearrange("p (t s) -> p t s", t=2))
                        if g % 2:
                            take(("oT", g // 2), oaT[:, g // 2, :], lambda ps: ps[:, 0:S])
                for g in range(2):
                    take(("obT", g), obT[:, 2 * g:2 * g + 2, :],
                         lambda ps: ps[:, :].rearrange("p (t s) -> p t s", t=2))
                roots(3, MT)
                for b in range(2):
                    modulate("x2T", b, 3 * DT, 4 * DT)
                take("router", router[:, 0, :], lambda ps: ps[:, 0:MT * E], ACT.Sigmoid)
                take(("g", "shared"), silu_g[:, 0, :], lambda ps: ps[:, :], ACT.Silu)
                take("wT", wT[:, :], lambda ps: ps[0:E, 0:S])
                banks.evacuated(act, "wT")
                act.dma_start(a["w_scratch"], wT[:, :]).then_inc(wT_stored, 16)
                with act.Fori(0, E // 4) as i:
                    for j in range(4):
                        b = 4 + 2 * (j % 2)
                        turns = i * 2 + (first_turn[b + 1] + j // 2)
                        act.wait_ge(freed[b + 1], turns)
                        act.wait_ge(filled[b], i * 2 + (first_turn[b] + j // 2 + 1))
                        f(silu_g[:, j % 2, :], banks.t[b][:, :], ACT.Silu).then_inc(freed[b], 1)
                roots(4, MT)
                leave(act, l)

        @block.vector
        def _(dve):
            v = nc.vector
            tt, ts, red = v.tensor_tensor, v.tensor_scalar, v.tensor_reduce

            dve.wait_ge(consts["landed"], consts["count"])
            dve.wait_ge(consts["x_landed"], 32)
            with dve.Fori(0, DEPTH) as l:
                step = Chain(dve, dve_steps)

                def modulate(name, bank, shift, scale):
                    ps = banks.read(dve, (name, bank))
                    for t in range(2):
                        j = 2 * bank + t
                        last = ts(hT[:, j, :], ps[:, t * S:(t + 1) * S], modp1[:, scale + j:scale + j + 1],
                                  mod[:, shift + j:shift + j + 1], ALU.mult, ALU.add)
                    banks.free(last, (name, bank))

                def take_gate(name):
                    for g in range(2):
                        ps = banks.read(dve, (name, g))
                        banks.free(v.tensor_copy(gate_b[:, g * 512:(g + 1) * 512], ps[:, :]), (name, g))
                    for g in range(2):
                        banks.evacuated(dve, (name, g))

                def residual(ps, m, n, done):
                    t = tmp[:, 512 * n:512 * (n + 1)] if done is not None else \
                        silu_g[:, n, :]
                    xs = x_tok[:, m, n * 512:(n + 1) * 512]
                    gated = tt(t, ps[:, :], gate_b[:, n * 512:(n + 1) * 512], ALU.mult)
                    if done is None:
                        step(gated)
                    else:
                        banks.free(gated, done)
                        banks.evacuated(dve, done)
                    step(v.scalar_tensor_tensor(xs, xs, ALPHA, t, ALU.mult, ALU.add))

                def norm_x(n, landed, done):
                    for m in range(MT):
                        for h in range(2):
                            last = v.bn_stats(stats[:, m, h, :], x_tok[:, m, h * 512:(h + 1) * 512])
                    step(last)
                    for m in range(MT):
                        last = v.bn_aggr(mv[:, m, :], stats[:, m, :, :].rearrange("p a b -> p (a b)"))
                    step(last)
                    ts(small[:, 0:MT], mv[:, :, 1], 1e-5, None, ALU.add).then_inc(var_ready, 1)
                    dve.wait_ge(std_ready, n)
                    step(v.reciprocal(small[:, 64:64 + MT], small[:, 32:32 + MT]))
                    for m in range(MT):
                        last = ts(x_tok[:, m, :], x_tok[:, m, :], mv[:, m, 0:1], small[:, 64 + m:65 + m],
                                  ALU.subtract, ALU.mult)
                    step(last)
                    dve.wait_ge(landed, l * 32 + 32)
                    for m in range(MT):
                        last = tt(x_tok[:, m, :], x_tok[:, m, :], lnp[:, 0, :], ALU.mult)
                    step(last)
                    for m in range(MT):
                        last = tt(x_tok[:, m, :], x_tok[:, m, :], lnp[:, 1, :], ALU.add)
                    last.then_inc(x_ready, 1)
                    dve.wait_ge(x_ready, done)

                banks.evacuated(dve, "cols")
                ps = banks.read(dve, "ada")
                banks.free(tt(mod[:, :], ps[:, 0:MODS], cols[:, 0:MODS], ALU.add), "ada")
                banks.evacuated(dve, "ada")
                ts(modp1[:, :], mod[:, :], 1.0, None, ALU.add).then_inc(mod_ready, 1)
                dve.wait_ge(mod_ready, 1)
                for b in range(2, 4):
                    modulate("xT", b, 0, DT)

                NH = QH + KVH
                for key in (("q", 0), ("q", 1), ("kv", 0), ("kv", 1)):
                    banks.evacuated(dve, key)
                qn = tmp[:, 0:MT * QKW].rearrange("p (m c) -> p m c", m=MT)
                for m in range(MT):
                    last = tt(qn[:, m, :], p_tok[:, m, 0:QKW], p_tok[:, m, 0:QKW], ALU.mult)
                step(last)
                step(red(small[:, 64:64 + MT * NH], tmp[:, 0:MT * QKW].rearrange("p (h d) -> p h d", d=HD),
                         AX, ALU.add))
                ts(small[:, 0:MT * NH], small[:, 64:64 + MT * NH], 1.0 / HD, 1e-6, ALU.mult, ALU.add
                   ).then_inc(var_ready, 1)
                dve.wait_ge(std_ready, 1)
                step(v.reciprocal(small[:, 64:64 + MT * NH], small[:, 32:32 + MT * NH]))
                qh = qn.rearrange("p m (h d) -> p m h d", d=HD)
                for m in range(MT):
                    last = tt(qh[:, m], p_tok[:, m, 0:QKW].rearrange("p (h d) -> p h d", d=HD),
                              spread(small[:, 64 + m * NH:64 + (m + 1) * NH], 2, HD), ALU.mult)
                step(last)
                for m in range(MT):
                    tt(qh[:, m, 0:QH], qh[:, m, 0:QH], spread(qks[:, 0, :], 1, QH), ALU.mult)
                    last = tt(qh[:, m, QH:NH], qh[:, m, QH:NH], spread(qks[:, 1, :], 1, KVH), ALU.mult)
                step(last)
                half = NH * HD // 2
                parts = [tmp[:, MT * QKW + n * half:MT * QKW + (n + 1) * half].rearrange(
                    "p (h d) -> p h d", d=HD // 2) for n in range(4)]
                for m in range(MT):
                    even, odd = qh[:, m, :, 0::2], qh[:, m, :, 1::2]
                    c, s = spread(cosr[:, m, :], 1, NH), spread(sinr[:, m, :], 1, NH)
                    for n, (x, y) in enumerate(((even, c), (odd, s), (even, s), (odd, c))):
                        last = tt(parts[n], x, y, ALU.mult)
                    step(last)
                    out = qkr[:, m, :].rearrange("p (h d) -> p h d", d=HD)
                    tt(out[:, :, 0::2], parts[0], parts[1], ALU.subtract)
                    step(tt(out[:, :, 1::2], parts[2], parts[3], ALU.add))
                for m in range(MT):
                    for g in range(KVH):
                        last = v.tensor_copy(
                            kdup[:, m, g * 2 * HD:(g + 1) * 2 * HD].rearrange("p (a d) -> p a d", a=2),
                            spread(qkr[:, m, QW + g * HD:QW + (g + 1) * HD], 1, 2))
                last.then_inc(rotated, 1)

                for m in range(MT):
                    banks.evacuated(dve, ("v", m))
                for m in range(MT):
                    last = v.bn_stats(stats[:, m, 0, :], p_tok[:, m, v0:v0 + SGU])
                step(last)
                for m in range(MT):
                    last = v.bn_aggr(mv[:, m, :], stats[:, m, 0, :])
                step(last)
                ts(small[:, 0:MT], mv[:, :, 1], 1e-5, None, ALU.add).then_inc(var_ready, 1)
                dve.wait_ge(std_ready, 2)
                step(v.reciprocal(small[:, 64:64 + MT], small[:, 32:32 + MT]))
                for m in range(MT):
                    last = ts(v_ln[:, m, :], p_tok[:, m, v0:v0 + SGU], mv[:, m, 0:1], small[:, 64 + m:65 + m],
                              ALU.subtract, ALU.mult)
                step(last)
                dve.wait_ge(params_landed, l * n_params + n_params)
                for m in range(MT):
                    last = tt(v_ln[:, m, :], v_ln[:, m, :], sgu_ln[:, 0, :], ALU.mult)
                step(last)
                for m in range(MT):
                    last = tt(v_ln[:, m, :], v_ln[:, m, :], sgu_ln[:, 1, :], ALU.add)
                last.then_inc(vln_ready, 1)
                for g in range(2):
                    ps = banks.read(dve, ("wsT", g))
                    banks.free(v.tensor_copy(wsT[:, 4 * g:4 * g + 4, :],
                                             ps[:, :].rearrange("p (g i) -> p g i", g=4)), ("wsT", g))
                for m in range(MT):
                    ps = banks.read(dve, ("sv", m))
                    mixed = tmp[:, 2048:2560]
                    if m:
                        dve.wait_ge(gated_ready, m)
                    banks.free(tt(mixed.rearrange("p (g d) -> p g d", g=SG),
                                  ps[:, :].rearrange("p (g d) -> p g d", g=SG),
                                  spread(cols[:, MODS:MODS + SG], 2, SGD), ALU.add), ("sv", m))
                    banks.evacuated(dve, ("sv", m))
                    tt(p_tok[:, m, u0:u0 + SGU], p_tok[:, m, u0:u0 + SGU], mixed, ALU.mult
                       ).then_inc(gated_ready, 1)

                for h in range(QH + 1):
                    if h < QH:
                        o = 2 * (h % 2)
                        ps = banks.read(dve, ("score", h))
                        step(red(small[:, 100 + o:102 + o], ps[:, :].rearrange("p (m s) -> p m s", m=MT),
                                 AX, ALU.max))
                        ts(small[:, 104 + o:106 + o], small[:, 100 + o:102 + o], -HD ** -0.5, None, ALU.mult
                           ).then_inc(max_ready, 1)
                    if h:
                        g = h - 1
                        o = 2 * (g % 2)
                        banks.evacuated(dve, ("score", g))
                        step(v.reciprocal(small[:, 112 + o:114 + o], small[:, 108 + o:110 + o]))
                        for m in range(MT):
                            last = ts(prob[:, g % 2, m, :], prob[:, g % 2, m, :],
                                      small[:, 112 + o + m:113 + o + m], None, ALU.mult)
                        last.then_inc(prob_ready, 1)

                for g in range(8):
                    banks.evacuated(dve, ("gates", g))
                for t in range(DT):
                    ps = banks.read(dve, ("branch", t))
                    o = 512 * (t % 2)
                    tt(tmp[:, o:o + S], ps[:, 0:S], gates[:, t, :], ALU.mult)
                    banks.free(tt(tmp[:, o + S:o + 2 * S], ps[:, S:2 * S], gates[:, DT + t, :], ALU.mult),
                               ("branch", t))
                    banks.evacuated(dve, ("branch", t))
                    tt(yT[:, t, :], tmp[:, o:o + S], tmp[:, o + S:o + 2 * S], ALU.add).then_inc(merged, 1)

                take_gate("gate1")
                dve.wait_ge(merged, DT)
                for n in range(2):
                    for m in range(MT):
                        residual(banks.read(dve, ("out", n, m)), m, n, ("out", n, m))
                norm_x(3, ln1_landed, 1)
                for b in range(2, 4):
                    modulate("x2T", b, 3 * DT, 4 * DT)
                take_gate("gate2")

                def r(n):
                    return router[:, n, :]

                def groups(ap):
                    return ap.rearrange("p (g e) -> p g e", e=PG)

                def tokens(ap):
                    return ap.rearrange("p (m e) -> p m e", m=MT)

                banks.evacuated(dve, "router")
                step(tt(tokens(r(1)), tokens(r(0)), spread(rbias[:, :], 1, MT), ALU.add))
                for g in range(MT * NG):
                    last = v.max(out=r(5)[:, g * 8:(g + 1) * 8], in_=r(1)[:, g * PG:(g + 1) * PG])
                step(last)
                gs, rank = small[:, 120:136], small[:, 136:152]
                keep, pen, top = small[:, 152:168], small[:, 168:184], small[:, 184:200]
                best = r(5).rearrange("p (g e) -> p g e", e=8)
                step(tt(gs, best[:, :, 0], best[:, :, 1], ALU.add))
                gsm = gs.rearrange("p (m g) -> p m g", m=MT)
                pairs = [r(n).rearrange("p (m i j) -> p m i j", m=MT, i=NG) for n in (6, 7)]
                theirs, own = spread(gsm, 2, NG), spread(gsm, 3, NG)
                tt(pairs[0], theirs, own, ALU.is_gt)
                step(tt(pairs[1], theirs, own, ALU.is_equal))
                step(tt(pairs[1], pairs[1], spread(jlt[:, :].rearrange("p (i j) -> p i j", i=NG), 1, MT),
                        ALU.mult))
                step(tt(r(6), r(6), r(7), ALU.add))
                step(red(rank, r(6).rearrange("p (g j) -> p g j", j=NG), AX, ALU.add))
                step(ts(keep, rank, KEEP_G - 0.5, None, ALU.is_lt))
                step(ts(pen, keep, -1.0, -NEG, ALU.add, ALU.mult))
                step(tt(groups(r(2)), groups(r(1)), spread(keep, 2, PG), ALU.mult))
                step(tt(groups(r(2)), groups(r(2)), spread(pen, 2, PG), ALU.add))
                for m in range(MT):
                    step(v.max(out=top[:, m * 8:(m + 1) * 8], in_=r(2)[:, m * E:(m + 1) * E]))
                    step(v.match_replace(out=r(3)[:, m * E:(m + 1) * E], in_to_replace=top[:, m * 8:(m + 1) * 8],
                                         in_values=r(2)[:, m * E:(m + 1) * E], imm_value=TAKEN))
                step(tt(r(4), r(3), r(2), ALU.not_equal))
                step(tt(r(4), r(4), r(0), ALU.mult))
                step(red(small[:, 200:202], tokens(r(4)), AX, ALU.add))
                step(v.reciprocal(small[:, 202:204], small[:, 200:202]))
                v.scalar_tensor_tensor(tokens(r(8)), tokens(r(4)), ROUTED_SCALE, spread(small[:, 202:204], 2, E),
                                       ALU.mult, ALU.mult).then_inc(weights_ready, 1)

                ps = banks.read(dve, ("u", "shared"))
                banks.evacuated(dve, ("g", "shared"))
                banks.free(tt(hid[:, 0, :], silu_g[:, 0, :], ps[:, :], ALU.mult), ("u", "shared"))
                with dve.Fori(0, E // 4) as i:
                    dve.wait_ge(w_all_landed, l * (4 * E) + i * 16 + 16)
                    for j in range(4):
                        b = 4 + 2 * (j % 2)
                        s = (j + 1) % 2
                        dve.wait_ge(freed[b], i * 2 + (first_turn[b] + j // 2 + 1))
                        dve.wait_ge(filled[b + 1], i * 2 + (first_turn[b + 1] + j // 2 + 1))
                        dve.wait_ge(down_done, i * 4 + j)
                        tt(hid[:, s, :], silu_g[:, j % 2, :], banks.t[b + 1][:, :], ALU.mult
                           ).then_inc(freed[b + 1], 1)
                        dve.wait_ge(freed[b + 1], i * 2 + (first_turn[b + 1] + j // 2 + 1))
                        hv = hid[:, s, :].rearrange("p (t s) -> p t s", t=2)
                        tt(hv, hv, spread(w_all[:, bass.ds(i * 4 + j, 1), :].rearrange("p a s -> p (a s)"), 1, 2),
                           ALU.mult).then_inc(hidden_ready, 1)

                dve.wait_ge(down_done, E + 1)
                for m in range(MT):
                    for n in range(2):
                        residual(banks.t[2 * m + n], m, n, None)
                norm_x(4, ln2_landed, 2)
                leave(dve, l)


def second_block(nc, a, x_tok, consts):
    with ExitStack() as ctx:
        def sb(name, shape):
            return ctx.enter_context(nc.sbuf_tensor("s_" + name, shape, F32))

        def sem(name):
            return ctx.enter_context(nc.semaphore("s_" + name))

        ident = consts["ident"]
        slots_A = 3
        n_rows = 3 * DT + CT + 4 * RT + 3 * RT
        r_ffn1, r_mix, r_ffn2, r_mu = 0, DT, 2 * DT, 3 * DT
        r_w0 = r_mu + CT
        r_a0 = r_w0 + 2 * RT
        r_kk = r_a0 + 2 * RT
        r_ka, r_rk = r_kk + RT, r_kk + 2 * RT
        assert n_rows == r_rk + RT

        ringA = sb("ringA", [P, slots_A, A_W])
        hT = sb("hT", [P, DT, S])
        ARENA = 29072
        arena = sb("arena", [P, ARENA])
        rows = sb("rows", [n_rows, P])
        cols = sb("cols", [P, n_rows])
        mus = sb("mus", [P, 2, CT])
        w2 = sb("w2", [P, RW])
        a2 = sb("a2", [P, RW])
        g2 = sb("g2", [P, RW])
        lnx = sb("lnx", [P, 2, RW])
        qkg = sb("qkg", [P, 2, HD])
        subg = sb("subg", [P, 2 * HD])
        lamv = sb("lamv", [P, 4, HD])
        lamc = sb("lamc", [P, 2])
        masks = sb("masks", [P, 12, P])
        dist = sb("dist", [P, MT, S])
        heads1 = sb("heads1", [P, P])
        headsel = sb("headsel", [P, RT, 8])
        small = sb("small", [P, 256])
        edge = sb("edge", [P, 2, 2, S + 2])
        ones = sb("ones", [P, CH])
        lam = small[:, 200:206]
        dcol = small[:, 208:224]
        bonus = small[:, 224:256].rearrange("p (d m h) -> p d m h", d=2, m=MT)

        def view(lo, n, dims=None, **kw):
            assert lo + n <= ARENA, (lo, n)
            ap = arena[:, lo:lo + n]
            return ap.rearrange(dims, **kw) if dims else ap

        ringB = view(0, B_SLOTS * B_W, "p (b c) -> p b c", b=B_SLOTS)
        silu_g = view(8192, 1024, "p (b c) -> p b c", b=2)
        hid = view(9216, 1024, "p (b c) -> p b c", b=2)
        xn = view(10240, 2048, "p (m d) -> p m d", m=MT)
        rkv = view(0, 3072, "p (t s) -> p t s", s=S)
        low = view(3072, 768, "p (t s) -> p t s", s=S)
        oaT = view(3840, 1024, "p (t s) -> p t s", s=S)
        obT = view(4864, 1024, "p (t s) -> p t s", s=S)
        base = 5888
        nbr = view(base, 1024, "p (b t s) -> p b t s", b=2, t=2)
        at_tok = view(base + 1024, 3072, "p (m c) -> p m c", m=MT)
        sq = view(base + 4096, 2048)
        qT = view(base + 6144, 1024, "p (t s) -> p t s", s=S)
        kT = view(base + 7168, 1024, "p (t s) -> p t s", s=S)
        prob = view(base + 8192, 2048, "p (b a m s) -> p b a m s", b=2, a=2, m=MT)
        comb = view(base + 10240, 1024, "p (b m s) -> p b m s", b=2, m=MT)
        combT = view(base + 11264, 1024, "p (b t s) -> p b t s", b=2, t=MT)
        ob = view(base + 12288, 1024, "p (m c) -> p m c", m=MT)
        kk = view(base, 1024, "p (t s) -> p t s", s=S)
        AR = view(base + 1024, 2048, "p (t r s) -> p t r s", r=2, s=S)
        Bt = view(base + 3072, 1024, "p (t s) -> p t s", s=S)
        Kt = view(base + 4096, 1024, "p (t s) -> p t s", s=S)
        state = view(base + 13312, 2048, "p (c q v) -> p c q v", c=NCH, q=RT)
        SA = view(base + 4096, 1024, "p (m c) -> p m c", m=MT)
        Btok = view(base + 5120, 1024, "p (m c) -> p m c", m=MT)
        Ktok = view(base + 6144, 1024, "p (m c) -> p m c", m=MT)
        Vtok = view(base + 7168, 1024, "p (m c) -> p m c", m=MT)
        MRB = view(base + 8192, 2048, "p (q u t) -> p q u t", q=RT, u=4)
        MRK = view(base + 10240, 2048, "p (q u t) -> p q u t", q=RT, u=4)
        sw = view(base + 8192, 1024)
        ic = view(base + 9216, 1024)
        cs = view(base + 10240, 1024)
        ce = view(base + 11264, 1024)
        SA0 = view(base + 12288, 1024, "p (m c) -> p m c", m=MT)
        XAT = view(base + 15360, 1024, "p (q s) -> p q s", q=RT)
        Y = view(base + 16384, 1024, "p (m c) -> p m c", m=MT)
        gbase = base + 17408
        U, L2T, X, XT, W1, Z = [view(gbase + n * 1024, 1024, "p (b u t) -> p b u t", b=2, u=4)
                                for n in range(5)] + [view(base + 13312, 1024, "p (b u t) -> p b u t", b=2, u=4)]
        Q1 = view(gbase + 5120, 256)
        Atok = view(gbase + 5376, 256, "p (m c) -> p m c", m=MT)
        ytmp = view(gbase, 1024)
        ytmp2 = view(gbase + 1024, 1024)
        gates = view(base + 1024, 4096, "p (t s) -> p t s", s=S)
        btmp = view(base + 5120, 1024)
        yT = view(base + 6144, 2048, "p (t s) -> p t s", s=S)

        s_go = sem("layer_cleared")
        params_landed = sem("params_landed")
        names = ["a_slot0", "a_slot1", "a_slot2", "b_slot0", "b_slot1", "b_slot2", "b_slot3",
                 "squares_ready", "var_ready", "std_ready", "xn_ready", "x_ready", "down_done",
                 "mixed_ready", "neighbours_read", "at_ready", "lam_asked", "lam_exp", "max_ready", "exp_done",
                 "comb_ready", "ob_ready", "kk_squared", "low_ready", "cum_ready", "exps_ready", "ABKR_ready",
                 "bonus_ready", "units_ready", "z_ready", "inv_ready", "sa_ready", "state_ready",
                 "oa_ready", "merged", "dve_steps", "arrived"]
        names += [f"bank_filled{i}" for i in range(8)] + [f"bank_freed{i}" for i in range(8)]
        each = {n: sem(n) for n in names}
        nums = [s.num for s in each.values()]
        cleared = range(min(nums), max(nums) + 1)
        assert len(cleared) == len(nums) and not {s_go.num, params_landed.num} & set(cleared)
        a_landed = [each[f"a_slot{i}"] for i in range(slots_A)]
        b_landed = [each[f"b_slot{i}"] for i in range(B_SLOTS)]
        squares_ready, var_ready, std_ready = each["squares_ready"], each["var_ready"], each["std_ready"]
        xn_ready, x_ready, down_done = each["xn_ready"], each["x_ready"], each["down_done"]
        mixed_ready, neighbours_read, at_ready = each["mixed_ready"], each["neighbours_read"], each["at_ready"]
        lam_asked, lam_exp, max_ready = each["lam_asked"], each["lam_exp"], each["max_ready"]
        exp_done, comb_ready, ob_ready = each["exp_done"], each["comb_ready"], each["ob_ready"]
        kk_squared, low_ready, cum_ready = each["kk_squared"], each["low_ready"], each["cum_ready"]
        exps_ready, ABKR_ready, bonus_ready = each["exps_ready"], each["ABKR_ready"], each["bonus_ready"]
        units_ready, z_ready, inv_ready = each["units_ready"], each["z_ready"], each["inv_ready"]
        sa_ready, state_ready, oa_ready = each["sa_ready"], each["state_ready"], each["oa_ready"]
        merged, dve_steps, arrived = each["merged"], each["dve_steps"], each["arrived"]
        filled = [each[f"bank_filled{i}"] for i in range(8)]
        freed = [each[f"bank_freed{i}"] for i in range(8)]

        banks = Banks([ctx.enter_context(nc.psum_tensor(f"s_bank{i}", [P, BANK], F32)) for i in range(8)],
                      filled, freed)
        LEVELS = 5
        scan_order = [list(range(NCH)), list(range(NCH))[::-1]]

        def take_ffn(f):
            for b in range(4):
                banks.take(("xT", f, b), b)
            if f == 0:
                banks.take("cols", 7)
            for n in range(4):
                banks.take(("y", f, n), n)
            for s in range(STEPS):
                banks.take(("g", f, s), 4 + 2 * (s % 2))
                banks.take(("u", f, s), 5 + 2 * (s % 2))

        take_ffn(0)
        for b in range(4):
            banks.take(("xT", 1, b), b)
        for g in range(8):
            banks.take(("rw", g), g % 4)
        for c in range(3):
            for m in range(MT):
                banks.take(("at", c, m), (2 * c + m) % 4)
        for g in range(4):
            banks.take(("qkT", g), 4 + g)
        for m in range(MT):
            banks.take(("o", m), m)
        for s in range(2 * BH + 2):
            if s < 2 * BH:
                banks.take(("score", s), 4 + s % 2)
            if s % 2 and s > 1:
                banks.take(("combT", s // 2 - 1), 6 + (s // 2 - 1) % 2)
        for g in range(2):
            banks.take(("obT", g), 2 + g)
        for g in range(2):
            banks.take(("kkss", g), g)
        for m in range(MT):
            banks.take(("Vtok", m), 2 + m)
        for d in range(2):
            for g in range(2):
                banks.take(("dec", d, g), 4 + g)
            for g in range(2):
                banks.take(("rate", d, g), 6 + g)
            banks.take(("bonus", d), 2)
            for m in range(MT):
                banks.take(("Btok", d, m), 3 + m)
            for m in range(MT):
                banks.take(("Ktok", d, m), 5 + m)
            for duo in range(2):
                for q in range(2):
                    for hh in range(2):
                        for n, name in enumerate(("UR", "KR", "L")):
                            banks.take((name, d, duo, q, hh), 3 * hh + n)
                for lv in range(LEVELS):
                    for q in range(2):
                        banks.take(("W", d, duo, q, lv), 3 * q)
                    for q in range(2):
                        banks.take(("dXT", d, duo, q, lv), 3 * q + 1)
                        if lv < LEVELS - 1:
                            banks.take(("dX", d, duo, q, lv), 3 * q + 2)
                for q in range(2):
                    banks.take(("Q1", d, duo, q), 6)
                    banks.take(("Atok", d, duo, q), 7)
                    banks.take(("SA0", d, duo, q), 2)
                    banks.take(("XAT", d, duo, q), 5)
            for n in range(NCH):
                if n:
                    banks.take(("SA", d, n), 0)
                if n < NCH - 1:
                    banks.take(("state", d, n), 1)
            for m in range(MT):
                banks.take(("Y", d, m), 2 + m)
        for m in range(MT):
            banks.take(("gate", m), 6 + m)
        for g in range(8):
            banks.take(("gates", g), g % 4)
        for g in range(2):
            banks.take(("oaT", g), 4 + g)
        for t in range(DT):
            banks.take(("branch", t), t % 4)
        for n in range(2):
            for m in range(MT):
                banks.take(("out", n, m), 4 + 2 * n + m)
        take_ffn(2)

        a_in, a_at = STEPS, STEPS + 4
        a_gate = a_at + 3
        a_wa = a_gate + 4
        a_wb, a_out, a_ffn2 = a_wa + 1, a_wa + 2, a_wa + 4
        last_use = {s: ("u", 0, s) for s in range(STEPS)}
        last_use |= {a_in + c: ("rw", 2 * c + 1) for c in range(4)}
        last_use |= {a_at + c: ("at", c, 1) for c in range(3)}
        last_use |= {a_gate + c: ("gates", 2 * c + 1) for c in range(4)}
        last_use |= {a_wa: ("branch", DT - 1), a_wb: ("branch", DT - 1)}
        last_use |= {a_out + n: ("out", n, 1) for n in range(2)}
        last_use |= {a_ffn2 + s: ("u", 2, s) for s in range(STEPS)}
        ffn_first = {0: 0, 2: a_ffn2}

        def slotA(n):
            return ringA[:, n % slots_A, :]

        def rows8(ap):
            return ap.rearrange("p (k c) -> p k c", k=DT)

        def slotB(n):
            return ringB[:, n % B_SLOTS, :].rearrange("p (k c) -> p k c", k=2)

        def pair_of(ps):
            return ps[:, :].rearrange("p (t s) -> p t s", t=2)

        block = ctx.enter_context(nc.Block())

        def leave(eng, l):
            eng.nop().then_inc(arrived, 1)
            eng.wait_ge(s_go, l + 1)

        @block.sync
        def _(sp):
            with sp.Fori(0, DEPTH) as l:
                def slot_free(n):
                    if n >= slots_A:
                        banks.read(sp, last_use[n - slots_A])

                def load(n, dst, src):
                    slot_free(n)
                    half = dst.shape[1] // 2
                    for h in range(2):
                        sp.dma_start(dst[:, h * half:(h + 1) * half], src[:, h * half:(h + 1) * half]
                                     ).then_inc(a_landed[n % slots_A], 16)

                def load_up(f, s):
                    w = a[("ffn1_in_2", None, "ffn2_in_2")[f]]
                    n = ffn_first[f] + s
                    slot_free(n)
                    gu = slotA(n).rearrange("p (h k c) -> p h k c", h=2, k=DT)
                    for h in range(2):
                        c = h * DFF + s * FF
                        sp.dma_start(gu[:, h], w[l, :, c:c + FF].rearrange("(k p) c -> p k c", p=P)
                                     ).then_inc(a_landed[n % slots_A], 16)

                def load_down(f, s):
                    w = a[("ffn1_out_2", None, "ffn2_out_2")[f]]
                    if s >= B_SLOTS:
                        sp.wait_ge(down_done, (f // 2) * (STEPS - 1) + s - B_SLOTS + 1)
                    sp.dma_start(slotB(s), w[l, s * FF:(s + 1) * FF, :].rearrange("(k p) c -> p k c", p=P)
                                 ).then_inc(b_landed[s % B_SLOTS], 16)

                for s in range(STEPS):
                    load_up(0, s)
                    load_down(0, s)
                edges = [0, 512, 1024, 1536, CRW] + [CRW + 512 * (i + 1) for i in range(7)]
                for c in range(11):
                    w = edges[c + 1] - edges[c]
                    load(a_in + c, rows8(slotA(a_in + c))[:, :, 0:w],
                         a["w_in_2"][l, :, edges[c]:edges[c + 1]].rearrange("(k p) c -> p k c", p=P))
                for b in range(2):
                    load(a_wa + b, slotA(a_wa + b).rearrange("p (k c) -> p k c", k=4),
                         a["w_branch_2"][l, b].rearrange("(k p) c -> p k c", p=P))
                for c in range(2):
                    load(a_out + c, rows8(slotA(a_out + c)),
                         a["w_out_2"][l, :, c * 512:(c + 1) * 512].rearrange("(k p) c -> p k c", p=P))
                load_up(2, 0)
                sp.wait_ge(x_ready, 2)
                for s in range(STEPS):
                    if s:
                        load_up(2, s)
                    load_down(2, s)
                sp.wait_ge(arrived, 4)
                sp.sem_clear(cleared)
                sp.nop().then_inc(s_go, 1)

        n_params = 16 * 23

        @block.gpsimd
        def _(pool):
            with pool.Fori(0, DEPTH) as l:
                def param(dst, src):
                    pool.dma_start(dst, src).then_inc(params_landed, 16)
                    count.append(16)

                def on_all(src):
                    return src.unsqueeze(0).broadcast_to([P] + list(src.shape))

                count = []
                for at, name in ((r_ffn1, "norm_ffn1_2"), (r_mix, "norm_mix_2"), (r_ffn2, "norm_ffn2_2"),
                                 (r_mu, "rwkv_mu_2"), (r_kk, "k_k_2"), (r_ka, "k_a_2")):
                    src = a[name][l].rearrange("(r p) -> r p", p=P)
                    param(rows[at:at + src.shape[0], :], src)
                for at, name in ((r_w0, "decay_w0_2"), (r_a0, "iclr_a0_2")):
                    param(rows[at:at + 2 * RT, :], a[name][l].rearrange("d (r p) -> (d r) p", p=P))
                param(rows[r_rk:r_rk + RT, :], a["r_k_2"][l].rearrange("(r h) n -> r (h n)", h=2))
                param(w2[:, :], a["decay_w2_2"][l].rearrange("d r c -> (d r) c"))
                param(a2[:, :], a["iclr_a2_2"][l].rearrange("d r c -> (d r) c"))
                param(g2[:, :], a["gate_g2_2"][l])
                param(lnx[:, 0, :], on_all(a["ln_x_g_2"][l]))
                param(lnx[:, 1, :], on_all(a["ln_x_b_2"][l]))
                param(qkg[:, 0, :], on_all(a["q_gain_2"][l]))
                param(qkg[:, 1, :], on_all(a["k_gain_2"][l]))
                param(subg[:, :], on_all(a["subln_g_2"][l]))
                param(lamv[:, :, :], on_all(a["diff_lambda_2"][l]))
                param(lamc[:, :], a["const_lam"][l])
                param(masks[:, :, :], a["const_masks"])
                param(dist[:, :, :], a["const_dist"])
                param(heads1[:, :], a["const_heads"])
                param(headsel[:, :, :], a["const_headsel"])
                assert sum(count) == n_params
                leave(pool, l)
        @block.tensor
        def _(pe):
            mm = nc.tensor.matmul
            turn = nc.tensor.transpose

            def landed(n):
                pe.wait_ge(a_landed[n % slots_A], 32 * (n // slots_A + 1))

            def to_features(key, src, n_banks):
                for b in range(n_banks):
                    ps = banks.claim(pe, (*key, b))
                    for t in range(2):
                        for m in range(MT):
                            o = t * S + m * P
                            last = turn(ps[:, o:o + P], src[:, m, (2 * b + t) * P:(2 * b + t + 1) * P],
                                        ident[:, :])
                    banks.fill(last, (*key, b))

            def hidden(ps, w, n=2):
                for t in range(n):
                    for k in range(DT):
                        last = mm(ps[:, t * S:(t + 1) * S], w[:, k, t * P:(t + 1) * P], hT[:, k, :],
                                  start=(k == 0), stop=(k == DT - 1))
                return last

            def ffn(f, l):
                pe.wait_ge(xn_ready, f + 1)
                if f == 0:
                    pe.wait_ge(params_landed, l * n_params + n_params)
                to_features(("xT", f), xn, 4)
                if f == 0:
                    ps = banks.claim(pe, "cols")
                    banks.fill(turn(ps[:, 0:n_rows], rows[:, :], ident[0:n_rows, 0:n_rows]), "cols")
                for b in range(4):
                    banks.evacuated(pe, ("xT", f, b))
                for n in range(4):
                    banks.claim(pe, ("y", f, n))
                for s in range(STEPS + 1):
                    if s < STEPS:
                        n = ffn_first[f] + s
                        landed(n)
                        gu = slotA(n).rearrange("p (h k c) -> p h k c", h=2, k=DT)
                        for half, name in enumerate("gu"):
                            ps = banks.claim(pe, (name, f, s))
                            banks.fill(hidden(ps, gu[:, half]), (name, f, s))
                    if s:
                        r = s - 1
                        fills = r // B_SLOTS + 1 + (f // 2) * ((STEPS - 1 - r % B_SLOTS) // B_SLOTS + 1)
                        pe.wait_ge(b_landed[r % B_SLOTS], 16 * fills)
                        banks.evacuated(pe, ("u", f, r))
                        wd = slotB(r)
                        for m in range(MT):
                            for n in range(2):
                                for k in range(2):
                                    last = mm(banks.t[2 * m + n][:, :],
                                              hid[:, r % 2, k * S + m * P:k * S + (m + 1) * P],
                                              wd[:, k, n * 512:(n + 1) * 512], start=(r == 0 and k == 0),
                                              stop=(r == STEPS - 1 and k == 1), skip_group_check=True)
                                if r == STEPS - 1:
                                    banks.fill(last, ("y", f, 2 * m + n))
                        if r < STEPS - 1:
                            last.then_inc(down_done, 1)

            with pe.Fori(0, DEPTH) as l:
                ffn(0, l)

                pe.wait_ge(xn_ready, 2)
                to_features(("xT", 1), xn, 4)
                for b in range(4):
                    banks.evacuated(pe, ("xT", 1, b))
                for g in range(8):
                    c = a_in + g // 2
                    if g % 2 == 0:
                        landed(c)
                    w = rows8(slotA(c))
                    ps = banks.claim(pe, ("rw", g))
                    o = (g % 2) * 2 * P
                    banks.fill(hidden(ps, w[:, :, o:o + 2 * P], 1 if g == 7 else 2), ("rw", g))
                for c in range(3):
                    landed(a_at + c)
                    w = rows8(slotA(a_at + c))
                    for m in range(MT):
                        ps = banks.claim(pe, ("at", c, m))
                        for k in range(DT):
                            last = mm(ps[:, :], hT[:, k, m * P:(m + 1) * P], w[:, k, :],
                                      start=(k == 0), stop=(k == DT - 1))
                        banks.fill(last, ("at", c, m))

                pe.wait_ge(at_ready, 1)
                for g in range(4):
                    ps = banks.claim(pe, ("qkT", g))
                    for t in range(2):
                        for m in range(MT):
                            c = (2 * g + t) * P
                            last = turn(ps[:, t * S + m * P:t * S + (m + 1) * P], at_tok[:, m, c:c + P],
                                        ident[:, :])
                    banks.fill(last, ("qkT", g))
                for g in range(4):
                    banks.evacuated(pe, ("qkT", g))
                for m in range(MT):
                    banks.claim(pe, ("o", m))
                for s in range(2 * BH + 2):
                    if s < 2 * BH:
                        h, o = s // 2, (s % 2) * HD
                        ps = banks.claim(pe, ("score", s))
                        for m in range(MT):
                            last = mm(ps[:, m * S:(m + 1) * S], qT[o:o + HD, h, m * P:(m + 1) * P],
                                      kT[o:o + HD, h, :], start=True, stop=True)
                        banks.fill(last, ("score", s))
                    if s % 2 and s > 1:
                        h = s // 2 - 1
                        pe.wait_ge(comb_ready, h + 1)
                        ps = banks.claim(pe, ("combT", h))
                        for t in range(MT):
                            for m in range(MT):
                                last = turn(ps[:, t * S + m * P:t * S + (m + 1) * P],
                                            comb[:, h % 2, m, t * P:(t + 1) * P], ident[:, :])
                        banks.fill(last, ("combT", h))
                        banks.evacuated(pe, ("combT", h))
                        for m in range(MT):
                            for t in range(MT):
                                last = mm(banks.t[m][:, h * P:(h + 1) * P], combT[:, h % 2, t, m * P:(m + 1) * P],
                                          at_tok[:, t, 2 * RW + h * P:2 * RW + (h + 1) * P],
                                          start=(t == 0), stop=(t == MT - 1))
                            if h == BH - 1:
                                banks.fill(last, ("o", m))
                pe.wait_ge(ob_ready, 1)
                to_features(("obT",), ob, 2)

                pe.wait_ge(kk_squared, 1)
                for g in range(2):
                    ps = banks.claim(pe, ("kkss", g))
                    for t in range(2):
                        last = mm(ps[:, t * S:(t + 1) * S], heads1[:, :], sq[:, (2 * g + t) * S:(2 * g + t + 1) * S],
                                  start=True, stop=True)
                    banks.fill(last, ("kkss", g))
                for m in range(MT):
                    ps = banks.claim(pe, ("Vtok", m))
                    for t in range(RT):
                        last = turn(ps[:, t * P:(t + 1) * P], rkv[:, 2 * RT + t, m * P:(m + 1) * P], ident[:, :])
                    banks.fill(last, ("Vtok", m))
                pe.wait_ge(low_ready, 1)
                for d in range(2):
                    o = d * LORA
                    for name, w, src in (("dec", w2, low[:, 0, :]), ("rate", a2, low[:, 1, :])):
                        for g in range(2):
                            ps = banks.claim(pe, (name, d, g))
                            for t in range(2):
                                c = (2 * g + t) * P
                                last = mm(ps[:, t * S:(t + 1) * S], w[o:o + LORA, c:c + P], src[o:o + LORA, :],
                                          start=True, stop=True)
                            banks.fill(last, (name, d, g))
                    pe.wait_ge(bonus_ready, d + 1)
                    ps = banks.claim(pe, ("bonus", d))
                    for m in range(MT):
                        for t in range(RT):
                            last = mm(ps[:, m * 8:(m + 1) * 8], sw[:, t * S + m * P:t * S + (m + 1) * P],
                                      headsel[:, t, :], start=(t == 0), stop=(t == RT - 1))
                    banks.fill(last, ("bonus", d))
                    pe.wait_ge(ABKR_ready, d + 1)
                    for name, src in (("Btok", Bt), ("Ktok", Kt)):
                        for m in range(MT):
                            ps = banks.claim(pe, (name, d, m))
                            for t in range(RT):
                                last = turn(ps[:, t * P:(t + 1) * P], src[:, t, m * P:(m + 1) * P], ident[:, :])
                            banks.fill(last, (name, d, m))
                    for duo in range(2):
                        for q in range(2):
                            p = 2 * duo + q
                            for hh in range(2):
                                o = hh * HD
                                for name in ("UR", "KR", "L"):
                                    ps = banks.claim(pe, (name, d, duo, q, hh))
                                    for m in range(MT):
                                        s = slice(m * P, (m + 1) * P)
                                        if name == "L":
                                            last = mm(ps[:, m * P:(m + 1) * P], AR[o:o + HD, p, 0, s],
                                                      Bt[o:o + HD, p, s], start=True, stop=True)
                                        else:
                                            left = Bt if name == "UR" else Kt
                                            last = mm(ps[:, m * S:(m + 1) * S], left[o:o + HD, p, s],
                                                      AR[o:o + HD, p, :, s], start=True, stop=True)
                                    banks.fill(last, (name, d, duo, q, hh))
                        for lv in range(LEVELS):
                            n = (d * 2 + duo) * LEVELS + lv
                            for q in range(2):
                                pe.wait_ge(z_ready, 2 * n + q + 1)
                                ps = banks.claim(pe, ("W", d, duo, q, lv))
                                for u in range(4):
                                    last = mm(ps[:, u * P:(u + 1) * P], Z[:, q, u, :], X[:, q, u, :],
                                              start=True, stop=True)
                                banks.fill(last, ("W", d, duo, q, lv))
                            for q in range(2):
                                banks.evacuated(pe, ("W", d, duo, q, lv))
                                ps = banks.claim(pe, ("dXT", d, duo, q, lv))
                                for u in range(4):
                                    last = mm(ps[:, u * P:(u + 1) * P], W1[:, q, u, :], XT[:, q, u, :],
                                              start=True, stop=True)
                                banks.fill(last, ("dXT", d, duo, q, lv))
                                if lv < LEVELS - 1:
                                    ps = banks.claim(pe, ("dX", d, duo, q, lv))
                                    for u in range(4):
                                        last = mm(ps[:, u * P:(u + 1) * P], XT[:, q, u, :], W1[:, q, u, :],
                                                  start=True, stop=True)
                                    banks.fill(last, ("dX", d, duo, q, lv))
                        if duo == 0:
                            for m in range(MT):
                                if d == 0:
                                    banks.evacuated(pe, ("Vtok", m))
                        for q in range(2):
                            p = 2 * duo + q
                            ps = banks.claim(pe, ("Q1", d, duo, q))
                            for u in range(4):
                                c = (2 * p + u // 2) * HD
                                last = mm(ps[:, u * HD:(u + 1) * HD], L2T[:, q, u, :], Vtok[:, u % 2, c:c + HD],
                                          start=True, stop=True)
                            banks.fill(last, ("Q1", d, duo, q))
                            ps = banks.claim(pe, ("Atok", d, duo, q))
                            for m in range(MT):
                                last = turn(ps[:, m * P:(m + 1) * P], AR[:, p, 0, m * P:(m + 1) * P], ident[:, :])
                            banks.fill(last, ("Atok", d, duo, q))
                            pe.wait_ge(inv_ready, 4 * d + 2 * duo + q + 1)
                            banks.evacuated(pe, ("Q1", d, duo, q))
                            ps = banks.claim(pe, ("SA0", d, duo, q))
                            for u in range(4):
                                last = mm(ps[:, u * HD:(u + 1) * HD], XT[:, q, u, :], Q1[:, u * HD:(u + 1) * HD],
                                          start=True, stop=True)
                            banks.fill(last, ("SA0", d, duo, q))
                            banks.evacuated(pe, ("Atok", d, duo, q))
                            ps = banks.claim(pe, ("XAT", d, duo, q))
                            for u in range(4):
                                o, m = (u // 2) * HD, u % 2
                                last = mm(ps[o:o + HD, m * P:(m + 1) * P], Atok[:, m, o:o + HD], XT[:, q, u, :],
                                          start=True, stop=True)
                            banks.fill(last, ("XAT", d, duo, q))
                    for n, c in enumerate(scan_order[d]):
                        o, m = (c % 2) * CH, c // 2
                        if n:
                            pe.wait_ge(state_ready, 3 * d + n)
                            ps = banks.claim(pe, ("SA", d, n))
                            for p in range(RT):
                                last = mm(ps[o:o + CH, p * P:(p + 1) * P], XAT[:, p, c * CH:(c + 1) * CH],
                                          state[:, c, p, :], start=True, stop=True)
                            banks.fill(last, ("SA", d, n))
                        if n < NCH - 1:
                            pe.wait_ge(sa_ready, 4 * d + n + 1)
                            ps = banks.claim(pe, ("state", d, n))
                            for p in range(RT):
                                s = slice(p * P, (p + 1) * P)
                                mm(ps[:, s], Btok[o:o + CH, m, s], SA[o:o + CH, m, s], start=True, stop=False)
                                last = mm(ps[:, s], Ktok[o:o + CH, m, s], Vtok[o:o + CH, m, s],
                                          start=False, stop=True)
                            banks.fill(last, ("state", d, n))
                    pe.wait_ge(sa_ready, 4 * d + 4)
                    for m in range(MT):
                        ps = banks.claim(pe, ("Y", d, m))
                        for p in range(RT):
                            for hh in range(2):
                                cs_ = slice(p * P + hh * HD, p * P + (hh + 1) * HD)
                                mm(ps[:, cs_], MRB[:, p, 2 * hh + m, :], SA[:, m, cs_],
                                   start=(hh == 0), stop=False, skip_group_check=True)
                                last = mm(ps[:, cs_], MRK[:, p, 2 * hh + m, :], Vtok[:, m, cs_],
                                          start=False, stop=False, skip_group_check=True)
                            for c in (2 * m, 2 * m + 1):
                                if c != scan_order[d][0]:
                                    o = (c % 2) * CH
                                    last = mm(ps[o:o + CH, p * P:(p + 1) * P], AR[:, p, 1, c * CH:(c + 1) * CH],
                                              state[:, c, p, :], start=False, stop=True, skip_group_check=True)
                        banks.fill(last, ("Y", d, m))
                for m in range(MT):
                    ps = banks.claim(pe, ("gate", m))
                    banks.fill(mm(ps[:, :], low[:, 2, m * P:(m + 1) * P], g2[:, :], start=True, stop=True),
                               ("gate", m))
                for g in range(8):
                    c = a_gate + g // 2
                    if g % 2 == 0:
                        landed(c)
                    o = (g % 2) * 2 * P
                    ps = banks.claim(pe, ("gates", g))
                    banks.fill(hidden(ps, rows8(slotA(c))[:, :, o:o + 2 * P]), ("gates", g))
                pe.wait_ge(oa_ready, 1)
                to_features(("oaT",), ytmp.rearrange("p (m c) -> p m c", m=MT), 2)
                landed(a_wa)
                landed(a_wb)
                for g in range(2):
                    banks.evacuated(pe, ("obT", g))
                    banks.evacuated(pe, ("oaT", g))
                for t in range(DT):
                    ps = banks.claim(pe, ("branch", t))
                    for half, (n, src) in enumerate(((a_wa, oaT), (a_wb, obT))):
                        w = slotA(n).rearrange("p (k c) -> p k c", k=4)
                        for k in range(4):
                            last = mm(ps[:, half * S:(half + 1) * S], w[:, k, t * P:(t + 1) * P], src[:, k, :],
                                      start=(k == 0), stop=(k == 3))
                    banks.fill(last, ("branch", t))
                pe.wait_ge(merged, DT)
                for n in range(2):
                    landed(a_out + n)
                    w = rows8(slotA(a_out + n))
                    for m in range(MT):
                        ps = banks.claim(pe, ("out", n, m))
                        for k in range(DT):
                            last = mm(ps[:, :], yT[:, k, m * P:(m + 1) * P], w[:, k, :],
                                      start=(k == 0), stop=(k == DT - 1))
                        banks.fill(last, ("out", n, m))
                ffn(2, l)
                leave(pe, l)

        @block.scalar
        def _(act):
            f = nc.scalar.activation
            root_count = [0]

            def roots(width):
                root_count[0] += 1
                act.wait_ge(var_ready, root_count[0])
                f(small[:, 32:32 + width], small[:, 0:width], ACT.Sqrt).then_inc(std_ready, 1)

            def take(key, dst, view_, func=ACT.Copy, **kw):
                banks.free(f(dst, view_(banks.read(act, key)), func, **kw), key)

            def norm(k, at):
                if k:
                    act.wait_ge(x_ready, k)
                for m in range(MT):
                    last = f(xn[:, m, :], x_tok[:, m, :], ACT.Square, accum_out=small[:, 120 + m:121 + m])
                last.then_inc(squares_ready, 1)
                roots(MT)
                if k == 0:
                    take("cols", cols[:, :], lambda ps: ps[:, 0:n_rows])
                    banks.evacuated(act, "cols")
                for b in range(2):
                    key = ("xT", k, b)
                    ps = banks.read(act, key)
                    for t in range(2):
                        j = 2 * b + t
                        last = f(hT[:, j, :], ps[:, t * S:(t + 1) * S], ACT.Copy, scale=cols[:, at + j:at + j + 1])
                    banks.free(last, key)

            def ffn(k):
                for s in range(STEPS):
                    if s >= 2:
                        banks.evacuated(act, ("u", k, s - 2))
                    take(("g", k, s), silu_g[:, s % 2, :], lambda ps: ps[:, :], ACT.Silu)

            with act.Fori(0, DEPTH) as l:
                root_count[0] = 0
                norm(0, r_ffn1)
                ffn(0)
                norm(1, r_mix)
                dst = [rkv[:, t, :] for t in range(12)] + [low[:, t, :] for t in range(3)]
                for g in range(8):
                    n = 1 if g == 7 else 2
                    ps = banks.read(act, ("rw", g))
                    if g >= 2:
                        act.wait_ge(neighbours_read, g - 1)
                    f(edge[:, g % 2, 0:n, 1:S + 1], pair_of(ps)[:, 0:n, :], ACT.Copy)
                    for t in range(n):
                        j = 2 * g + t
                        last = f(dst[j], ps[:, t * S:(t + 1) * S], ACT.Copy, scale=mus[:, 0, j:j + 1])
                    banks.free(last, ("rw", g))
                act.wait_ge(mixed_ready, 8)
                f(low[:, 0, :], low[:, 0, :], ACT.Tanh)
                f(low[:, 2, :], low[:, 2, :], ACT.Sigmoid).then_inc(low_ready, 1)
                for c in range(3):
                    for m in range(MT):
                        take(("at", c, m), at_tok[:, m, c * 512:(c + 1) * 512], lambda ps: ps[:, :])
                act.wait_ge(lam_asked, 1)
                f(lam[:, 2:4], lam[:, 0:2], ACT.Exp).then_inc(lam_exp, 1)
                roots(32)
                for g in range(4):
                    take(("qkT", g), (qT if g < 2 else kT)[:, 2 * (g % 2):2 * (g % 2) + 2, :], pair_of)
                for s in range(2 * BH + 2):
                    if s < 2 * BH:
                        o = 72 + 4 * (s % 4)
                        act.wait_ge(max_ready, s + 1)
                        for m in range(MT):
                            pr = prob[:, (s // 2) % 2, s % 2, m, :]
                            last = f(pr, pr, ACT.Exp, bias=small[:, o + m:o + m + 1], scale=HD ** -0.5,
                                     accum_out=small[:, o + 2 + m:o + 3 + m])
                        last.then_inc(exp_done, 1)
                    if s % 2 and s > 1:
                        h = s // 2 - 1
                        take(("combT", h), combT[:, h % 2, :, :], pair_of)
                roots(8)
                for g in range(2):
                    take(("obT", g), obT[:, 2 * g:2 * g + 2, :], pair_of)
                for g in range(2):
                    take(("kkss", g), sq[:, 512 * g:512 * (g + 1)], lambda ps: ps[:, :], ACT.Sqrt)
                for m in range(MT):
                    take(("Vtok", m), Vtok[:, m, :], lambda ps: ps[:, :])
                for d in range(2):
                    if d:
                        for m in range(MT):
                            banks.evacuated(act, ("Y", 0, m))
                    for name, at, out in (("dec", r_w0, sw), ("rate", r_a0, ic)):
                        for g in range(2):
                            ps = banks.read(act, (name, d, g))
                            for t in range(2):
                                j = 2 * g + t
                                last = f(out[:, j * S:(j + 1) * S], ps[:, t * S:(t + 1) * S], ACT.Sigmoid,
                                         bias=cols[:, at + d * RT + j:at + d * RT + j + 1])
                            banks.free(last, (name, d, g))
                    act.wait_ge(cum_ready, d + 1)
                    f(AR[:, :, 1, :], cs.rearrange("p (t s) -> p t s", s=S), ACT.Exp, scale=-DECAY)
                    f(AR[:, :, 0, :], ce.rearrange("p (t s) -> p t s", s=S), ACT.Exp, scale=-DECAY)
                    f(Bt, cs.rearrange("p (t s) -> p t s", s=S), ACT.Exp, scale=DECAY).then_inc(exps_ready, 1)
                    take(("bonus", d), bonus[:, d], lambda ps: ps[:, 0:16].rearrange("p (m h) -> p m h", m=MT))
                    for name, dst_ in (("Btok", Btok), ("Ktok", Ktok)):
                        for m in range(MT):
                            take((name, d, m), dst_[:, m, :], lambda ps: ps[:, :])
                    for duo in range(2):
                        for lv in range(LEVELS):
                            for q in range(2):
                                take(("W", d, duo, q, lv), W1[:, q, :, :],
                                     lambda ps: ps[:, :].rearrange("p (u t) -> p u t", u=4))
                        for q in range(2):
                            p = 2 * duo + q
                            take(("Q1", d, duo, q), Q1, lambda ps: ps[:, 0:256])
                            take(("Atok", d, duo, q), Atok, lambda ps: ps[:, 0:256].rearrange("p (m c) -> p m c", m=MT))
                            out = SA0[:, :, p * P:(p + 1) * P].rearrange("p m (h c) -> p h m c", h=2)
                            for hh in range(2):
                                ps = banks.read(act, ("SA0", d, duo, q))
                                last = f(out[:, hh], ps[:, hh * P:(hh + 1) * P].rearrange("p (m c) -> p m c", m=MT),
                                         ACT.Copy)
                            banks.free(last, ("SA0", d, duo, q))
                            take(("XAT", d, duo, q), XAT[:, p, :], lambda ps: ps[:, 0:S])
                roots(16)
                for g in range(8):
                    if g == 0:
                        act.wait_ge(oa_ready, 1)
                    take(("gates", g), gates[:, 2 * g:2 * g + 2, :], pair_of, ACT.Sigmoid)
                for g in range(2):
                    take(("oaT", g), oaT[:, 2 * g:2 * g + 2, :], pair_of)
                norm(2, r_ffn2)
                ffn(2)
                leave(act, l)

        @block.vector
        def _(dve):
            v = nc.vector
            tt, ts, red, stt = v.tensor_tensor, v.tensor_scalar, v.tensor_reduce, v.scalar_tensor_tensor

            def mask(n, *lead):
                ap = masks[:, n, :]
                for k in lead:
                    ap = spread(ap, 1, k)
                return ap

            with dve.Fori(0, DEPTH) as l:
                step = Chain(dve, dve_steps)
                root_count = [0]

                def root(width):
                    root_count[0] += 1
                    dve.wait_ge(std_ready, root_count[0])
                    return step(v.reciprocal(small[:, 64:64 + width], small[:, 32:32 + width]))

                def variance(out, in_, scale, eps):
                    ts(out, in_, scale, eps, ALU.mult, ALU.add).then_inc(var_ready, 1)

                def norm(k, at):
                    dve.wait_ge(squares_ready, k + 1)
                    variance(small[:, 0:MT], small[:, 120:120 + MT], 1.0 / D, 1e-6)
                    root(MT)
                    for m in range(MT):
                        last = ts(xn[:, m, :], x_tok[:, m, :], small[:, 64 + m:65 + m], None, ALU.mult)
                    last.then_inc(xn_ready, 1)
                    if k == 0:
                        banks.evacuated(dve, "cols")
                    for b in range(2, 4):
                        key = ("xT", k, b)
                        ps = banks.read(dve, key)
                        for t in range(2):
                            j = 2 * b + t
                            last = ts(hT[:, j, :], ps[:, t * S:(t + 1) * S], cols[:, at + j:at + j + 1], None,
                                      ALU.mult)
                        banks.free(last, key)

                def ffn(k):
                    for s in range(STEPS):
                        if s >= 2:
                            dve.wait_ge(down_done, (k // 2) * (STEPS - 1) + s - 1)
                        banks.evacuated(dve, ("g", k, s))
                        ps = banks.read(dve, ("u", k, s))
                        banks.free(tt(hid[:, s % 2, :], silu_g[:, s % 2, :], ps[:, :], ALU.mult), ("u", k, s))
                    for m in range(MT):
                        for n in range(2):
                            key = ("y", k, 2 * m + n)
                            ps = banks.read(dve, key)
                            xs = x_tok[:, m, n * 512:(n + 1) * 512]
                            banks.free(stt(xs, ps[:, :], 0.5, xs, ALU.mult, ALU.add), key)
                    for n in range(4):
                        banks.evacuated(dve, ("y", k, n))
                    dve.nop().then_inc(x_ready, 1)

                norm(0, r_ffn1)
                ts(mus[:, 0, :], cols[:, r_mu:r_mu + CT], -1.0, 1.0, ALU.mult, ALU.add)
                ts(mus[:, 1, :], cols[:, r_mu:r_mu + CT], 0.5, None, ALU.mult)
                v.memset(ones[:, :], 1.0)
                step(v.memset(edge[:, :, :, 0:S + 2:S + 1], 0.0))
                ffn(0)
                norm(1, r_mix)

                dst = [rkv[:, t, :] for t in range(12)] + [low[:, t, :] for t in range(3)]
                for g in range(8):
                    n = 1 if g == 7 else 2
                    if g >= 2:
                        dve.wait_ge(mixed_ready, g - 1)
                    banks.evacuated(dve, ("rw", g))
                    tt(nbr[:, g % 2, 0:n, :], edge[:, g % 2, 0:n, 0:S], edge[:, g % 2, 0:n, 2:S + 2], ALU.add
                       ).then_inc(neighbours_read, 1)
                    dve.wait_ge(neighbours_read, g + 1)
                    for t in range(n):
                        j = 2 * g + t
                        last = stt(dst[j], nbr[:, g % 2, t, :], mus[:, 1, j:j + 1], dst[j], ALU.mult, ALU.add)
                    last.then_inc(mixed_ready, 1)

                dve.wait_ge(params_landed, l * n_params + n_params)
                lprod = sq[:, 0:2 * HD].rearrange("p (a d) -> p a d", a=2)
                step(tt(lprod, lamv[:, 0::2, :], lamv[:, 1::2, :], ALU.mult))
                red(lam[:, 0:2], lprod, AX, ALU.add).then_inc(lam_asked, 1)
                dve.wait_ge(lam_exp, 1)
                step(tt(lam[:, 4:5], lam[:, 3:4], lam[:, 2:3], ALU.subtract))
                step(tt(lam[:, 4:5], lam[:, 4:5], lamc[:, 0:1], ALU.subtract))
                for c in range(2):
                    for m in range(MT):
                        banks.evacuated(dve, ("at", c, m))
                sq3 = sq.rearrange("p (m c) -> p m c", m=MT)
                for m in range(MT):
                    last = tt(sq3[:, m], at_tok[:, m, 0:2 * RW], at_tok[:, m, 0:2 * RW], ALU.mult)
                step(last)
                step(red(small[:, 120:152], sq.rearrange("p (h d) -> p h d", d=HD), AX, ALU.add))
                variance(small[:, 0:32], small[:, 120:152], 1.0 / HD, 1e-6)
                root(32)
                for m in range(MT):
                    qk = at_tok[:, m, 0:2 * RW].rearrange("p (h d) -> p h d", d=HD)
                    step(tt(qk, qk, spread(small[:, 64 + 16 * m:80 + 16 * m], 2, HD), ALU.mult))
                    for n in range(2):
                        last = tt(qk[:, 8 * n:8 * n + 8], qk[:, 8 * n:8 * n + 8], spread(qkg[:, n, :], 1, 8),
                                  ALU.mult)
                last.then_inc(at_ready, 1)

                for s in range(2 * BH + 2):
                    if s < 2 * BH:
                        h, o = s // 2, 72 + 4 * (s % 4)
                        slope = 2.0 ** (-8.0 * (h + 1) / BH)
                        pr = prob[:, h % 2, s % 2, :, :]
                        ps = banks.read(dve, ("score", s))
                        banks.free(stt(pr, dist[:, :, :], -slope * HD ** 0.5, pair_of(ps), ALU.mult, ALU.add),
                                   ("score", s))
                        banks.evacuated(dve, ("score", s))
                        step(red(small[:, 88:90], pr, AX, ALU.max))
                        ts(small[:, o:o + 2], small[:, 88:90], -HD ** -0.5, None, ALU.mult).then_inc(max_ready, 1)
                        dve.wait_ge(max_ready, s + 1)
                    if s % 2 and s > 1:
                        h = s // 2 - 1
                        o = 72 + 8 * (h % 2)
                        dve.wait_ge(exp_done, 2 * h + 2)
                        if h >= 2:
                            banks.read(dve, ("combT", h - 2))
                        v.reciprocal(small[:, 92:94], small[:, o + 2:o + 4])
                        step(v.reciprocal(small[:, 94:96], small[:, o + 6:o + 8]))
                        step(ts(small[:, 94:96], small[:, 94:96], lam[:, 4:5], None, ALU.mult))
                        for m in range(MT):
                            last = ts(prob[:, h % 2, 1, m, :], prob[:, h % 2, 1, m, :], small[:, 94 + m:95 + m],
                                      None, ALU.mult)
                        step(last)
                        for m in range(MT):
                            last = stt(comb[:, h % 2, m, :], prob[:, h % 2, 0, m, :], small[:, 92 + m:93 + m],
                                       prob[:, h % 2, 1, m, :], ALU.mult, ALU.add)
                        last.then_inc(comb_ready, 1)
                        dve.wait_ge(comb_ready, h + 1)
                for m in range(MT):
                    ps = banks.read(dve, ("o", m))
                    banks.free(v.tensor_copy(ob[:, m, :], ps[:, :]), ("o", m))
                    banks.evacuated(dve, ("o", m))
                ob2 = ob.rearrange("p m c -> p (m c)")
                step(tt(sq[:, 0:1024], ob2, ob2, ALU.mult))
                step(red(small[:, 120:128], sq[:, 0:1024].rearrange("p (h d) -> p h d", d=2 * HD), AX, ALU.add))
                variance(small[:, 0:8], small[:, 120:128], 1.0 / (2 * HD), 1e-6)
                root(8)
                step(ts(small[:, 64:72], small[:, 64:72], lamc[:, 1:2], None, ALU.mult))
                obh = ob2.rearrange("p (h d) -> p h d", d=2 * HD)
                step(tt(obh, obh, spread(small[:, 64:72], 2, 2 * HD), ALU.mult))
                tt(obh, obh, spread(subg[:, :], 1, 8), ALU.mult).then_inc(ob_ready, 1)
                dve.wait_ge(ob_ready, 1)

                r3, k3 = rkv[:, 0:RT, :], rkv[:, RT:2 * RT, :]
                sqt = sq[:, 0:1024].rearrange("p (t s) -> p t s", s=S)
                dve.wait_ge(mixed_ready, 8)
                step(tt(kk, k3, spread(cols[:, r_kk:r_kk + RT], 2, S), ALU.mult))
                tt(sqt, kk, kk, ALU.mult).then_inc(kk_squared, 1)
                for g in range(2):
                    banks.evacuated(dve, ("kkss", g))
                step(ts(sqt, sqt, 1e-12, None, ALU.max))
                step(v.reciprocal(sqt, sqt))
                step(tt(kk, kk, sqt, ALU.mult))

                for d in range(2):
                    for g in range(2):
                        banks.evacuated(dve, ("dec", d, g))
                        banks.evacuated(dve, ("rate", d, g))
                    if d:
                        for m in range(MT):
                            banks.evacuated(dve, ("Y", 0, m))
                    for n in range(RT * NCH):
                        w = sw[:, n * CH:(n + 1) * CH]
                        c = cs[:, n * CH:(n + 1) * CH]
                        if d:
                            w, c = w[:, ::-1], c[:, ::-1]
                        last = v.tensor_tensor_scan(c, ones[:, :], w, 0.0, ALU.mult, ALU.add)
                    step(last)
                    tt(ce, cs, sw, ALU.subtract).then_inc(cum_ready, 1)
                    ic3 = ic.rearrange("p (t s) -> p t s", s=S)
                    sw3 = sw.rearrange("p (t s) -> p t s", s=S)
                    dve.wait_ge(cum_ready, d + 1)
                    kd = SA0.rearrange("p m c -> p (m c)").rearrange("p (t s) -> p t s", s=S)
                    step(stt(kd, ic3, -1.0, spread(cols[:, r_ka:r_ka + RT], 2, S), ALU.add, ALU.mult))
                    step(stt(kd, kd, 1.0, k3, ALU.add, ALU.mult))
                    step(tt(sw3, r3, spread(cols[:, r_rk:r_rk + RT], 2, S), ALU.mult))
                    tt(sw3, sw3, kd, ALU.mult).then_inc(bonus_ready, 1)
                    step(tt(ic3, ic3, kk, ALU.mult))
                    dve.wait_ge(exps_ready, d + 1)
                    ends = slice(CH - 1, S, CH) if d == 0 else slice(0, S, CH)
                    step(v.tensor_copy(dcol.rearrange("p (t c) -> p t c", c=NCH), AR[:, :, 1, ends]))
                    tt(AR[:, :, 1, :], AR[:, :, 1, :], r3, ALU.mult)
                    stt(AR[:, :, 0, :], AR[:, :, 0, :], -1.0, kk, ALU.mult, ALU.mult)
                    step(tt(Kt, Bt, kd, ALU.mult))
                    tt(Bt, Bt, ic3, ALU.mult).then_inc(ABKR_ready, 1)
                    dve.wait_ge(ABKR_ready, d + 1)
                    banks.evacuated(dve, ("bonus", d))

                    for duo in range(2):
                        for q in range(2):
                            p = 2 * duo + q
                            for hh in range(2):
                                for name, low_, high in (("UR", U, MRB), ("KR", L2T, MRK)):
                                    key = (name, d, duo, q, hh)
                                    ps = banks.read(dve, key)[:, :].rearrange("p (m r t) -> p m r t", m=MT, r=2)
                                    tt(low_[:, q, 2 * hh:2 * hh + 2, :], ps[:, :, 0, :], mask(d, MT), ALU.mult)
                                    banks.free(tt(high[:, p, 2 * hh:2 * hh + 2, :], ps[:, :, 1, :],
                                                  mask(2 + d, MT), ALU.mult), key)
                                key = ("L", d, duo, q, hh)
                                ps = banks.read(dve, key)[:, 0:S].rearrange("p (m t) -> p m t", m=MT)
                                banks.free(tt(X[:, q, 2 * hh:2 * hh + 2, :], ps, mask(4 + d, MT), ALU.mult), key)
                            banks.evacuated(dve, ("UR", d, duo, q, 1))
                            banks.evacuated(dve, ("L", d, duo, q, 1))
                            idn = spread(ident[:, :], 1, 4)
                            step(tt(XT[:, q], U[:, q], mask(6, 4), ALU.mult))
                            step(tt(X[:, q], X[:, q], idn, ALU.add))
                            step(tt(XT[:, q], XT[:, q], idn, ALU.add))
                        for lv in range(LEVELS):
                            for q in range(2):
                                if lv:
                                    u3 = [t_[:, q] for t_ in (XT, X)]
                                    for key, dst_ in ((("dXT", d, duo, q, lv - 1), u3[0]),
                                                      (("dX", d, duo, q, lv - 1), u3[1])):
                                        ps = banks.read(dve, key)
                                        if key[0] == "dXT":
                                            banks.read(dve, ("dX", d, duo, q, lv - 1))
                                        banks.free(tt(dst_, ps[:, :].rearrange("p (u t) -> p u t", u=4), dst_,
                                                      ALU.add), key)
                                    banks.evacuated(dve, ("dX", d, duo, q, lv - 1))
                                tt(Z[:, q], U[:, q], mask(7 + lv, 4), ALU.mult).then_inc(z_ready, 1)
                                dve.wait_ge(z_ready, 2 * ((d * 2 + duo) * LEVELS + lv) + q + 1)
                        for q in range(2):
                            key = ("dXT", d, duo, q, LEVELS - 1)
                            ps = banks.read(dve, key)
                            banks.free(tt(XT[:, q], ps[:, :].rearrange("p (u t) -> p u t", u=4), XT[:, q], ALU.add),
                                       key)
                            banks.evacuated(dve, key)
                            dve.nop().then_inc(inv_ready, 1)

                    for duo in range(2):
                        for q in range(2):
                            banks.evacuated(dve, ("SA0", d, duo, q))
                            banks.evacuated(dve, ("XAT", d, duo, q))
                    dc = dcol.rearrange("p (t c) -> p t c", c=NCH)
                    for n, c in enumerate(scan_order[d]):
                        o, m = (c % 2) * CH, c // 2
                        part = slice(o, o + CH)
                        if n == 0:
                            v.tensor_copy(SA[part, m, :], SA0[part, m, :]).then_inc(sa_ready, 1)
                        else:
                            key = ("SA", d, n)
                            ps = banks.read(dve, key)
                            banks.free(tt(SA[part, m, :], ps[part, :], SA0[part, m, :], ALU.add), key)
                            banks.evacuated(dve, key)
                            dve.nop().then_inc(sa_ready, 1)
                        if n < NCH - 1:
                            nxt = scan_order[d][n + 1]
                            key = ("state", d, n)
                            ps = banks.read(dve, key)[:, :].rearrange("p (q v) -> p q v", q=RT)
                            S1 = state[:, nxt]
                            decay = spread(dc[:, :, c], 2, P)
                            if n:
                                banks.free(tt(S1, ps, state[:, c], ALU.add), key)
                                banks.evacuated(dve, key)
                                step(tt(S1, S1, decay, ALU.mult))
                            else:
                                banks.free(tt(S1, ps, decay, ALU.mult), key)
                                banks.evacuated(dve, key)
                            tt(S1, S1, spread(heads1[:, :], 1, RT), ALU.mult).then_inc(state_ready, 1)
                            dve.wait_ge(state_ready, 3 * d + n + 1)
                    for m in range(MT):
                        key = ("Y", d, m)
                        ps = banks.read(dve, key)
                        if d == 0:
                            last = v.tensor_copy(Y[:, m, :], ps[:, :])
                        else:
                            last = tt(Y[:, m, :], ps[:, :], Y[:, m, :], ALU.add)
                        banks.free(last, key)
                        banks.evacuated(dve, key)

                y1 = Y.rearrange("p m c -> p (m c)")
                yh = y1.rearrange("p (h d) -> p h d", d=HD)
                t1 = ytmp.rearrange("p (h d) -> p h d", d=HD)
                t2 = ytmp2.rearrange("p (h d) -> p h d", d=HD)
                step(red(small[:, 120:136], yh, AX, ALU.add))
                step(ts(small[:, 120:136], small[:, 120:136], 1.0 / HD, None, ALU.mult))
                step(tt(t1, yh, spread(small[:, 120:136], 2, HD), ALU.subtract))
                step(tt(t2, t1, t1, ALU.mult))
                step(red(small[:, 136:152], t2, AX, ALU.add))
                variance(small[:, 0:16], small[:, 136:152], 1.0 / HD, 64e-5)
                root(16)
                step(tt(t1, t1, spread(small[:, 64:80], 2, HD), ALU.mult))
                ym = ytmp.rearrange("p (m c) -> p m c", m=MT)
                step(tt(ym, ym, spread(lnx[:, 0, :], 1, MT), ALU.mult))
                step(tt(ym, ym, spread(lnx[:, 1, :], 1, MT), ALU.add))
                step(tt(small[:, 152:168].rearrange("p (m h) -> p m h", m=MT), bonus[:, 0], bonus[:, 1], ALU.add))
                step(tt(t2, Vtok.rearrange("p m (h d) -> p (m h) d", d=HD), spread(small[:, 152:168], 2, HD),
                        ALU.mult))
                step(tt(ytmp, ytmp, ytmp2, ALU.add))
                for m in range(MT):
                    ps = banks.read(dve, ("gate", m))
                    banks.free(tt(ym[:, m], ps[:, :], ym[:, m], ALU.mult), ("gate", m))
                for m in range(MT):
                    banks.evacuated(dve, ("gate", m))
                dve.nop().then_inc(oa_ready, 1)

                for g in range(8):
                    banks.evacuated(dve, ("gates", g))
                for t in range(DT):
                    ps = banks.read(dve, ("branch", t))
                    o = 512 * (t % 2)
                    if t >= 2:
                        dve.wait_ge(merged, t - 1)
                    tt(btmp[:, o:o + S], ps[:, 0:S], gates[:, t, :], ALU.mult)
                    banks.free(tt(btmp[:, o + S:o + 2 * S], ps[:, S:2 * S], gates[:, DT + t, :], ALU.mult),
                               ("branch", t))
                    banks.evacuated(dve, ("branch", t))
                    tt(yT[:, t, :], btmp[:, o:o + S], btmp[:, o + S:o + 2 * S], ALU.add).then_inc(merged, 1)
                dve.wait_ge(merged, DT)
                for n in range(2):
                    for m in range(MT):
                        key = ("out", n, m)
                        ps = banks.read(dve, key)
                        xs = x_tok[:, m, n * 512:(n + 1) * 512]
                        banks.free(tt(xs, ps[:, :], xs, ALU.add), key)
                for n in range(2):
                    for m in range(MT):
                        banks.evacuated(dve, ("out", n, m))
                dve.nop().then_inc(x_ready, 1)
                norm(2, r_ffn2)
                ffn(2)
                leave(dve, l)


def program(nc, a, out):
    with ExitStack() as ctx:
        def sb(name, shape):
            return ctx.enter_context(nc.sbuf_tensor(name, shape, F32))

        x_tok = sb("x_tok", [P, MT, D])
        consts = {
            "ident": sb("ident", [P, P]),
            "cos": sb("cos", [P, MT, HD // 2]),
            "sin": sb("sin", [P, MT, HD // 2]),
            "jlt": sb("jlt", [P, NG * NG]),
            "landed": ctx.enter_context(nc.semaphore("constants_landed")),
            "x_landed": ctx.enter_context(nc.semaphore("x_landed")),
            "count": 4 * 16,
        }
        stored = ctx.enter_context(nc.semaphore("out_stored"))
        x_v = a["x"][0].rearrange("(m p) d -> p m d", p=P)
        with nc.Block() as block:
            @block.sync
            def _(sp):
                for m in range(MT):
                    sp.dma_start(x_tok[:, m, :], x_v[:, m, :]).then_inc(consts["x_landed"], 16)
                for name in ("ident", "cos", "sin", "jlt"):
                    sp.dma_start(consts[name][:, :] if name in ("ident", "jlt") else consts[name][:, :, :],
                                 a["const_" + name]).then_inc(consts["landed"], 16)

        first_block(nc, a, x_tok, consts)
        second_block(nc, a, x_tok, consts)

        with nc.Block() as block:
            @block.sync
            def _(sp):
                sp.dma_start(out[0].rearrange("(m p) d -> p m d", p=P), x_tok[:, :, :]).then_inc(stored, 16)
                sp.wait_ge(stored, 16)


def shape_constants():
    t = np.arange(S)
    cols_, rows_ = 64, S // 64
    place = [(t // cols_ - rows_ // 2).astype(np.float32), (t % cols_ - cols_ // 2).astype(np.float32)]
    freq = (10000.0 ** (-np.arange(HD // 4, dtype=np.float32) / (HD // 4))).astype(np.float32)
    angle = np.concatenate([p[:, None] * freq for p in place], -1).astype(np.float32)

    def by_token(x):
        return np.ascontiguousarray(x.reshape(MT, P, -1).transpose(1, 0, 2), np.float32)

    g = np.arange(NG)
    earlier = np.tile((g[None, :] < g[:, None]).astype(np.float32).reshape(1, NG * NG), (P, 1))
    j, c = np.arange(P)[:, None], np.arange(P)[None, :]
    same = j // CH == c // CH
    pair = j // 2 == c // 2
    masks = [same & (j < c), same & (j > c), same & (j <= c), same & (j >= c), pair & (j > c), pair & (j < c)]
    masks += [(j // (2 * b) == c // (2 * b)) & (j // b != c // b) for b in (1, 2, 4, 8, 16, 32)]
    head_of = np.zeros((P, RT, 2 * RT), np.float32)
    for r in range(RT):
        head_of[:, r, 2 * r:2 * r + 2] = np.arange(P)[:, None] // HD == np.arange(2)[None, :]
    lam = np.zeros((DEPTH, P, 2), np.float32)
    for l in range(DEPTH):
        start = 0.8 - 0.6 * math.exp(-0.3 * l)
        lam[l] = start, 1.0 - start
    return {
        "const_ident": np.eye(P, dtype=np.float32),
        "const_cos": by_token(np.cos(angle)),
        "const_sin": by_token(np.sin(angle)),
        "const_jlt": earlier,
        "const_masks": np.ascontiguousarray(np.stack(masks, 1), np.float32),
        "const_dist": by_token(np.abs(t[:, None] - t[None, :]).astype(np.float32)),
        "const_heads": same.astype(np.float32),
        "const_headsel": head_of,
        "const_lam": lam,
    }


def kernel(**inputs):
    import concourse.bacc as _bacc
    from concourse.bass_utils import run_bass_kernel_spmd as _run

    nc = _bacc.Bacc("TRN2", target_bir_lowering=False, num_devices=1)
    arrays = {"in_" + name: np.ascontiguousarray(value) for name, value in inputs.items()}
    arrays.update(shape_constants())
    tensors = {name[3:] if name.startswith("in_") else name:
               nc.dram_tensor(name, value.shape, F32, kind="ExternalInput").ap() for name, value in arrays.items()}
    tensors["w_scratch"] = nc.dram_tensor("w_scratch", (E, S), F32, kind="Internal").ap()
    out = nc.dram_tensor("out", (1, S, D), F32, kind="ExternalOutput").ap()
    program(nc, tensors, out)
    result = _run(nc, [arrays], core_ids=[0])
    return result.results[0]["out"]
```

```python
import math
from contextlib import ExitStack

import numpy as np

import concourse.bass as bass
from concourse import mybir
from concourse.alu_op_type import AluOpType as ALU

ACT = mybir.ActivationFunctionType
F32 = mybir.dt.float32
F32R = mybir.dt.float32r
AX = mybir.AxisListType.X

P = 128
D = 1024
S = 256
DT = D // P
MT = S // P
DEPTH = 2
BANK = 512
HD = 64

QH, KVH = 8, 2
QW, KVW = QH * HD, KVH * HD
QKW = QW + KVW
SGU = 512
SG = 8
SGD = SGU // SG
TOKC = QW + 2 * KVW + 2 * SGU
E, TOPK, NG, PG, KEEP_G = 64, 8, 8, 8, 4
OCT = 8
FF = 256
ROUTED_SCALE = 2.5
ALPHA = (2 * DEPTH) ** 0.25
ADA = 6 * D
MODS = ADA // P
ROWS = MODS + SG + DT

RW = 512
RT = RW // P
LORA = 64
CRW = 3 * RW + 4 * LORA + P
CT = CRW // P
CAT = 3 * RW
DFF = 2816
STEPS = DFF // FF
CH = 64
NCH = S // CH
DECAY = 0.6065306597126334
BH = 4

A_SLOTS, A_W = 4, 4096
B_SLOTS, B_W = 4, 2048
NEG = -3.0e38
TAKEN = -3.3e38


def spread(ap, axis, n):
    a = ap.unsqueeze(axis)
    shape = list(a.shape)
    shape[axis] = n
    return a.broadcast_to(shape)


class Banks:

    def __init__(self, tensors, filled, freed):
        self.t, self.filled, self.freed = tensors, filled, freed
        self.count = [0] * len(tensors)
        self.claims = [0] * len(tensors)
        self.uses = {}

    def take(self, key, bank):
        assert key not in self.uses, key
        self.uses[key] = (bank, self.count[bank])
        self.count[bank] += 1

    def claim(self, pe, key):
        b, n = self.uses[key]
        assert self.claims[b] == n, key
        self.claims[b] += 1
        if n:
            pe.wait_ge(self.freed[b], n)
        return self.t[b]

    def fill(self, ins, key):
        ins.then_inc(self.filled[self.uses[key][0]], 1)

    def read(self, eng, key):
        b, n = self.uses[key]
        eng.wait_ge(self.filled[b], n + 1)
        return self.t[b]

    def free(self, ins, key):
        ins.then_inc(self.freed[self.uses[key][0]], 1)

    def evacuated(self, eng, key):
        b, n = self.uses[key]
        eng.wait_ge(self.freed[b], n + 1)


class Chain:

    def __init__(self, eng, sem):
        self.eng, self.sem, self.n = eng, sem, 0

    def mark(self, ins):
        self.n += 1
        ins.then_inc(self.sem, 1)

    def __call__(self, ins):
        self.mark(ins)
        self.eng.wait_ge(self.sem, self.n)
        return ins


class Splits:

    def __init__(self, nc, ctx, prefix):
        self.nc, self.ctx, self.prefix, self.twins = nc, ctx, prefix, {}

    def buffer(self, name, shape):
        at = self.nc.sbuf_base
        plain = self.ctx.enter_context(self.nc.sbuf_tensor(self.prefix + name, shape, F32))
        self.twin(plain[:], name, at)
        return plain

    def part(self, name, arena, at, lo, n):
        view = arena[:, lo:lo + n]
        self.twin(view, name, at + 4 * lo)
        return view

    def twin(self, view, name, at):
        assert at % 32 == 0
        n = 1
        for w in view.shape[1:]:
            n *= w
        twin = self.nc.alloc_sbuf_tensor_at(f"{self.prefix}{name}_parts", [P, n], F32R, offset=at)
        self.twins.setdefault(view.name, []).append((view.offset, n, twin))

    def __call__(self, ap):
        for lo, n, twin in self.twins[ap.name]:
            if lo <= ap.offset < lo + n:
                return bass.AP(twin, ap.offset - lo, [(n, P)] + list(ap.ap)[1:])
        raise KeyError(ap.name)

    def value(self, ap):
        return self(ap).bitcast(F32)


def first_block(nc, a, x_tok, consts):
    with ExitStack() as ctx:
        def sb(name, shape):
            return ctx.enter_context(nc.sbuf_tensor("f_" + name, shape, F32))

        parts_of = Splits(nc, ctx, "f_")

        def sem(name):
            return ctx.enter_context(nc.semaphore("f_" + name))

        ident, cosr, sinr, jlt = consts["ident"], consts["cos"], consts["sin"], consts["jlt"]

        ringA = parts_of.buffer("ringA", [P, A_SLOTS, A_W])
        ringB = parts_of.buffer("ringB", [P, B_SLOTS, B_W])
        hT = parts_of.buffer("hT", [P, DT, S])
        ARENA = 16384
        arena_at = nc.sbuf_base
        arena = sb("arena", [P, ARENA])
        lnp = sb("lnp", [P, 2, D])
        gate_b = sb("gate_b", [P, D])
        silu_g = sb("silu_g", [P, 2, BANK])
        hid = parts_of.buffer("hid", [P, 2, BANK])
        hid_high = parts_of.buffer("hid_high", [P, 2, BANK])
        rows = sb("rows", [ROWS, P])
        cols = sb("cols", [P, ROWS])
        mod = sb("mod", [P, MODS])
        modp1 = sb("modp1", [P, MODS])
        cond = sb("cond", [P, DT])
        one = sb("one", [P, 1])
        qks = sb("qks", [P, 2, HD])
        rw = sb("rw", [P, DT, E])
        rbias = sb("rbias", [P, E])
        stats = sb("stats", [P, MT, 2, 6])
        mv = sb("mv", [P, MT, 2])
        small = sb("small", [P, 320])
        wT = sb("wT", [E, S])

        at = [0]

        def part(n):
            at[0] += n
            assert at[0] <= ARENA, at
            return arena[:, at[0] - n:at[0]]

        tmp = part(2560)
        p_tok = part(MT * TOKC).rearrange("p (m c) -> p m c", m=MT)
        gates = part(2 * DT * S).rearrange("p (t s) -> p t s", s=S)
        turned = part(2304)
        qT = part(4 * S).rearrange("p (t s) -> p t s", s=S)
        kT = part(KVH * S).rearrange("p (t s) -> p t s", s=S)
        wsT = part(SG * P).rearrange("p (g i) -> p g i", g=SG)
        oaT = part(4 * S).rearrange("p (t s) -> p t s", s=S)
        obT = wsT.rearrange("p g i -> p (g i)").rearrange("p (t s) -> p t s", s=S)
        qkr = turned[:, 0:MT * QKW].rearrange("p (m c) -> p m c", m=MT)
        kdup = turned[:, MT * QKW:MT * QKW + MT * 4 * HD * 2]
        kdup = kdup.rearrange("p (m c) -> p m c", m=MT)
        yT = turned[:, 0:DT * S].rearrange("p (t s) -> p t s", s=S)
        v_ln = p_tok[:, :, 0:SGU]
        u0, v0 = QKW + KVW, QKW + KVW + SGU
        prob = tmp[:, 0:1024].rearrange("p (b m s) -> p b m s", b=2, m=MT)
        probT = tmp[:, 1024:2048].rearrange("p (b t s) -> p b t s", b=2, t=MT)
        router = tmp[:, 0:9 * MT * E].rearrange("p (n c) -> p n c", n=9)
        w_four = arena[:, 0:2 * 4 * S].rearrange("p (b e s) -> p b e s", b=2, s=S)
        hT_high = parts_of.part("hT_high", arena, arena_at, 2048, 2048).rearrange("p (t s) -> p t s", s=S)
        highA = parts_of.part("highA", arena, arena_at, 4096, 8192).rearrange("p (b c) -> p b c", b=2)
        highB = parts_of.part("highB", arena, arena_at, 12288, 4096).rearrange("p (b c) -> p b c", b=2)
        ws_nat = hid[:, :, :].rearrange("p a b -> p (a b)").rearrange("p (g j) -> p g j", g=SG)
        sums = hid_high
        late_sums, late_part = [lnp[:, h, :].rearrange("p (b c) -> p b c", b=2) for h in range(2)]
        sgu_ln = silu_g


        s_go = sem("layer_cleared")
        names = ["a_slot0", "a_slot1", "a_slot2", "a_slot3", "b_slot0", "b_slot1", "b_slot2",
                 "b_slot3", "wT_stored", "early_summed", "late_summed", "early_used", "late_used",
                 "pool_steps", "cond_ready", "mod_ready",
                 "rotated", "vln_ready", "gated_ready", "max_ready", "prob_ready", "merged", "var_ready",
                 "std_ready", "x_ready", "weights_ready", "hidden_ready", "down_done", "dve_steps", "rows_landed",
                 "highA_ready", "lowA_ready", "highB_ready", "lowB_ready", "hT_split", "weighted",
                 "four_landed0", "four_landed1", "arrived"]
        names += [f"bank_filled{i}" for i in range(8)] + [f"bank_freed{i}" for i in range(8)]
        each = {n: sem(n) for n in names}
        nums = [s.num for s in each.values()]
        cleared = range(min(nums), max(nums) + 1)
        assert len(cleared) == len(nums) and s_go.num not in cleared
        params_landed, ln1_landed, ln2_landed = sem("params_landed"), sem("ln1_landed"), sem("ln2_landed")
        a_landed = [each[f"a_slot{i}"] for i in range(A_SLOTS)]
        b_landed = [each[f"b_slot{i}"] for i in range(B_SLOTS)]
        early_summed, late_summed = each["early_summed"], each["late_summed"]
        early_used, late_used = each["early_used"], each["late_used"]
        pool_steps = each["pool_steps"]
        mod_ready, rotated = each["mod_ready"], each["rotated"]
        vln_ready, gated_ready, max_ready = each["vln_ready"], each["gated_ready"], each["max_ready"]
        prob_ready, merged, var_ready = each["prob_ready"], each["merged"], each["var_ready"]
        std_ready, x_ready, weights_ready = each["std_ready"], each["x_ready"], each["weights_ready"]
        hidden_ready, down_done, dve_steps = each["hidden_ready"], each["down_done"], each["dve_steps"]
        wT_stored = each["wT_stored"]
        highA_ready, lowA_ready, highB_ready = each["highA_ready"], each["lowA_ready"], each["highB_ready"]
        four_landed = [each["four_landed0"], each["four_landed1"]]
        lowB_ready, hT_split, weighted = each["lowB_ready"], each["hT_split"], each["weighted"]
        arrived, cond_ready = each["arrived"], each["cond_ready"]
        rows_landed = each["rows_landed"]
        filled = [each[f"bank_filled{i}"] for i in range(8)]
        freed = [each[f"bank_freed{i}"] for i in range(8)]

        banks = Banks([ctx.enter_context(nc.psum_tensor(f"f_bank{i}", [P, BANK], F32)) for i in range(8)],
                      filled, freed)

        for b in range(4):
            banks.take(("xT", b), b)
        banks.take("cols", 5)
        banks.take("ada", 4)
        gemm = [("q", 0), ("q", 1), ("kv", 0), ("kv", 1), ("u", 0), ("u", 1), ("v", 0), ("v", 1)]
        for n, key in enumerate(gemm):
            banks.take(key, n % 4)
        banks.take("rest ada", 1)
        for g in range(4):
            banks.take(("gates", g), (0, 2, 3, 0)[g])
        for g in range(2):
            banks.take(("wsT", g), 4 + g)
        for g in range(3):
            banks.take(("qkT", g), (6, 7, 4)[g])
        for m in range(MT):
            banks.take(("sv", m), 2 + m)
        for h in range(QH + 1):
            if 1 <= h <= 4:
                banks.take(("gates", 3 + h), 0)
            if h < QH:
                banks.take(("score", h), 4 + h % 2)
            if h:
                banks.take(("probT", h - 1), 6 + (h - 1) % 2)
                if h % 2:
                    banks.take(("oT", h // 2), 2 + (h // 2) % 2)
        for g in range(2):
            banks.take(("obT", g), g)
        for t in range(DT):
            banks.take(("branch", t), t % 4)
        for g in range(2):
            banks.take(("gate1", g), 4 + g)
        for n in range(2):
            for m in range(MT):
                banks.take(("out", n, m), 2 * n + m)
        for b in range(4):
            banks.take(("x2T", b), b)
        for g in range(2):
            banks.take(("gate2", g), 4 + g)
        banks.take("router", 6)
        banks.take(("g", "shared"), 4)
        banks.take(("u", "shared"), 5)
        for n in range(4):
            banks.take(("y", n), n)
        banks.take("wT", 7)
        first_turn = list(banks.count)

        n_ada, n_in = ADA // 512, 8
        third = n_ada // 3
        stream = [("ada", c) for c in range(third)]
        stream += [("in", 0), ("ada", 8), ("in", 1), ("in", 2), ("ada", 9), ("in", 3), ("in", 4), ("ada", 4),
                   ("in", 5), ("ada", 5), ("ada", 10), ("in", 6), ("ada", 6), ("in", 7), ("ada", 7), ("ada", 11)]
        assert len(stream) == n_ada + n_in and third == 4
        a_ada = [stream.index(("ada", c)) for c in range(n_ada)]
        a_in = [stream.index(("in", c)) for c in range(n_in)]
        a_wa = len(stream)
        a_wb, a_out, a_shared = a_wa + 1, a_wa + 2, a_wa + 4
        a_exp = a_shared + 1
        last_use = {a_in[c]: (name, 1) for c, name in enumerate(("q", "kv", "u", "v"))}
        last_use |= {a_in[4 + c]: ("gates", 2 * c + 1) for c in range(4)}
        last_use |= {a_wa: ("branch", DT - 1), a_wb: ("branch", DT - 1), a_out: ("out", 0, 1),
                     a_out + 1: ("out", 1, 1), a_shared: ("u", "shared")}

        def slotA(n):
            return ringA[:, n % A_SLOTS, :]

        def slotB(n):
            return ringB[:, n % B_SLOTS, :]

        def octets(eng, turn_):
            turn_(0)
            with eng.Fori(1, E // OCT - 1) as i:
                turn_(i)
            turn_(E // OCT - 1)

        def start_of(i, j):
            return isinstance(i, int) and i == 0 and j == 0

        def end_of(i, j):
            return isinstance(i, int) and i == E // OCT - 1 and j == OCT - 1

        def rows8(ap):
            return ap.rearrange("p (k c) -> p k c", k=DT)

        def sums_free(eng, c):
            if c >= 2 * third:
                if c >= 2 * third + 2:
                    eng.wait_ge(late_used, c - 2 - 2 * third + 1)
            elif c - 2 == third - 1:
                banks.read(eng, "ada")
            elif c >= 2:
                eng.wait_ge(early_used, c - 1 if c - 2 < third else c - 2)

        block = ctx.enter_context(nc.Block())

        def leave(eng, l):
            eng.nop().then_inc(arrived, 1)
            eng.wait_ge(s_go, l + 1)

        def on_all(src):
            return src.unsqueeze(0).broadcast_to([P] + list(src.shape))

        @block.sync
        def _(sp):
            with sp.Fori(0, DEPTH) as l:
                def slot_free(n):
                    old = n - A_SLOTS
                    if old in last_use:
                        banks.read(sp, last_use[old])
                    elif old >= 0:
                        c = stream[old][1]
                        sp.wait_ge(late_summed if c >= 2 * third else early_summed, c % (2 * third) + 1)

                def load(n, dst, src):
                    slot_free(n)
                    half = dst.shape[1] // 2
                    for h in range(2):
                        sp.dma_start(dst[:, h * half:(h + 1) * half], src[:, h * half:(h + 1) * half]
                                     ).then_inc(a_landed[n % A_SLOTS], 16)

                def load_ada(n, c):
                    load(n, rows8(slotA(n)),
                         a["w_ada"][l, :, c * 512:(c + 1) * 512].rearrange("(k p) c -> p k c", p=P))

                def row(dst, src):
                    sp.dma_start(dst, src).then_inc(rows_landed, 16)

                row(rows[0:MODS, :], a["b_ada"][l].rearrange("(m p) -> m p", p=P))
                row(rows[MODS:MODS + SG, :], a["b_spatial"][l])
                row(rows[MODS + SG:ROWS, :], a["c"][0].rearrange("(j p) -> j p", p=P))
                edges = [0, QW, u0, v0, TOKC] + [TOKC + 512 * (i + 1) for i in range(4)]
                for n, (kind, c) in enumerate(stream):
                    if kind == "ada":
                        load_ada(n, c)
                    else:
                        w = edges[c + 1] - edges[c]
                        load(n, rows8(slotA(n))[:, :, 0:w],
                             a["w_in"][l, :, edges[c]:edges[c + 1]].rearrange("(k p) c -> p k c", p=P))
                for n, name in ((a_wa, "w_branch_a"), (a_wb, "w_branch_b")):
                    load(n, slotA(n).rearrange("p (k c) -> p k c", k=4),
                         a[name][l].rearrange("(k p) c -> p k c", p=P))
                for c in range(2):
                    load(a_out + c, rows8(slotA(a_out + c)),
                         a["w_out"][l, :, c * 512:(c + 1) * 512].rearrange("(k p) c -> p k c", p=P))

                def gate_up_down(nA, nB, srcs):
                    gu = slotA(nA).rearrange("p (h k c) -> p h k c", h=2, k=DT)
                    for half in range(2):
                        sp.dma_start(gu[:, half], srcs[half].rearrange("(k p) c -> p k c", p=P)
                                     ).then_inc(a_landed[nA % A_SLOTS], 16)
                    yield
                    sp.dma_start(slotB(nB).rearrange("p (k c) -> p k c", k=2),
                                 srcs[2].rearrange("(k p) c -> p k c", p=P)
                                 ).then_inc(b_landed[nB % B_SLOTS], 16)
                    yield

                slot_free(a_shared)
                for _ in gate_up_down(a_shared, 0, [a[n][l] for n in ("ws_gate", "ws_up", "ws_down")]):
                    pass

                def expert(i, j):
                    e = i * OCT + j
                    steps = gate_up_down(a_exp + j, 1 + j, [a[n][l, e] for n in ("w_gate", "w_up", "w_down")])
                    b = 5 + 2 * (j % 2)
                    if isinstance(i, int) and j < 4:
                        slot_free(a_exp + j)
                    else:
                        sp.wait_ge(filled[b], i * (OCT // 2) + (first_turn[b] + j // 2 - 1))
                    next(steps)
                    if not isinstance(i, int) or 1 + j >= B_SLOTS:
                        sp.wait_ge(down_done, i * OCT + (j - 2))
                    next(steps)

                def four_weights(i, h):
                    sp.dma_start(w_four[:, h], on_all(a["w_scratch"][bass.ds(i * OCT + 4 * h, 4), :])
                                 ).then_inc(four_landed[h], 16)

                for j in range(OCT):
                    expert(0, j)
                    if j == 3:
                        sp.wait_ge(wT_stored, 16)
                        for h in range(2):
                            four_weights(0, h)
                with sp.Fori(1, E // OCT) as i:
                    for j in range(OCT):
                        if j % 4 == 0:
                            sp.wait_ge(hidden_ready, i * OCT + (j - 3))
                            four_weights(i, j // 4)
                        expert(i, j)
                sp.wait_ge(arrived, 4)
                sp.sem_clear(cleared)
                sp.nop().then_inc(s_go, 1)

        @block.gpsimd
        def _(pool):
            with pool.Fori(0, DEPTH) as l:
                def param(dst, src):
                    pool.dma_start(dst, src).then_inc(params_landed, 16)

                param(qks[:, 0, :], on_all(a["q_scale"][l]))
                param(qks[:, 1, :], on_all(a["k_scale"][l]))
                param(sgu_ln[:, 0, :], on_all(a["sgu_ln_g"][l]))
                param(sgu_ln[:, 1, :], on_all(a["sgu_ln_b"][l]))
                param(ws_nat, a["w_spatial"][l].rearrange("g i j -> i g j"))
                param(rw[:, :, :], a["router_w"][l].rearrange("(k p) e -> p k e", p=P))
                param(rbias[:, :], on_all(a["router_bias"][l]))
                step = Chain(pool, pool_steps)
                pool.wait_ge(cond_ready, 1)
                for c in range(2 * third, n_ada):
                    n = a_ada[c]
                    pool.wait_ge(a_landed[n % A_SLOTS], 32 * (n // A_SLOTS + 1))
                    sums_free(pool, c)
                    w, out, engine = rows8(slotA(n)), late_sums[:, c % 2, :], nc.gpsimd
                    step(engine.tensor_scalar(out, w[:, 0, :], cond[:, 0:1], None, ALU.mult))
                    for k in range(1, DT):
                        part_ = late_part[:, k % 2, :]
                        step(engine.tensor_scalar(part_, w[:, k, :], cond[:, k:k + 1], None, ALU.mult))
                        last = engine.tensor_tensor(out, out, part_, ALU.add)
                        if k < DT - 1:
                            step(last)
                    last.then_inc(late_summed, 1)
                banks.read(pool, "rest ada")
                for half, name in enumerate(("ln1_g", "ln1_b")):
                    pool.dma_start(lnp[:, half, :], on_all(a[name][l])).then_inc(ln1_landed, 16)
                pool.wait_ge(x_ready, 1)
                for half, name in enumerate(("ln2_g", "ln2_b")):
                    pool.dma_start(lnp[:, half, :], on_all(a[name][l])).then_inc(ln2_landed, 16)
                leave(pool, l)
        n_params = 16 * 7

        @block.tensor
        def _(pe):
            mm = nc.tensor.matmul
            turn = nc.tensor.transpose

            def landed(n):
                pe.wait_ge(a_landed[n % A_SLOTS], 32 * (n // A_SLOTS + 1))

            def to_features(name, src, n_banks):
                for b in range(n_banks):
                    ps = banks.claim(pe, (name, b))
                    for t in range(2):
                        for m in range(MT):
                            o = t * S + m * P
                            last = turn(ps[:, o:o + P], src[:, m, (2 * b + t) * P:(2 * b + t + 1) * P],
                                        ident[:, :])
                    banks.fill(last, (name, b))

            def gate_rows(name, first):
                for g in range(2):
                    ps = banks.claim(pe, (name, g))
                    for t in range(4):
                        j = first + 4 * g + t
                        last = mm(ps[:, t * P:(t + 1) * P], mod[:, j:j + 1].broadcast_to([P, P]),
                                  ident[:, :], start=True, stop=True)
                    banks.fill(last, (name, g))

            def hidden(ps, w):
                for t in range(2):
                    for k in range(DT):
                        last = mm(ps[:, t * S:(t + 1) * S], w[:, k, t * P:(t + 1) * P], hT[:, k, :],
                                  start=(k == 0), stop=(k == DT - 1))
                return last

            def up(half, slot, place, ps, done, fresh=False):
                low, high = [w.rearrange("p (h k c) -> p h k c", h=2, k=DT)[:, half]
                             for w in (slot, highA[:, place, :])]
                for t in range(2):
                    for k in range(DT):
                        if fresh and t == 0 and k % 2 == 0:
                            pe.wait_ge(hT_split, k // 2 + 1)
                        for x, (wx, hx) in enumerate(((high, hT_high), (high, hT), (low, hT_high))):
                            last = mm(ps[:, t * S:(t + 1) * S], parts_of(wx[:, k, t * P:(t + 1) * P]),
                                      parts_of(hx[:, k, :]), start=(k == 0 and x == 0),
                                      stop=(k == DT - 1 and x == 2))
                last.then_inc(done, 1)

            def down(place, slot, start):
                low, high = [w.rearrange("p (k c) -> p k c", k=2) for w in (slot, highB[:, place, :])]
                for m in range(MT):
                    for n in range(2):
                        for k in range(2):
                            o = k * S + m * P
                            for x, (hx, wx) in enumerate(((hid_high, high), (hid, high), (hid_high, low))):
                                last = mm(banks.t[2 * m + n][:, :], parts_of(hx[:, place, o:o + P]),
                                          parts_of(wx[:, k, n * 512:(n + 1) * 512]),
                                          start=start and k == 0 and x == 0, stop=False, skip_group_check=True)
                last.then_inc(down_done, 1)

            pe.wait_ge(consts["landed"], consts["count"])
            pe.wait_ge(consts["x_landed"], 32)
            with pe.Fori(0, DEPTH) as l:
                pe.wait_ge(rows_landed, 16 * 3)
                to_features("xT", x_tok, 4)
                ps = banks.claim(pe, "cols")
                banks.fill(turn(ps[:, 0:ROWS], rows[:, :], ident[0:ROWS, 0:ROWS]), "cols")

                def ada_columns(c):
                    if c in (0, 2 * third):
                        banks.claim(pe, "rest ada" if c else "ada")
                    ps = banks.t[banks.uses["rest ada" if c >= third else "ada"][0]]
                    late = c >= 2 * third
                    pe.wait_ge(late_summed if late else early_summed, c % (2 * third) + 1)
                    for t in range(4):
                        col = 4 * (c - third if c >= third else c) + t
                        last = mm(ps[:, col:col + 1], (late_sums if late else sums)[:, c % 2, t * P:(t + 1) * P],
                                  one[:, :], start=True, stop=True)
                    if c in (third - 1, n_ada - 1):
                        banks.fill(last, "rest ada" if c >= third else "ada")
                    else:
                        last.then_inc(late_used if late else early_used, 1)

                def gate_columns(g):
                    w = rows8(slotA(a_in[4 + g // 2]))
                    if g % 2 == 0:
                        landed(a_in[4 + g // 2])
                    ps = banks.claim(pe, ("gates", g))
                    o = 2 * (g % 2) * P
                    banks.fill(hidden(ps, w[:, :, o:o + 2 * P]), ("gates", g))

                for c in range(third):
                    ada_columns(c)

                for b in range(4):
                    banks.evacuated(pe, ("xT", b))
                for c, name in enumerate(("q", "kv", "u", "v")):
                    width = 2 * KVW if name == "kv" else 512
                    w = rows8(slotA(a_in[c]))
                    landed(a_in[c])
                    for m in range(MT):
                        ps = banks.claim(pe, (name, m))
                        for k in range(DT):
                            last = mm(ps[:, 0:width], hT[:, k, m * P:(m + 1) * P], w[:, k, 0:width],
                                      start=(k == 0), stop=(k == DT - 1))
                        banks.fill(last, (name, m))
                for g in range(4):
                    gate_columns(g)
                    if g == 1:
                        ada_columns(8)
                ada_columns(4)

                pe.wait_ge(params_landed, l * n_params + n_params)
                for g in range(2):
                    ps = banks.claim(pe, ("wsT", g))
                    for i in range(4):
                        last = turn(ps[:, i * P:(i + 1) * P], ws_nat[:, 4 * g + i, :], ident[:, :])
                    banks.fill(last, ("wsT", g))
                pe.wait_ge(rotated, 1)
                for g in range(3):
                    ps = banks.claim(pe, ("qkT", g))
                    for t in range(2):
                        for m in range(MT):
                            src = kdup[:, m, t * P:(t + 1) * P] if g == 2 else \
                                qkr[:, m, (2 * g + t) * P:(2 * g + t + 1) * P]
                            last = turn(ps[:, t * S + m * P:t * S + (m + 1) * P], src, ident[:, :])
                    banks.fill(last, ("qkT", g))
                for g in range(2):
                    banks.evacuated(pe, ("wsT", g))
                pe.wait_ge(vln_ready, 1)
                for m in range(MT):
                    ps = banks.claim(pe, ("sv", m))
                    for g in range(SG):
                        last = mm(ps[:, g * SGD:(g + 1) * SGD], wsT[:, g, :],
                                  v_ln[:, m, g * SGD:(g + 1) * SGD], start=True, stop=True)
                    banks.fill(last, ("sv", m))

                for g in range(3):
                    banks.evacuated(pe, ("qkT", g))
                beside = {0: [9], 1: [5], 3: [6], 4: [10], 5: [7], 8: [11]}
                for h in range(QH + 1):
                    if 1 <= h <= 4:
                        gate_columns(3 + h)
                    for c in beside.get(h, []):
                        ada_columns(c)
                    if h < QH:
                        o = (h % 2) * HD
                        ps = banks.claim(pe, ("score", h))
                        for m in range(MT):
                            last = mm(ps[:, m * S:(m + 1) * S], qT[o:o + HD, h // 2, m * P:(m + 1) * P],
                                      kT[o:o + HD, h // (QH // KVH), :], start=True, stop=True)
                        banks.fill(last, ("score", h))
                    if h:
                        g = h - 1
                        pe.wait_ge(prob_ready, g + 1)
                        ps = banks.claim(pe, ("probT", g))
                        for t in range(MT):
                            for m in range(MT):
                                last = turn(ps[:, t * S + m * P:t * S + (m + 1) * P],
                                            prob[:, g % 2, m, t * P:(t + 1) * P], ident[:, :])
                        banks.fill(last, ("probT", g))
                        banks.evacuated(pe, ("probT", g))
                        key = ("oT", g // 2)
                        ps = banks.claim(pe, key) if g % 2 == 0 else banks.t[banks.uses[key][0]]
                        o, kv = (g % 2) * HD, QKW + (g // (QH // KVH)) * HD
                        for t in range(MT):
                            last = mm(ps[o:o + HD, 0:S], p_tok[:, t, kv:kv + HD], probT[:, g % 2, t, :],
                                      start=(t == 0), stop=(t == MT - 1))
                        if g % 2:
                            banks.fill(last, key)

                pe.wait_ge(gated_ready, MT)
                to_features("obT", p_tok[:, :, u0:u0 + SGU], 2)

                landed(a_wa)
                landed(a_wb)
                for g in range(4):
                    banks.evacuated(pe, ("oT", g))
                for g in range(2):
                    banks.evacuated(pe, ("obT", g))
                for t in range(DT):
                    ps = banks.claim(pe, ("branch", t))
                    for half, (n, src) in enumerate(((a_wa, oaT), (a_wb, obT))):
                        w = slotA(n).rearrange("p (k c) -> p k c", k=4)
                        for k in range(4):
                            last = mm(ps[:, half * S:(half + 1) * S], w[:, k, t * P:(t + 1) * P], src[:, k, :],
                                      start=(k == 0), stop=(k == 3))
                    banks.fill(last, ("branch", t))
                pe.wait_ge(mod_ready, 2)
                gate_rows("gate1", 2 * DT)

                pe.wait_ge(merged, DT)
                for n in range(2):
                    w = rows8(slotA(a_out + n))
                    landed(a_out + n)
                    for m in range(MT):
                        ps = banks.claim(pe, ("out", n, m))
                        for k in range(DT):
                            last = mm(ps[:, :], yT[:, k, m * P:(m + 1) * P], w[:, k, :],
                                      start=(k == 0), stop=(k == DT - 1))
                        banks.fill(last, ("out", n, m))

                pe.wait_ge(x_ready, 1)
                to_features("x2T", x_tok, 4)
                pe.wait_ge(mod_ready, 2)
                gate_rows("gate2", 5 * DT)
                for b in range(4):
                    banks.evacuated(pe, ("x2T", b))
                ps = banks.claim(pe, "router")
                for m in range(MT):
                    for k in range(DT):
                        last = mm(ps[:, m * E:(m + 1) * E], hT[:, k, m * P:(m + 1) * P], rw[:, k, :],
                                  start=(k == 0), stop=(k == DT - 1))
                banks.fill(last, "router")

                pe.wait_ge(lowA_ready, 1)
                for half, name in enumerate("gu"):
                    ps = banks.claim(pe, (name, "shared"))
                    up(half, slotA(a_shared), 0, ps, filled[banks.uses[(name, "shared")][0]], half == 0)
                for n in range(4):
                    banks.claim(pe, ("y", n))

                def turn_of(i):
                    for j in range(OCT):
                        b = 4 + 2 * (j % 2)
                        pe.wait_ge(lowA_ready, i * OCT + (j + 2))
                        for q in range(2):
                            pe.wait_ge(freed[b + q], i * (OCT // 2) + (first_turn[b + q] + j // 2))
                            up(q, slotA(a_exp + j), (j + 1) % 2, banks.t[b + q], filled[b + q])
                        if start_of(i, j):
                            pe.wait_ge(weights_ready, 1)
                            ps = banks.claim(pe, "wT")
                            for m in range(MT):
                                last = turn(ps[0:E, m * P:(m + 1) * P], router[:, 8, m * E:(m + 1) * E],
                                            ident[:, :])
                            banks.fill(last, "wT")
                        pe.wait_ge(lowB_ready, i * OCT + (j + 1))
                        pe.wait_ge(hidden_ready, i * OCT + (j + 1))
                        down(j % 2, slotB(j), start_of(i, j))

                octets(pe, turn_of)
                pe.wait_ge(lowB_ready, E + 1)
                pe.wait_ge(hidden_ready, E + 1)
                down(0, slotB(0), False)
                leave(pe, l)

        @block.scalar
        def _(act):
            f = nc.scalar.activation

            def roots(n, width):
                act.wait_ge(var_ready, n)
                f(small[:, 32:32 + width], small[:, 0:width], ACT.Sqrt).then_inc(std_ready, 1)

            def modulate(name, bank, shift, scale):
                ps = banks.read(act, (name, bank))
                for t in range(2):
                    j = 2 * bank + t
                    last = f(hT[:, j, :], ps[:, t * S:(t + 1) * S], ACT.Identity,
                             bias=mod[:, shift + j:shift + j + 1], scale=modp1[:, scale + j:scale + j + 1])
                    if name == "x2T":
                        last = f(parts_of(hT_high[:, j, :]), ps[:, t * S:(t + 1) * S], ACT.Identity,
                                 bias=mod[:, shift + j:shift + j + 1], scale=modp1[:, scale + j:scale + j + 1])
                banks.free(last, (name, bank))

            def take(key, dst, view, func=ACT.Copy):
                banks.free(f(dst, view(banks.read(act, key)), func), key)

            def split_up(i, j):
                n, b = a_exp + j, 5 + 2 * (j % 2)
                act.wait_ge(a_landed[n % A_SLOTS], i * (OCT * 8) + 32 * (n // A_SLOTS + 1))
                if isinstance(i, int) and i == 0 and j == 1:
                    banks.read(act, ("u", "shared"))
                elif not isinstance(i, int) or i * OCT + j > 1:
                    act.wait_ge(filled[b], i * (OCT // 2) + (first_turn[b] + j // 2))
                f(parts_of(highA[:, (j + 1) % 2, :]), slotA(n), ACT.Copy).then_inc(highA_ready, 1)

            def split_down(i, j):
                n = 1 + j
                act.wait_ge(b_landed[n % B_SLOTS], i * (OCT * 4) + 16 * (n // B_SLOTS + 1))
                if not isinstance(i, int) or i * OCT + j > 0:
                    act.wait_ge(down_done, i * OCT + j)
                f(parts_of(highB[:, n % 2, :]), slotB(n), ACT.Copy).then_inc(highB_ready, 1)

            with act.Fori(0, DEPTH) as l:
                take("cols", cols[:, :], lambda ps: ps[:, 0:ROWS])
                banks.evacuated(act, "cols")
                f(cond[:, :], cols[:, MODS + SG:ROWS], ACT.Silu).then_inc(cond_ready, 1)
                act.wait_ge(mod_ready, 1)
                for b in range(2):
                    modulate("xT", b, 0, DT)
                for m in range(MT):
                    take(("q", m), p_tok[:, m, 0:QW], lambda ps: ps[:, :])
                for m in range(MT):
                    take(("kv", m), p_tok[:, m, QW:u0], lambda ps: ps[:, 0:2 * KVW])
                roots(1, MT * 10)
                for name, c0 in (("u", u0), ("v", v0)):
                    for m in range(MT):
                        take((name, m), p_tok[:, m, c0:c0 + SGU], lambda ps: ps[:, :], ACT.Gelu)
                roots(2, MT)
                def take_gates(g):
                    take(("gates", g), gates[:, 2 * g:2 * g + 2, :],
                         lambda ps: ps[:, :].rearrange("p (t s) -> p t s", t=2), ACT.Sigmoid)

                for g in range(4):
                    take_gates(g)
                for g in range(3):
                    dst = kT if g == 2 else qT[:, 2 * g:2 * g + 2, :]
                    take(("qkT", g), dst, lambda ps: ps[:, :].rearrange("p (t s) -> p t s", t=2))
                for h in range(QH + 1):
                    if 1 <= h <= 4:
                        take_gates(3 + h)
                    if h < QH:
                        act.wait_ge(max_ready, h + 1)
                        if h >= 2:
                            banks.read(act, ("probT", h - 2))
                        ps = banks.t[banks.uses[("score", h)][0]]
                        for m in range(MT):
                            last = f(prob[:, h % 2, m, :], ps[:, m * S:(m + 1) * S], ACT.Exp,
                                     bias=small[:, 104 + 2 * (h % 2) + m:105 + 2 * (h % 2) + m],
                                     scale=HD ** -0.5,
                                     accum_out=small[:, 108 + 2 * (h % 2) + m:109 + 2 * (h % 2) + m])
                        banks.free(last, ("score", h))
                    if h:
                        g = h - 1
                        take(("probT", g), probT[:, g % 2, :, :],
                             lambda ps: ps[:, :].rearrange("p (t s) -> p t s", t=2))
                        if g % 2:
                            take(("oT", g // 2), oaT[:, g // 2, :], lambda ps: ps[:, 0:S])
                for g in range(2):
                    take(("obT", g), obT[:, 2 * g:2 * g + 2, :],
                         lambda ps: ps[:, :].rearrange("p (t s) -> p t s", t=2))
                banks.read(act, ("out", 1, 1))
                split_up(0, -1)
                roots(3, MT)
                split_down(0, -1)
                act.wait_ge(mod_ready, 2)
                for b in range(2):
                    modulate("x2T", b, 3 * DT, 4 * DT)
                take("router", router[:, 0, :], lambda ps: ps[:, 0:MT * E], ACT.Sigmoid)
                split_up(0, 0)
                take(("g", "shared"), silu_g[:, 0, :], lambda ps: ps[:, :], ACT.Silu)
                take("wT", wT[:, :], lambda ps: ps[0:E, 0:S])
                banks.evacuated(act, "wT")
                act.dma_start(a["w_scratch"], wT[:, :]).then_inc(wT_stored, 16)

                def turn_of(i):
                    for j in range(OCT):
                        split_down(i, j)
                        if not end_of(i, j):
                            split_up(i, j + 1)
                        b = 4 + 2 * (j % 2)
                        if not start_of(i, j):
                            act.wait_ge(hidden_ready, i * OCT + j)
                        act.wait_ge(filled[b], i * (OCT // 2) + (first_turn[b] + j // 2 + 1))
                        f(silu_g[:, (j + 1) % 2, :], banks.t[b][:, :], ACT.Silu).then_inc(freed[b], 1)

                octets(act, turn_of)
                roots(4, MT)
                leave(act, l)

        @block.vector
        def _(dve):
            v = nc.vector
            tt, ts, red = v.tensor_tensor, v.tensor_scalar, v.tensor_reduce

            dve.wait_ge(consts["landed"], consts["count"])
            dve.wait_ge(consts["x_landed"], 32)
            v.memset(one[:, :], 1.0)
            with dve.Fori(0, DEPTH) as l:
                step = Chain(dve, dve_steps)

                def modulate(name, bank, shift, scale):
                    ps = banks.read(dve, (name, bank))
                    for t in range(2):
                        j = 2 * bank + t
                        last = ts(hT[:, j, :], ps[:, t * S:(t + 1) * S], modp1[:, scale + j:scale + j + 1],
                                  mod[:, shift + j:shift + j + 1], ALU.mult, ALU.add)
                        if name == "x2T":
                            last = ts(parts_of(hT_high[:, j, :]), ps[:, t * S:(t + 1) * S],
                                      modp1[:, scale + j:scale + j + 1], mod[:, shift + j:shift + j + 1],
                                      ALU.mult, ALU.add)
                    banks.free(last, (name, bank))

                def split_up(i, j):
                    w = slotA(a_exp + j)
                    dve.wait_ge(highA_ready, i * OCT + (j + 2))
                    tt(parts_of(w), w, parts_of.value(highA[:, (j + 1) % 2, :]), ALU.subtract).then_inc(lowA_ready, 1)

                def split_down(i, j):
                    w = slotB(1 + j)
                    dve.wait_ge(highB_ready, i * OCT + (j + 2))
                    tt(parts_of(w), w, parts_of.value(highB[:, (j + 1) % 2, :]), ALU.subtract).then_inc(lowB_ready, 1)

                def take_gate(name):
                    for g in range(2):
                        ps = banks.read(dve, (name, g))
                        banks.free(v.tensor_copy(gate_b[:, g * 512:(g + 1) * 512], ps[:, :]), (name, g))
                    for g in range(2):
                        banks.evacuated(dve, (name, g))

                def residual(ps, m, n, done):
                    t = tmp[:, 512 * n:512 * (n + 1)] if done is not None else \
                        silu_g[:, n, :]
                    xs = x_tok[:, m, n * 512:(n + 1) * 512]
                    gated = tt(t, ps[:, :], gate_b[:, n * 512:(n + 1) * 512], ALU.mult)
                    if done is None:
                        step(gated)
                    else:
                        banks.free(gated, done)
                        banks.evacuated(dve, done)
                    step(v.scalar_tensor_tensor(xs, xs, ALPHA, t, ALU.mult, ALU.add))

                def norm_x(n, landed, done):
                    for m in range(MT):
                        for h in range(2):
                            last = v.bn_stats(stats[:, m, h, :], x_tok[:, m, h * 512:(h + 1) * 512])
                    step(last)
                    for m in range(MT):
                        last = v.bn_aggr(mv[:, m, :], stats[:, m, :, :].rearrange("p a b -> p (a b)"))
                    step(last)
                    ts(small[:, 0:MT], mv[:, :, 1], 1e-5, None, ALU.add).then_inc(var_ready, 1)
                    dve.wait_ge(std_ready, n)
                    step(v.reciprocal(small[:, 64:64 + MT], small[:, 32:32 + MT]))
                    for m in range(MT):
                        last = ts(x_tok[:, m, :], x_tok[:, m, :], mv[:, m, 0:1], small[:, 64 + m:65 + m],
                                  ALU.subtract, ALU.mult)
                    step(last)
                    dve.wait_ge(landed, l * 32 + 32)
                    for m in range(MT):
                        last = tt(x_tok[:, m, :], x_tok[:, m, :], lnp[:, 0, :], ALU.mult)
                    step(last)
                    for m in range(MT):
                        last = tt(x_tok[:, m, :], x_tok[:, m, :], lnp[:, 1, :], ALU.add)
                    last.then_inc(x_ready, 1)
                    dve.wait_ge(x_ready, done)

                dve.wait_ge(cond_ready, 1)

                def sum_chunk(c):
                    n = a_ada[c]
                    dve.wait_ge(a_landed[n % A_SLOTS], 32 * (n // A_SLOTS + 1))
                    sums_free(dve, c)
                    w, out = rows8(slotA(n)), sums[:, c % 2, :]
                    last = ts(out, w[:, 0, :], cond[:, 0:1], None, ALU.mult)
                    for k in range(1, DT):
                        step(last)
                        last = v.scalar_tensor_tensor(out, w[:, k, :], cond[:, k:k + 1], out, ALU.mult, ALU.add)
                    last.then_inc(early_summed, 1)

                for c in range(third):
                    sum_chunk(c)

                def take_mod(n):
                    name, c0, c1 = (("ada", 0, 4 * third), ("rest ada", 4 * third, MODS))[n]
                    ps = banks.read(dve, name)
                    banks.free(tt(mod[:, c0:c1], ps[:, 0:c1 - c0], cols[:, c0:c1], ALU.add), name)
                    banks.evacuated(dve, name)
                    ts(modp1[:, c0:c1], mod[:, c0:c1], 1.0, None, ALU.add).then_inc(mod_ready, 1)
                    dve.wait_ge(mod_ready, n + 1)

                take_mod(0)
                for b in range(2, 4):
                    modulate("xT", b, 0, DT)

                NH = QH + KVH
                for key in (("q", 0), ("q", 1), ("kv", 0), ("kv", 1)):
                    banks.evacuated(dve, key)
                dve.wait_ge(params_landed, l * n_params + n_params)
                qn = tmp[:, 0:MT * QKW].rearrange("p (m c) -> p m c", m=MT)
                for m in range(MT):
                    last = tt(qn[:, m, :], p_tok[:, m, 0:QKW], p_tok[:, m, 0:QKW], ALU.mult)
                step(last)
                step(red(small[:, 64:64 + MT * NH], tmp[:, 0:MT * QKW].rearrange("p (h d) -> p h d", d=HD),
                         AX, ALU.add))
                ts(small[:, 0:MT * NH], small[:, 64:64 + MT * NH], 1.0 / HD, 1e-6, ALU.mult, ALU.add
                   ).then_inc(var_ready, 1)
                dve.wait_ge(std_ready, 1)
                step(v.reciprocal(small[:, 64:64 + MT * NH], small[:, 32:32 + MT * NH]))
                qh = qn.rearrange("p m (h d) -> p m h d", d=HD)
                for m in range(MT):
                    last = tt(qh[:, m], p_tok[:, m, 0:QKW].rearrange("p (h d) -> p h d", d=HD),
                              spread(small[:, 64 + m * NH:64 + (m + 1) * NH], 2, HD), ALU.mult)
                step(last)
                for m in range(MT):
                    tt(qh[:, m, 0:QH], qh[:, m, 0:QH], spread(qks[:, 0, :], 1, QH), ALU.mult)
                    last = tt(qh[:, m, QH:NH], qh[:, m, QH:NH], spread(qks[:, 1, :], 1, KVH), ALU.mult)
                step(last)
                half = NH * HD // 2
                parts = [tmp[:, MT * QKW + n * half:MT * QKW + (n + 1) * half].rearrange(
                    "p (h d) -> p h d", d=HD // 2) for n in range(4)]
                for m in range(MT):
                    even, odd = qh[:, m, :, 0::2], qh[:, m, :, 1::2]
                    c, s = spread(cosr[:, m, :], 1, NH), spread(sinr[:, m, :], 1, NH)
                    for n, (x, y) in enumerate(((even, c), (odd, s), (even, s), (odd, c))):
                        last = tt(parts[n], x, y, ALU.mult)
                    step(last)
                    out = qkr[:, m, :].rearrange("p (h d) -> p h d", d=HD)
                    tt(out[:, :, 0::2], parts[0], parts[1], ALU.subtract)
                    step(tt(out[:, :, 1::2], parts[2], parts[3], ALU.add))
                for m in range(MT):
                    for g in range(KVH):
                        last = v.tensor_copy(
                            kdup[:, m, g * 2 * HD:(g + 1) * 2 * HD].rearrange("p (a d) -> p a d", a=2),
                            spread(qkr[:, m, QW + g * HD:QW + (g + 1) * HD], 1, 2))
                last.then_inc(rotated, 1)

                for m in range(MT):
                    banks.evacuated(dve, ("v", m))
                for m in range(MT):
                    last = v.bn_stats(stats[:, m, 0, :], p_tok[:, m, v0:v0 + SGU])
                step(last)
                for m in range(MT):
                    last = v.bn_aggr(mv[:, m, :], stats[:, m, 0, :])
                step(last)
                ts(small[:, 0:MT], mv[:, :, 1], 1e-5, None, ALU.add).then_inc(var_ready, 1)
                dve.wait_ge(std_ready, 2)
                step(v.reciprocal(small[:, 64:64 + MT], small[:, 32:32 + MT]))
                for m in range(MT):
                    last = ts(v_ln[:, m, :], p_tok[:, m, v0:v0 + SGU], mv[:, m, 0:1], small[:, 64 + m:65 + m],
                              ALU.subtract, ALU.mult)
                step(last)
                for m in range(MT):
                    last = tt(v_ln[:, m, :], v_ln[:, m, :], sgu_ln[:, 0, :], ALU.mult)
                step(last)
                for m in range(MT):
                    last = tt(v_ln[:, m, :], v_ln[:, m, :], sgu_ln[:, 1, :], ALU.add)
                last.then_inc(vln_ready, 1)
                for c in (4, 5):
                    sum_chunk(c)
                for g in range(2):
                    ps = banks.read(dve, ("wsT", g))
                    banks.free(v.tensor_copy(wsT[:, 4 * g:4 * g + 4, :],
                                             ps[:, :].rearrange("p (g i) -> p g i", g=4)), ("wsT", g))
                for m in range(MT):
                    ps = banks.read(dve, ("sv", m))
                    mixed = tmp[:, 2048:2560]
                    if m:
                        dve.wait_ge(gated_ready, m)
                    banks.free(tt(mixed.rearrange("p (g d) -> p g d", g=SG),
                                  ps[:, :].rearrange("p (g d) -> p g d", g=SG),
                                  spread(cols[:, MODS:MODS + SG], 2, SGD), ALU.add), ("sv", m))
                    banks.evacuated(dve, ("sv", m))
                    tt(p_tok[:, m, u0:u0 + SGU], p_tok[:, m, u0:u0 + SGU], mixed, ALU.mult
                       ).then_inc(gated_ready, 1)

                for h in range(QH + 1):
                    if h in (2, 4):
                        sum_chunk(5 + h // 2)
                    if h < QH:
                        o = 2 * (h % 2)
                        ps = banks.read(dve, ("score", h))
                        step(red(small[:, 100 + o:102 + o], ps[:, :].rearrange("p (m s) -> p m s", m=MT),
                                 AX, ALU.max))
                        ts(small[:, 104 + o:106 + o], small[:, 100 + o:102 + o], -HD ** -0.5, None, ALU.mult
                           ).then_inc(max_ready, 1)
                    if h:
                        g = h - 1
                        o = 2 * (g % 2)
                        banks.evacuated(dve, ("score", g))
                        step(v.reciprocal(small[:, 112 + o:114 + o], small[:, 108 + o:110 + o]))
                        for m in range(MT):
                            last = ts(prob[:, g % 2, m, :], prob[:, g % 2, m, :],
                                      small[:, 112 + o + m:113 + o + m], None, ALU.mult)
                        last.then_inc(prob_ready, 1)

                take_mod(1)

                for g in range(8):
                    banks.evacuated(dve, ("gates", g))
                for t in range(DT):
                    ps = banks.read(dve, ("branch", t))
                    o = 512 * (t % 2)
                    tt(tmp[:, o:o + S], ps[:, 0:S], gates[:, t, :], ALU.mult)
                    banks.free(tt(tmp[:, o + S:o + 2 * S], ps[:, S:2 * S], gates[:, DT + t, :], ALU.mult),
                               ("branch", t))
                    banks.evacuated(dve, ("branch", t))
                    tt(yT[:, t, :], tmp[:, o:o + S], tmp[:, o + S:o + 2 * S], ALU.add).then_inc(merged, 1)

                take_gate("gate1")
                dve.wait_ge(merged, DT)
                for n in range(2):
                    for m in range(MT):
                        residual(banks.read(dve, ("out", n, m)), m, n, ("out", n, m))
                norm_x(3, ln1_landed, 1)
                split_up(0, -1)
                for b in range(2, 4):
                    modulate("x2T", b, 3 * DT, 4 * DT)
                banks.read(dve, "router")
                for b in range(4):
                    banks.evacuated(dve, ("x2T", b))
                    two = slice(2 * b, 2 * b + 2)
                    tt(parts_of(hT[:, two, :]), hT[:, two, :], parts_of.value(hT_high[:, two, :]),
                       ALU.subtract).then_inc(hT_split, 1)
                take_gate("gate2")
                split_down(0, -1)
                split_up(0, 0)

                def r(n):
                    return router[:, n, :]

                def groups(ap):
                    return ap.rearrange("p (g e) -> p g e", e=PG)

                def tokens(ap):
                    return ap.rearrange("p (m e) -> p m e", m=MT)

                banks.evacuated(dve, "router")
                step(tt(tokens(r(1)), tokens(r(0)), spread(rbias[:, :], 1, MT), ALU.add))
                for g in range(MT * NG):
                    last = v.max(out=r(5)[:, g * 8:(g + 1) * 8], in_=r(1)[:, g * PG:(g + 1) * PG])
                step(last)
                gs, rank = small[:, 120:136], small[:, 136:152]
                keep, pen, top = small[:, 152:168], small[:, 168:184], small[:, 184:200]
                best = r(5).rearrange("p (g e) -> p g e", e=8)
                step(tt(gs, best[:, :, 0], best[:, :, 1], ALU.add))
                gsm = gs.rearrange("p (m g) -> p m g", m=MT)
                pairs = [r(n).rearrange("p (m i j) -> p m i j", m=MT, i=NG) for n in (6, 7)]
                theirs, own = spread(gsm, 2, NG), spread(gsm, 3, NG)
                tt(pairs[0], theirs, own, ALU.is_gt)
                step(tt(pairs[1], theirs, own, ALU.is_equal))
                step(tt(pairs[1], pairs[1], spread(jlt[:, :].rearrange("p (i j) -> p i j", i=NG), 1, MT),
                        ALU.mult))
                step(tt(r(6), r(6), r(7), ALU.add))
                step(red(rank, r(6).rearrange("p (g j) -> p g j", j=NG), AX, ALU.add))
                step(ts(keep, rank, KEEP_G - 0.5, None, ALU.is_lt))
                step(ts(pen, keep, -1.0, -NEG, ALU.add, ALU.mult))
                step(tt(groups(r(2)), groups(r(1)), spread(keep, 2, PG), ALU.mult))
                step(tt(groups(r(2)), groups(r(2)), spread(pen, 2, PG), ALU.add))
                assert TOPK == 8
                for m in range(MT):
                    step(v.max(out=top[:, m * 8:(m + 1) * 8], in_=r(2)[:, m * E:(m + 1) * E]))
                    step(v.match_replace(out=r(3)[:, m * E:(m + 1) * E], in_to_replace=top[:, m * 8:(m + 1) * 8],
                                         in_values=r(2)[:, m * E:(m + 1) * E], imm_value=TAKEN))
                step(tt(r(4), r(3), r(2), ALU.not_equal))
                step(tt(r(4), r(4), r(0), ALU.mult))
                step(red(small[:, 200:202], tokens(r(4)), AX, ALU.add))
                step(v.reciprocal(small[:, 202:204], small[:, 200:202]))
                v.scalar_tensor_tensor(tokens(r(8)), tokens(r(4)), ROUTED_SCALE, spread(small[:, 202:204], 2, E),
                                       ALU.mult, ALU.mult).then_inc(weights_ready, 1)

                ps = banks.read(dve, ("u", "shared"))
                banks.evacuated(dve, ("g", "shared"))
                tt(parts_of(hid_high[:, 0, :]), silu_g[:, 0, :], ps[:, :], ALU.mult)
                banks.free(tt(hid[:, 0, :], silu_g[:, 0, :], ps[:, :], ALU.mult), ("u", "shared"))
                banks.evacuated(dve, ("u", "shared"))
                tt(parts_of(hid[:, 0, :]), hid[:, 0, :], parts_of.value(hid_high[:, 0, :]), ALU.subtract
                   ).then_inc(hidden_ready, 1)

                def turn_of(i):
                    for j in range(OCT):
                        split_down(i, j)
                        if not end_of(i, j):
                            split_up(i, j + 1)
                        if j % 4 == 0:
                            dve.wait_ge(four_landed[j // 4], i * 16 + 16)
                        b = 4 + 2 * (j % 2)
                        s = (j + 1) % 2
                        dve.wait_ge(freed[b], i * (OCT // 2) + (first_turn[b] + j // 2 + 1))
                        dve.wait_ge(filled[b + 1], i * (OCT // 2) + (first_turn[b + 1] + j // 2 + 1))
                        sv = silu_g[:, s, :].rearrange("p (t s) -> p t s", t=2)
                        tt(silu_g[:, s, :], silu_g[:, s, :], banks.t[b + 1][:, :], ALU.mult
                           ).then_inc(freed[b + 1], 1)
                        if not start_of(i, j):
                            dve.wait_ge(down_done, i * OCT + j)
                        dve.wait_ge(freed[b + 1], i * (OCT // 2) + (first_turn[b + 1] + j // 2 + 1))
                        weight = spread(w_four[:, j // 4, j % 4, :], 1, 2)
                        hh, hl = [t_[:, s, :].rearrange("p (t s) -> p t s", t=2) for t_ in (hid_high, hid)]
                        tt(parts_of(hh), sv, weight, ALU.mult)
                        step_of_experts(tt(hl, sv, weight, ALU.mult), i, j)
                        tt(parts_of(hl), hl, parts_of.value(hh), ALU.subtract).then_inc(hidden_ready, 1)

                def step_of_experts(ins, i, j):
                    ins.then_inc(weighted, 1)
                    dve.wait_ge(weighted, i * OCT + (j + 1))

                octets(dve, turn_of)
                dve.wait_ge(down_done, E + 1)
                for m in range(MT):
                    for n in range(2):
                        residual(banks.t[2 * m + n], m, n, None)
                norm_x(4, ln2_landed, 2)
                leave(dve, l)


def second_block(nc, a, x_tok, consts):
    with ExitStack() as ctx:
        def sb(name, shape):
            return ctx.enter_context(nc.sbuf_tensor("s_" + name, shape, F32))

        parts_of = Splits(nc, ctx, "s_")

        def sem(name):
            return ctx.enter_context(nc.semaphore("s_" + name))

        ident = consts["ident"]
        slots_A = 3
        n_rows = 3 * DT + CT + 4 * RT + 3 * RT
        r_ffn1, r_mix, r_ffn2, r_mu = 0, DT, 2 * DT, 3 * DT
        r_w0 = r_mu + CT
        r_a0 = r_w0 + 2 * RT
        r_kk = r_a0 + 2 * RT
        r_ka, r_rk = r_kk + RT, r_kk + 2 * RT
        assert n_rows == r_rk + RT

        ringA = parts_of.buffer("ringA", [P, slots_A, A_W])
        hT = parts_of.buffer("hT", [P, DT, S])
        ARENA = 29072
        arena_at = nc.sbuf_base
        arena = sb("arena", [P, ARENA])
        rows = sb("rows", [n_rows, P])
        cols = sb("cols", [P, n_rows])
        mus = sb("mus", [P, 2, CT])
        w2 = sb("w2", [P, RW])
        a2 = sb("a2", [P, RW])
        g2 = sb("g2", [P, RW])
        lnx = sb("lnx", [P, 2, RW])
        qkg = sb("qkg", [P, 2, HD])
        subg = sb("subg", [P, 2 * HD])
        lamv = sb("lamv", [P, 4, HD])
        lamc = sb("lamc", [P, 2])
        masks = sb("masks", [P, 12, P])
        dist = sb("dist", [P, MT, S])
        heads1 = sb("heads1", [P, P])
        headsel = sb("headsel", [P, RT, 8])
        small = sb("small", [P, 256])
        edge = sb("edge", [P, 2, 2, S + 2])
        ones = sb("ones", [P, CH])
        lam = small[:, 200:206]
        dcol = small[:, 208:224]
        bonus = small[:, 224:256].rearrange("p (d m h) -> p d m h", d=2, m=MT)

        def view(lo, n, dims=None, **kw):
            assert lo + n <= ARENA, (lo, n)
            ap = arena[:, lo:lo + n]
            return ap.rearrange(dims, **kw) if dims else ap

        ringB = parts_of.part("ringB", arena, arena_at, 0, B_SLOTS * B_W).rearrange("p (b c) -> p b c", b=B_SLOTS)
        silu_g = view(8192, 1024, "p (b c) -> p b c", b=2)
        hid = parts_of.part("hid", arena, arena_at, 9216, 1024).rearrange("p (b c) -> p b c", b=2)
        xn = view(10240, 2048, "p (m d) -> p m d", m=MT)
        highA = parts_of.part("highA", arena, arena_at, 12288, 2 * A_W).rearrange("p (b c) -> p b c", b=2)
        highB = parts_of.part("highB", arena, arena_at, 20480, 2 * B_W).rearrange("p (b c) -> p b c", b=2)
        hid_high = parts_of.part("hid_high", arena, arena_at, 24576, 1024).rearrange("p (b c) -> p b c", b=2)
        hT_high = parts_of.part("hT_high", arena, arena_at, 25600, 2048).rearrange("p (t s) -> p t s", s=S)
        rkv = view(0, 3072, "p (t s) -> p t s", s=S)
        low = view(3072, 768, "p (t s) -> p t s", s=S)
        oaT = view(3840, 1024, "p (t s) -> p t s", s=S)
        obT = view(4864, 1024, "p (t s) -> p t s", s=S)
        base = 5888
        nbr = view(base, 1024, "p (b t s) -> p b t s", b=2, t=2)
        at_tok = view(base + 1024, 3072, "p (m c) -> p m c", m=MT)
        sq = view(base + 4096, 2048)
        qT = view(base + 6144, 1024, "p (t s) -> p t s", s=S)
        kT = view(base + 7168, 1024, "p (t s) -> p t s", s=S)
        prob = view(base + 8192, 2048, "p (b a m s) -> p b a m s", b=2, a=2, m=MT)
        comb = view(base + 10240, 1024, "p (b m s) -> p b m s", b=2, m=MT)
        combT = view(base + 11264, 1024, "p (b t s) -> p b t s", b=2, t=MT)
        ob = view(base + 12288, 1024, "p (m c) -> p m c", m=MT)
        kk = view(base, 1024, "p (t s) -> p t s", s=S)
        AR = view(base + 1024, 2048, "p (t r s) -> p t r s", r=2, s=S)
        Bt = view(base + 3072, 1024, "p (t s) -> p t s", s=S)
        Kt = view(base + 4096, 1024, "p (t s) -> p t s", s=S)
        state = view(base + 13312, 2048, "p (c q v) -> p c q v", c=NCH, q=RT)
        SA = view(base + 4096, 1024, "p (m c) -> p m c", m=MT)
        Btok = view(base + 5120, 1024, "p (m c) -> p m c", m=MT)
        Ktok = view(base + 6144, 1024, "p (m c) -> p m c", m=MT)
        Vtok = view(base + 7168, 1024, "p (m c) -> p m c", m=MT)
        MRB = view(base + 8192, 2048, "p (q u t) -> p q u t", q=RT, u=4)
        MRK = view(base + 10240, 2048, "p (q u t) -> p q u t", q=RT, u=4)
        sw = view(base + 8192, 1024)
        ic = view(base + 9216, 1024)
        cs = view(base + 10240, 1024)
        ce = view(base + 11264, 1024)
        SA0 = view(base + 12288, 1024, "p (m c) -> p m c", m=MT)
        XAT = view(base + 15360, 1024, "p (q s) -> p q s", q=RT)
        Y = view(base + 16384, 1024, "p (m c) -> p m c", m=MT)
        gbase = base + 17408
        U, L2T, X, XT, W1, Z = [view(gbase + n * 1024, 1024, "p (b u t) -> p b u t", b=2, u=4)
                                for n in range(5)] + [view(base + 13312, 1024, "p (b u t) -> p b u t", b=2, u=4)]
        Q1 = view(gbase + 5120, 256)
        Atok = view(gbase + 5376, 256, "p (m c) -> p m c", m=MT)
        ytmp = view(gbase, 1024)
        ytmp2 = view(gbase + 1024, 1024)
        gates = view(base + 1024, 4096, "p (t s) -> p t s", s=S)
        btmp = view(base + 5120, 1024)
        yT = view(base + 6144, 2048, "p (t s) -> p t s", s=S)

        s_go = sem("layer_cleared")
        params_landed, tables_landed = sem("params_landed"), sem("tables_landed")
        names = ["a_slot0", "a_slot1", "a_slot2", "b_slot0", "b_slot1", "b_slot2", "b_slot3",
                 "squares_ready", "var_ready", "std_ready", "xn_ready", "x_ready", "down_done",
                 "mixed_ready", "neighbours_read", "at_ready", "lam_asked", "lam_exp", "max_ready", "exp_done",
                 "comb_ready", "ob_ready", "kk_squared", "low_ready", "cum_ready", "exps_ready", "ABKR_ready",
                 "bonus_ready", "z_ready", "inv_ready", "sa_ready", "state_ready",
                 "highA_ready", "lowA_ready", "highB_ready", "lowB_ready", "hT_split", "hid_split",
                 "oa_ready", "merged", "dve_steps", "rows_landed", "arrived"]
        names += [f"bank_filled{i}" for i in range(8)] + [f"bank_freed{i}" for i in range(8)]
        each = {n: sem(n) for n in names}
        nums = [s.num for s in each.values()]
        cleared = range(min(nums), max(nums) + 1)
        assert len(cleared) == len(nums) and not {s_go.num, params_landed.num, tables_landed.num} & set(cleared)
        a_landed = [each[f"a_slot{i}"] for i in range(slots_A)]
        b_landed = [each[f"b_slot{i}"] for i in range(B_SLOTS)]
        squares_ready, var_ready, std_ready = each["squares_ready"], each["var_ready"], each["std_ready"]
        xn_ready, x_ready, down_done = each["xn_ready"], each["x_ready"], each["down_done"]
        mixed_ready, neighbours_read, at_ready = each["mixed_ready"], each["neighbours_read"], each["at_ready"]
        lam_asked, lam_exp, max_ready = each["lam_asked"], each["lam_exp"], each["max_ready"]
        exp_done, comb_ready, ob_ready = each["exp_done"], each["comb_ready"], each["ob_ready"]
        kk_squared, low_ready, cum_ready = each["kk_squared"], each["low_ready"], each["cum_ready"]
        exps_ready, ABKR_ready, bonus_ready = each["exps_ready"], each["ABKR_ready"], each["bonus_ready"]
        z_ready, inv_ready = each["z_ready"], each["inv_ready"]
        sa_ready, state_ready, oa_ready = each["sa_ready"], each["state_ready"], each["oa_ready"]
        highA_ready, lowA_ready, highB_ready = each["highA_ready"], each["lowA_ready"], each["highB_ready"]
        lowB_ready, hT_split, hid_split = each["lowB_ready"], each["hT_split"], each["hid_split"]
        merged, dve_steps, arrived = each["merged"], each["dve_steps"], each["arrived"]
        rows_landed = each["rows_landed"]
        filled = [each[f"bank_filled{i}"] for i in range(8)]
        freed = [each[f"bank_freed{i}"] for i in range(8)]

        banks = Banks([ctx.enter_context(nc.psum_tensor(f"s_bank{i}", [P, BANK], F32)) for i in range(8)],
                      filled, freed)
        LEVELS = 5
        scan_order = [list(range(NCH)), list(range(NCH))[::-1]]

        def take_ffn(f):
            for b in range(4):
                banks.take(("xT", f, b), b)
            if f == 0:
                banks.take("cols", 7)
            for n in range(4):
                banks.take(("y", f, n), n)
            for s in range(STEPS):
                banks.take(("g", f, s), 4 + 2 * (s % 2))
                banks.take(("u", f, s), 5 + 2 * (s % 2))

        take_ffn(0)
        for b in range(4):
            banks.take(("xT", 1, b), b)
        for c in range(3):
            for m in range(MT):
                banks.take(("at", c, m), (2 * c + m) % 4)
        for g in range(8):
            banks.take(("rw", g), (2 + g) % 4)
        for g in range(4):
            banks.take(("qkT", g), 4 + g)
        for m in range(MT):
            banks.take(("o", m), m)
        for s in range(2 * BH + 2):
            if s < 2 * BH:
                banks.take(("score", s), 4 + s % 2)
            if s % 2 and s > 1:
                banks.take(("combT", s // 2 - 1), 6 + (s // 2 - 1) % 2)
        for g in range(2):
            banks.take(("obT", g), 2 + g)
        for g in range(2):
            banks.take(("kkss", g), g)
        for m in range(MT):
            banks.take(("Vtok", m), 2 + m)
        for d in range(2):
            for g in range(2):
                banks.take(("dec", d, g), 4 + g)
            for g in range(2):
                banks.take(("rate", d, g), 6 + g)
            banks.take(("bonus", d), 2)
            for m in range(MT):
                banks.take(("Btok", d, m), 3 + m)
            for m in range(MT):
                banks.take(("Ktok", d, m), 5 + m)
            for duo in range(2):
                for q in range(2):
                    for hh in range(2):
                        for n, name in enumerate(("UR", "KR", "L")):
                            banks.take((name, d, duo, q, hh), 3 * hh + n)
                for lv in range(LEVELS):
                    for q in range(2):
                        banks.take(("W", d, duo, q, lv), 3 * q)
                    for q in range(2):
                        banks.take(("dXT", d, duo, q, lv), 3 * q + 1)
                        if lv < LEVELS - 1:
                            banks.take(("dX", d, duo, q, lv), 3 * q + 2)
                for q in range(2):
                    banks.take(("Q1", d, duo, q), 6)
                    banks.take(("Atok", d, duo, q), 7)
                    banks.take(("SA0", d, duo, q), 2)
                    banks.take(("XAT", d, duo, q), 5)
            for n in range(NCH):
                if n:
                    banks.take(("SA", d, n), 0)
                if n < NCH - 1:
                    banks.take(("state", d, n), 1)
            for m in range(MT):
                banks.take(("Y", d, m), 2 + m)
        for m in range(MT):
            banks.take(("gate", m), 6 + m)
        for g in range(8):
            banks.take(("gates", g), g % 4)
        for g in range(2):
            banks.take(("oaT", g), 4 + g)
        for t in range(DT):
            banks.take(("branch", t), t % 4)
        for n in range(2):
            for m in range(MT):
                banks.take(("out", n, m), 4 + 2 * n + m)
        take_ffn(2)

        a_at = STEPS
        a_in = a_at + 3
        a_gate = a_in + 4
        a_wa = a_gate + 4
        a_wb, a_out, a_ffn2 = a_wa + 1, a_wa + 2, a_wa + 4
        last_use = {s: ("u", 0, s) for s in range(STEPS)}
        last_use |= {a_in + c: ("rw", 2 * c + 1) for c in range(4)}
        last_use |= {a_at + c: ("at", c, 1) for c in range(3)}
        last_use |= {a_gate + c: ("gates", 2 * c + 1) for c in range(4)}
        last_use |= {a_wa: ("branch", DT - 1), a_wb: ("branch", DT - 1)}
        last_use |= {a_out + n: ("out", n, 1) for n in range(2)}
        last_use |= {a_ffn2 + s: ("u", 2, s) for s in range(STEPS)}
        ffn_first = {0: 0, 2: a_ffn2}

        def slotA(n):
            return ringA[:, n % slots_A, :]

        def rows8(ap):
            return ap.rearrange("p (k c) -> p k c", k=DT)

        def slotB(n):
            return ringB[:, n % B_SLOTS, :].rearrange("p (k c) -> p k c", k=2)

        def pair_of(ps):
            return ps[:, :].rearrange("p (t s) -> p t s", t=2)

        block = ctx.enter_context(nc.Block())

        def leave(eng, l):
            eng.nop().then_inc(arrived, 1)
            eng.wait_ge(s_go, l + 1)

        @block.sync
        def _(sp):
            with sp.Fori(0, DEPTH) as l:
                def slot_free(n):
                    if n >= slots_A:
                        banks.read(sp, last_use[n - slots_A])

                def load(n, dst, src):
                    slot_free(n)
                    half = dst.shape[1] // 2
                    for h in range(2):
                        sp.dma_start(dst[:, h * half:(h + 1) * half], src[:, h * half:(h + 1) * half]
                                     ).then_inc(a_landed[n % slots_A], 16)

                def load_up(f, s):
                    w = a[("ffn1_in_2", None, "ffn2_in_2")[f]]
                    n = ffn_first[f] + s
                    slot_free(n)
                    gu = slotA(n).rearrange("p (h k c) -> p h k c", h=2, k=DT)
                    for h in range(2):
                        c = h * DFF + s * FF
                        sp.dma_start(gu[:, h], w[l, :, c:c + FF].rearrange("(k p) c -> p k c", p=P)
                                     ).then_inc(a_landed[n % slots_A], 16)

                def load_down(f, s):
                    w = a[("ffn1_out_2", None, "ffn2_out_2")[f]]
                    if s >= B_SLOTS:
                        sp.wait_ge(down_done, (f // 2) * (STEPS - 1) + s - B_SLOTS + 1)
                    sp.dma_start(slotB(s), w[l, s * FF:(s + 1) * FF, :].rearrange("(k p) c -> p k c", p=P)
                                 ).then_inc(b_landed[s % B_SLOTS], 16)

                def row(dst, src):
                    sp.dma_start(dst, src).then_inc(rows_landed, 16)

                for at, name in ((r_ffn1, "norm_ffn1_2"), (r_mix, "norm_mix_2"), (r_ffn2, "norm_ffn2_2"),
                                 (r_mu, "rwkv_mu_2"), (r_kk, "k_k_2"), (r_ka, "k_a_2")):
                    src = a[name][l].rearrange("(r p) -> r p", p=P)
                    row(rows[at:at + src.shape[0], :], src)
                for at, name in ((r_w0, "decay_w0_2"), (r_a0, "iclr_a0_2")):
                    row(rows[at:at + 2 * RT, :], a[name][l].rearrange("d (r p) -> (d r) p", p=P))
                row(rows[r_rk:r_rk + RT, :], a["r_k_2"][l].rearrange("(r h) n -> r (h n)", h=2))
                for s in range(STEPS):
                    load_up(0, s)
                    load_down(0, s)
                edges = [CRW + 512 * i for i in range(4)]
                chunks = list(zip(edges, edges[1:]))
                edges = [0, 512, 1024, 1536, CRW]
                chunks += list(zip(edges, edges[1:]))
                chunks += [(CRW + CAT + 512 * i, CRW + CAT + 512 * (i + 1)) for i in range(4)]
                for c, (lo, hi) in enumerate(chunks):
                    load(a_at + c, rows8(slotA(a_at + c))[:, :, 0:hi - lo],
                         a["w_in_2"][l, :, lo:hi].rearrange("(k p) c -> p k c", p=P))
                for b in range(2):
                    load(a_wa + b, slotA(a_wa + b).rearrange("p (k c) -> p k c", k=4),
                         a["w_branch_2"][l, b].rearrange("(k p) c -> p k c", p=P))
                for c in range(2):
                    load(a_out + c, rows8(slotA(a_out + c)),
                         a["w_out_2"][l, :, c * 512:(c + 1) * 512].rearrange("(k p) c -> p k c", p=P))
                load_up(2, 0)
                sp.wait_ge(x_ready, 2)
                for s in range(STEPS):
                    if s:
                        load_up(2, s)
                    load_down(2, s)
                sp.wait_ge(arrived, 4)
                sp.sem_clear(cleared)
                sp.nop().then_inc(s_go, 1)

        n_params = 16 * 10

        @block.gpsimd
        def _(pool):
            for dst, name in ((masks[:, :, :], "masks"), (dist[:, :, :], "dist"), (heads1[:, :], "heads"),
                              (headsel[:, :, :], "headsel")):
                pool.dma_start(dst, a["const_" + name]).then_inc(tables_landed, 16)
            with pool.Fori(0, DEPTH) as l:
                def param(dst, src):
                    pool.dma_start(dst, src).then_inc(params_landed, 16)

                def on_all(src):
                    return src.unsqueeze(0).broadcast_to([P] + list(src.shape))

                param(w2[:, :], a["decay_w2_2"][l].rearrange("d r c -> (d r) c"))
                param(a2[:, :], a["iclr_a2_2"][l].rearrange("d r c -> (d r) c"))
                param(g2[:, :], a["gate_g2_2"][l])
                param(lnx[:, 0, :], on_all(a["ln_x_g_2"][l]))
                param(lnx[:, 1, :], on_all(a["ln_x_b_2"][l]))
                param(qkg[:, 0, :], on_all(a["q_gain_2"][l]))
                param(qkg[:, 1, :], on_all(a["k_gain_2"][l]))
                param(subg[:, :], on_all(a["subln_g_2"][l]))
                param(lamv[:, :, :], on_all(a["diff_lambda_2"][l]))
                param(lamc[:, :], a["const_lam"][l])
                leave(pool, l)
        @block.tensor
        def _(pe):
            mm = nc.tensor.matmul
            turn = nc.tensor.transpose

            def landed(n):
                pe.wait_ge(a_landed[n % slots_A], 32 * (n // slots_A + 1))

            def to_features(key, src, n_banks):
                for b in range(n_banks):
                    ps = banks.claim(pe, (*key, b))
                    for t in range(2):
                        for m in range(MT):
                            o = t * S + m * P
                            last = turn(ps[:, o:o + P], src[:, m, (2 * b + t) * P:(2 * b + t + 1) * P],
                                        ident[:, :])
                    banks.fill(last, (*key, b))

            def hidden(ps, w, n=2):
                for t in range(n):
                    for k in range(DT):
                        last = mm(ps[:, t * S:(t + 1) * S], w[:, k, t * P:(t + 1) * P], hT[:, k, :],
                                  start=(k == 0), stop=(k == DT - 1))
                return last

            def split_hidden(ps, w, high, turns=None):
                for t in range(2):
                    cs_ = slice(t * P, (t + 1) * P)
                    for k in range(DT):
                        if turns is not None and t == 0 and k % 2 == 0:
                            pe.wait_ge(hT_split, turns + k // 2 + 1)
                        for x, (wx, hx) in enumerate(((high, hT_high), (high, hT), (w, hT_high))):
                            last = mm(ps[:, t * S:(t + 1) * S], parts_of(wx[:, k, cs_]),
                                      parts_of(hx[:, k, :]), start=(k == 0 and x == 0),
                                      stop=(k == DT - 1 and x == 2))
                return last

            def ffn(f, l):
                pe.wait_ge(xn_ready, f + 1)
                if f == 0:
                    pe.wait_ge(rows_landed, 16 * 9)
                to_features(("xT", f), xn, 4)
                if f == 0:
                    ps = banks.claim(pe, "cols")
                    banks.fill(turn(ps[:, 0:n_rows], rows[:, :], ident[0:n_rows, 0:n_rows]), "cols")
                for n in range(4):
                    banks.claim(pe, ("y", f, n))
                for s in range(STEPS + 1):
                    if s < STEPS:
                        n = ffn_first[f] + s
                        pe.wait_ge(lowA_ready, (f // 2) * STEPS + s + 1)
                        gu, gu_high = [w.rearrange("p (h k c) -> p h k c", h=2, k=DT)
                                       for w in (slotA(n), highA[:, s % 2, :])]
                        for half, name in enumerate("gu"):
                            ps = banks.claim(pe, (name, f, s))
                            banks.fill(split_hidden(ps, gu[:, half], gu_high[:, half],
                                                    f // 2 * 4 if s == half == 0 else None), (name, f, s))
                    if s:
                        r = s - 1
                        pe.wait_ge(lowB_ready, (f // 2) * STEPS + r + 1)
                        pe.wait_ge(hid_split, (f // 2) * STEPS + r + 1)
                        wd = slotB(r)
                        wd_high = highB[:, r % 2, :].rearrange("p (k c) -> p k c", k=2)
                        for m in range(MT):
                            for n in range(2):
                                for k in range(2):
                                    o = k * S + m * P
                                    for x, (hx, wx) in enumerate(((hid_high, wd_high), (hid, wd_high),
                                                                  (hid_high, wd))):
                                        last = mm(banks.t[2 * m + n][:, :],
                                                  parts_of(hx[:, r % 2, o:o + P]),
                                                  parts_of(wx[:, k, n * 512:(n + 1) * 512]),
                                                  start=(r == 0 and k == 0 and x == 0),
                                                  stop=(r == STEPS - 1 and k == 1 and x == 2),
                                                  skip_group_check=True)
                                if r == STEPS - 1:
                                    banks.fill(last, ("y", f, 2 * m + n))
                        if r < STEPS - 1:
                            last.then_inc(down_done, 1)

            with pe.Fori(0, DEPTH) as l:
                ffn(0, l)
                pe.wait_ge(params_landed, l * n_params + n_params)
                pe.wait_ge(tables_landed, 4 * 16)

                pe.wait_ge(xn_ready, 2)
                to_features(("xT", 1), xn, 4)
                for b in range(4):
                    banks.evacuated(pe, ("xT", 1, b))
                for c in range(3):
                    landed(a_at + c)
                    w = rows8(slotA(a_at + c))
                    for m in range(MT):
                        ps = banks.claim(pe, ("at", c, m))
                        for k in range(DT):
                            last = mm(ps[:, :], hT[:, k, m * P:(m + 1) * P], w[:, k, :],
                                      start=(k == 0), stop=(k == DT - 1))
                        banks.fill(last, ("at", c, m))
                for g in range(8):
                    c = a_in + g // 2
                    if g % 2 == 0:
                        landed(c)
                    w = rows8(slotA(c))
                    ps = banks.claim(pe, ("rw", g))
                    o = (g % 2) * 2 * P
                    banks.fill(hidden(ps, w[:, :, o:o + 2 * P], 1 if g == 7 else 2), ("rw", g))

                pe.wait_ge(at_ready, 1)
                for g in range(4):
                    ps = banks.claim(pe, ("qkT", g))
                    for t in range(2):
                        for m in range(MT):
                            c = (2 * g + t) * P
                            last = turn(ps[:, t * S + m * P:t * S + (m + 1) * P], at_tok[:, m, c:c + P],
                                        ident[:, :])
                    banks.fill(last, ("qkT", g))
                for g in range(4):
                    banks.evacuated(pe, ("qkT", g))
                for m in range(MT):
                    banks.claim(pe, ("o", m))
                for s in range(2 * BH + 2):
                    if s < 2 * BH:
                        h, o = s // 2, (s % 2) * HD
                        ps = banks.claim(pe, ("score", s))
                        for m in range(MT):
                            last = mm(ps[:, m * S:(m + 1) * S], qT[o:o + HD, h, m * P:(m + 1) * P],
                                      kT[o:o + HD, h, :], start=True, stop=True)
                        banks.fill(last, ("score", s))
                    if s % 2 and s > 1:
                        h = s // 2 - 1
                        pe.wait_ge(comb_ready, h + 1)
                        ps = banks.claim(pe, ("combT", h))
                        for t in range(MT):
                            for m in range(MT):
                                last = turn(ps[:, t * S + m * P:t * S + (m + 1) * P],
                                            comb[:, h % 2, m, t * P:(t + 1) * P], ident[:, :])
                        banks.fill(last, ("combT", h))
                        banks.evacuated(pe, ("combT", h))
                        for m in range(MT):
                            for t in range(MT):
                                last = mm(banks.t[m][:, h * P:(h + 1) * P], combT[:, h % 2, t, m * P:(m + 1) * P],
                                          at_tok[:, t, 2 * RW + h * P:2 * RW + (h + 1) * P],
                                          start=(t == 0), stop=(t == MT - 1))
                            if h == BH - 1:
                                banks.fill(last, ("o", m))
                pe.wait_ge(ob_ready, 1)
                to_features(("obT",), ob, 2)

                pe.wait_ge(kk_squared, 1)
                for g in range(2):
                    ps = banks.claim(pe, ("kkss", g))
                    for t in range(2):
                        last = mm(ps[:, t * S:(t + 1) * S], heads1[:, :], sq[:, (2 * g + t) * S:(2 * g + t + 1) * S],
                                  start=True, stop=True)
                    banks.fill(last, ("kkss", g))
                for m in range(MT):
                    ps = banks.claim(pe, ("Vtok", m))
                    for t in range(RT):
                        last = turn(ps[:, t * P:(t + 1) * P], rkv[:, 2 * RT + t, m * P:(m + 1) * P], ident[:, :])
                    banks.fill(last, ("Vtok", m))
                pe.wait_ge(low_ready, 1)
                for d in range(2):
                    o = d * LORA
                    for name, w, src in (("dec", w2, low[:, 0, :]), ("rate", a2, low[:, 1, :])):
                        for g in range(2):
                            ps = banks.claim(pe, (name, d, g))
                            for t in range(2):
                                c = (2 * g + t) * P
                                last = mm(ps[:, t * S:(t + 1) * S], w[o:o + LORA, c:c + P], src[o:o + LORA, :],
                                          start=True, stop=True)
                            banks.fill(last, (name, d, g))
                    pe.wait_ge(bonus_ready, d + 1)
                    ps = banks.claim(pe, ("bonus", d))
                    for m in range(MT):
                        for t in range(RT):
                            last = mm(ps[:, m * 8:(m + 1) * 8], sw[:, t * S + m * P:t * S + (m + 1) * P],
                                      headsel[:, t, :], start=(t == 0), stop=(t == RT - 1))
                    banks.fill(last, ("bonus", d))
                    pe.wait_ge(ABKR_ready, d + 1)
                    for name, src in (("Btok", Bt), ("Ktok", Kt)):
                        for m in range(MT):
                            ps = banks.claim(pe, (name, d, m))
                            for t in range(RT):
                                last = turn(ps[:, t * P:(t + 1) * P], src[:, t, m * P:(m + 1) * P], ident[:, :])
                            banks.fill(last, (name, d, m))
                    for duo in range(2):
                        for q in range(2):
                            p = 2 * duo + q
                            for hh in range(2):
                                o = hh * HD
                                for name in ("UR", "KR", "L"):
                                    ps = banks.claim(pe, (name, d, duo, q, hh))
                                    for m in range(MT):
                                        s = slice(m * P, (m + 1) * P)
                                        if name == "L":
                                            last = mm(ps[:, m * P:(m + 1) * P], AR[o:o + HD, p, 0, s],
                                                      Bt[o:o + HD, p, s], start=True, stop=True)
                                        else:
                                            left = Bt if name == "UR" else Kt
                                            last = mm(ps[:, m * S:(m + 1) * S], left[o:o + HD, p, s],
                                                      AR[o:o + HD, p, :, s], start=True, stop=True)
                                    banks.fill(last, (name, d, duo, q, hh))
                        for lv in range(LEVELS):
                            n = (d * 2 + duo) * LEVELS + lv
                            for q in range(2):
                                pe.wait_ge(z_ready, 2 * n + q + 1)
                                if lv:
                                    banks.evacuated(pe, ("dX", d, duo, q, lv - 1))
                                ps = banks.claim(pe, ("W", d, duo, q, lv))
                                for u in range(4):
                                    last = mm(ps[:, u * P:(u + 1) * P], Z[:, q, u, :], X[:, q, u, :],
                                              start=True, stop=True)
                                banks.fill(last, ("W", d, duo, q, lv))
                            for q in range(2):
                                banks.evacuated(pe, ("W", d, duo, q, lv))
                                if lv:
                                    banks.evacuated(pe, ("dXT", d, duo, q, lv - 1))
                                if lv < LEVELS - 1:
                                    ps = banks.claim(pe, ("dX", d, duo, q, lv))
                                    for u in range(4):
                                        last = mm(ps[:, u * P:(u + 1) * P], XT[:, q, u, :], W1[:, q, u, :],
                                                  start=True, stop=True)
                                    banks.fill(last, ("dX", d, duo, q, lv))
                                ps = banks.claim(pe, ("dXT", d, duo, q, lv))
                                for u in range(4):
                                    last = mm(ps[:, u * P:(u + 1) * P], W1[:, q, u, :], XT[:, q, u, :],
                                              start=True, stop=True)
                                banks.fill(last, ("dXT", d, duo, q, lv))
                        if duo == 0:
                            for m in range(MT):
                                if d == 0:
                                    banks.evacuated(pe, ("Vtok", m))
                        for q in range(2):
                            p = 2 * duo + q
                            ps = banks.claim(pe, ("Q1", d, duo, q))
                            for u in range(4):
                                c = (2 * p + u // 2) * HD
                                last = mm(ps[:, u * HD:(u + 1) * HD], L2T[:, q, u, :], Vtok[:, u % 2, c:c + HD],
                                          start=True, stop=True)
                            banks.fill(last, ("Q1", d, duo, q))
                            ps = banks.claim(pe, ("Atok", d, duo, q))
                            for m in range(MT):
                                last = turn(ps[:, m * P:(m + 1) * P], AR[:, p, 0, m * P:(m + 1) * P], ident[:, :])
                            banks.fill(last, ("Atok", d, duo, q))
                            pe.wait_ge(inv_ready, 4 * d + 2 * duo + q + 1)
                            banks.evacuated(pe, ("Q1", d, duo, q))
                            ps = banks.claim(pe, ("SA0", d, duo, q))
                            for u in range(4):
                                last = mm(ps[:, u * HD:(u + 1) * HD], XT[:, q, u, :], Q1[:, u * HD:(u + 1) * HD],
                                          start=True, stop=True)
                            banks.fill(last, ("SA0", d, duo, q))
                            banks.evacuated(pe, ("Atok", d, duo, q))
                            ps = banks.claim(pe, ("XAT", d, duo, q))
                            for u in range(4):
                                o, m = (u // 2) * HD, u % 2
                                last = mm(ps[o:o + HD, m * P:(m + 1) * P], Atok[:, m, o:o + HD], XT[:, q, u, :],
                                          start=True, stop=True)
                            banks.fill(last, ("XAT", d, duo, q))
                    own_part = [(m, p, hh) for m in range(MT) for p in range(RT) for hh in range(2)]
                    first_of = {}
                    for n in range(NCH - 1):
                        for m, p, hh in own_part[n::NCH - 1]:
                            first_of.setdefault(m, (p, hh))
                    for m in range(MT):
                        banks.claim(pe, ("Y", d, m))
                    for n, c in enumerate(scan_order[d]):
                        o, m = (c % 2) * CH, c // 2
                        if n:
                            pe.wait_ge(state_ready, 3 * d + n)
                            ps = banks.claim(pe, ("SA", d, n))
                            for p in range(RT):
                                last = mm(ps[o:o + CH, p * P:(p + 1) * P], XAT[:, p, c * CH:(c + 1) * CH],
                                          state[:, c, p, :], start=True, stop=True)
                            banks.fill(last, ("SA", d, n))
                        if n < NCH - 1:
                            pe.wait_ge(sa_ready, 4 * d + n + 1)
                            ps = banks.claim(pe, ("state", d, n))
                            for p in range(RT):
                                s = slice(p * P, (p + 1) * P)
                                mm(ps[:, s], Btok[o:o + CH, m, s], SA[o:o + CH, m, s], start=True, stop=False)
                                last = mm(ps[:, s], Ktok[o:o + CH, m, s], Vtok[o:o + CH, m, s],
                                          start=False, stop=True)
                            banks.fill(last, ("state", d, n))
                            for m, p, hh in own_part[n::NCH - 1]:
                                cs_ = slice(p * P + hh * HD, p * P + (hh + 1) * HD)
                                mm(banks.t[2 + m][:, cs_], MRK[:, p, 2 * hh + m, :], Vtok[:, m, cs_],
                                   start=(p, hh) == first_of[m], stop=False, skip_group_check=True)
                    pe.wait_ge(sa_ready, 4 * d + 4)
                    for m in range(MT):
                        ps = banks.t[2 + m]
                        for p in range(RT):
                            for hh in range(2):
                                cs_ = slice(p * P + hh * HD, p * P + (hh + 1) * HD)
                                last = mm(ps[:, cs_], MRB[:, p, 2 * hh + m, :], SA[:, m, cs_],
                                          start=False, stop=False, skip_group_check=True)
                            for c in (2 * m, 2 * m + 1):
                                if c != scan_order[d][0]:
                                    o = (c % 2) * CH
                                    last = mm(ps[o:o + CH, p * P:(p + 1) * P], AR[:, p, 1, c * CH:(c + 1) * CH],
                                              state[:, c, p, :], start=False, stop=True, skip_group_check=True)
                        banks.fill(last, ("Y", d, m))
                for m in range(MT):
                    ps = banks.claim(pe, ("gate", m))
                    banks.fill(mm(ps[:, :], low[:, 2, m * P:(m + 1) * P], g2[:, :], start=True, stop=True),
                               ("gate", m))
                for g in range(8):
                    c = a_gate + g // 2
                    if g % 2 == 0:
                        landed(c)
                    o = (g % 2) * 2 * P
                    ps = banks.claim(pe, ("gates", g))
                    banks.fill(hidden(ps, rows8(slotA(c))[:, :, o:o + 2 * P]), ("gates", g))
                pe.wait_ge(oa_ready, 1)
                to_features(("oaT",), ytmp.rearrange("p (m c) -> p m c", m=MT), 2)
                landed(a_wa)
                landed(a_wb)
                for g in range(2):
                    banks.evacuated(pe, ("obT", g))
                    banks.evacuated(pe, ("oaT", g))
                for t in range(DT):
                    ps = banks.claim(pe, ("branch", t))
                    for half, (n, src) in enumerate(((a_wa, oaT), (a_wb, obT))):
                        w = slotA(n).rearrange("p (k c) -> p k c", k=4)
                        for k in range(4):
                            last = mm(ps[:, half * S:(half + 1) * S], w[:, k, t * P:(t + 1) * P], src[:, k, :],
                                      start=(k == 0), stop=(k == 3))
                    banks.fill(last, ("branch", t))
                pe.wait_ge(merged, DT)
                for n in range(2):
                    landed(a_out + n)
                    w = rows8(slotA(a_out + n))
                    for m in range(MT):
                        ps = banks.claim(pe, ("out", n, m))
                        for k in range(DT):
                            last = mm(ps[:, :], yT[:, k, m * P:(m + 1) * P], w[:, k, :],
                                      start=(k == 0), stop=(k == DT - 1))
                        banks.fill(last, ("out", n, m))
                ffn(2, l)
                leave(pe, l)

        @block.scalar
        def _(act):
            f = nc.scalar.activation
            root_count = [0]

            def roots(width):
                root_count[0] += 1
                act.wait_ge(var_ready, root_count[0])
                f(small[:, 32:32 + width], small[:, 0:width], ACT.Sqrt).then_inc(std_ready, 1)

            def take(key, dst, view_, func=ACT.Copy, **kw):
                banks.free(f(dst, view_(banks.read(act, key)), func, **kw), key)

            def split_up(k, s):
                n = ffn_first[k] + s
                act.wait_ge(a_landed[n % slots_A], 32 * (n // slots_A + 1))
                if s >= 2:
                    banks.read(act, ("u", k, s - 2))
                f(parts_of(highA[:, s % 2, :]), slotA(n), ACT.Copy).then_inc(highA_ready, 1)

            def split_down(k, s):
                fills = s // B_SLOTS + 1 + (k // 2) * ((STEPS - 1 - s % B_SLOTS) // B_SLOTS + 1)
                act.wait_ge(b_landed[s % B_SLOTS], 16 * fills)
                if s >= 2:
                    act.wait_ge(down_done, (k // 2) * (STEPS - 1) + s - 1)
                f(parts_of(highB[:, s % 2, :]), ringB[:, s % B_SLOTS, :], ACT.Copy).then_inc(highB_ready, 1)

            def norm(k, at):
                if k:
                    act.wait_ge(x_ready, k)
                for m in range(MT):
                    last = f(xn[:, m, :], x_tok[:, m, :], ACT.Square, accum_out=small[:, 120 + m:121 + m])
                last.then_inc(squares_ready, 1)
                if k != 1:
                    split_up(k, 0)
                roots(MT)
                if k == 0:
                    take("cols", cols[:, :], lambda ps: ps[:, 0:n_rows])
                    banks.evacuated(act, "cols")
                for b in range(2):
                    key = ("xT", k, b)
                    ps = banks.read(act, key)
                    for t in range(2):
                        j = 2 * b + t
                        last = f(hT[:, j, :], ps[:, t * S:(t + 1) * S], ACT.Copy, scale=cols[:, at + j:at + j + 1])
                        if k != 1:
                            last = f(parts_of(hT_high[:, j, :]), ps[:, t * S:(t + 1) * S], ACT.Copy,
                                     scale=cols[:, at + j:at + j + 1])
                    banks.free(last, key)

            def ffn(k):
                for s in range(STEPS):
                    split_down(k, s)
                    if s + 1 < STEPS:
                        split_up(k, s + 1)
                    if s >= 2:
                        banks.evacuated(act, ("u", k, s - 2))
                    take(("g", k, s), silu_g[:, s % 2, :], lambda ps: ps[:, :], ACT.Silu)

            with act.Fori(0, DEPTH) as l:
                root_count[0] = 0
                norm(0, r_ffn1)
                ffn(0)
                norm(1, r_mix)
                for c in range(3):
                    for m in range(MT):
                        take(("at", c, m), at_tok[:, m, c * 512:(c + 1) * 512], lambda ps: ps[:, :])
                act.wait_ge(lam_asked, 1)
                f(lam[:, 2:4], lam[:, 0:2], ACT.Exp).then_inc(lam_exp, 1)
                roots(32)
                dst = [rkv[:, t, :] for t in range(12)] + [low[:, t, :] for t in range(3)]
                for g in range(8):
                    n = 1 if g == 7 else 2
                    ps = banks.read(act, ("rw", g))
                    if g >= 2:
                        act.wait_ge(neighbours_read, g - 1)
                    f(edge[:, g % 2, 0:n, 1:S + 1], pair_of(ps)[:, 0:n, :], ACT.Copy)
                    for t in range(n):
                        j = 2 * g + t
                        last = f(dst[j], ps[:, t * S:(t + 1) * S], ACT.Copy, scale=mus[:, 0, j:j + 1])
                    banks.free(last, ("rw", g))
                act.wait_ge(mixed_ready, 8)
                f(low[:, 0, :], low[:, 0, :], ACT.Tanh)
                f(low[:, 2, :], low[:, 2, :], ACT.Sigmoid).then_inc(low_ready, 1)
                for g in range(4):
                    take(("qkT", g), (qT if g < 2 else kT)[:, 2 * (g % 2):2 * (g % 2) + 2, :], pair_of)
                for s in range(2 * BH + 2):
                    if s < 2 * BH:
                        o = 72 + 4 * (s % 4)
                        act.wait_ge(max_ready, s + 1)
                        for m in range(MT):
                            pr = prob[:, (s // 2) % 2, s % 2, m, :]
                            last = f(pr, pr, ACT.Exp, bias=small[:, o + m:o + m + 1], scale=HD ** -0.5,
                                     accum_out=small[:, o + 2 + m:o + 3 + m])
                        last.then_inc(exp_done, 1)
                    if s % 2 and s > 1:
                        h = s // 2 - 1
                        take(("combT", h), combT[:, h % 2, :, :], pair_of)
                roots(8)
                for g in range(2):
                    take(("obT", g), obT[:, 2 * g:2 * g + 2, :], pair_of)
                for g in range(2):
                    take(("kkss", g), sq[:, 512 * g:512 * (g + 1)], lambda ps: ps[:, :], ACT.Sqrt)
                for m in range(MT):
                    take(("Vtok", m), Vtok[:, m, :], lambda ps: ps[:, :])
                for d in range(2):
                    if d:
                        for m in range(MT):
                            banks.evacuated(act, ("Y", 0, m))
                    for name, at, out in (("dec", r_w0, sw), ("rate", r_a0, ic)):
                        for g in range(2):
                            ps = banks.read(act, (name, d, g))
                            for t in range(2):
                                j = 2 * g + t
                                last = f(out[:, j * S:(j + 1) * S], ps[:, t * S:(t + 1) * S], ACT.Sigmoid,
                                         bias=cols[:, at + d * RT + j:at + d * RT + j + 1])
                            banks.free(last, (name, d, g))
                    act.wait_ge(cum_ready, d + 1)
                    f(AR[:, :, 1, :], cs.rearrange("p (t s) -> p t s", s=S), ACT.Exp, scale=-DECAY)
                    f(AR[:, :, 0, :], ce.rearrange("p (t s) -> p t s", s=S), ACT.Exp, scale=-DECAY)
                    f(Bt, cs.rearrange("p (t s) -> p t s", s=S), ACT.Exp, scale=DECAY).then_inc(exps_ready, 1)
                    take(("bonus", d), bonus[:, d], lambda ps: ps[:, 0:16].rearrange("p (m h) -> p m h", m=MT))
                    for name, dst_ in (("Btok", Btok), ("Ktok", Ktok)):
                        for m in range(MT):
                            take((name, d, m), dst_[:, m, :], lambda ps: ps[:, :])
                    for duo in range(2):
                        for lv in range(LEVELS):
                            for q in range(2):
                                take(("W", d, duo, q, lv), W1[:, q, :, :],
                                     lambda ps: ps[:, :].rearrange("p (u t) -> p u t", u=4))
                        for q in range(2):
                            p = 2 * duo + q
                            take(("Q1", d, duo, q), Q1, lambda ps: ps[:, 0:256])
                            take(("Atok", d, duo, q), Atok, lambda ps: ps[:, 0:256].rearrange("p (m c) -> p m c", m=MT))
                            out = SA0[:, :, p * P:(p + 1) * P].rearrange("p m (h c) -> p h m c", h=2)
                            for hh in range(2):
                                ps = banks.read(act, ("SA0", d, duo, q))
                                last = f(out[:, hh], ps[:, hh * P:(hh + 1) * P].rearrange("p (m c) -> p m c", m=MT),
                                         ACT.Copy)
                            banks.free(last, ("SA0", d, duo, q))
                            take(("XAT", d, duo, q), XAT[:, p, :], lambda ps: ps[:, 0:S])
                roots(16)
                for g in range(8):
                    if g == 0:
                        act.wait_ge(oa_ready, 1)
                    take(("gates", g), gates[:, 2 * g:2 * g + 2, :], pair_of, ACT.Sigmoid)
                for g in range(2):
                    take(("oaT", g), oaT[:, 2 * g:2 * g + 2, :], pair_of)
                norm(2, r_ffn2)
                ffn(2)
                leave(act, l)

        @block.vector
        def _(dve):
            v = nc.vector
            tt, ts, red, stt = v.tensor_tensor, v.tensor_scalar, v.tensor_reduce, v.scalar_tensor_tensor

            def mask(n, *lead):
                ap = masks[:, n, :]
                for k in lead:
                    ap = spread(ap, 1, k)
                return ap

            with dve.Fori(0, DEPTH) as l:
                step = Chain(dve, dve_steps)
                root_count = [0]

                def root(width):
                    root_count[0] += 1
                    dve.wait_ge(std_ready, root_count[0])
                    return step(v.reciprocal(small[:, 64:64 + width], small[:, 32:32 + width]))

                def variance(out, in_, scale, eps):
                    ts(out, in_, scale, eps, ALU.mult, ALU.add).then_inc(var_ready, 1)

                def norm(k, at):
                    dve.wait_ge(squares_ready, k + 1)
                    variance(small[:, 0:MT], small[:, 120:120 + MT], 1.0 / D, 1e-6)
                    root(MT)
                    for m in range(MT):
                        last = ts(xn[:, m, :], x_tok[:, m, :], small[:, 64 + m:65 + m], None, ALU.mult)
                    last.then_inc(xn_ready, 1)
                    if k != 1:
                        split_up(k, 0)
                    if k == 0:
                        banks.evacuated(dve, "cols")
                    for b in range(2, 4):
                        key = ("xT", k, b)
                        ps = banks.read(dve, key)
                        for t in range(2):
                            j = 2 * b + t
                            last = ts(hT[:, j, :], ps[:, t * S:(t + 1) * S], cols[:, at + j:at + j + 1], None,
                                      ALU.mult)
                            if k != 1:
                                last = ts(parts_of(hT_high[:, j, :]), ps[:, t * S:(t + 1) * S],
                                          cols[:, at + j:at + j + 1], None, ALU.mult)
                        banks.free(last, key)
                    if k != 1:
                        for b in range(4):
                            banks.evacuated(dve, ("xT", k, b))
                            two = slice(2 * b, 2 * b + 2)
                            tt(parts_of(hT[:, two, :]), hT[:, two, :], parts_of.value(hT_high[:, two, :]),
                               ALU.subtract).then_inc(hT_split, 1)

                def split_up(k, s):
                    w = slotA(ffn_first[k] + s)
                    dve.wait_ge(highA_ready, (k // 2) * STEPS + s + 1)
                    tt(parts_of(w), w, parts_of.value(highA[:, s % 2, :]), ALU.subtract).then_inc(lowA_ready, 1)

                def split_down(k, s):
                    w = ringB[:, s % B_SLOTS, :]
                    dve.wait_ge(highB_ready, (k // 2) * STEPS + s + 1)
                    tt(parts_of(w), w, parts_of.value(highB[:, s % 2, :]), ALU.subtract).then_inc(lowB_ready, 1)

                def ffn(k):
                    for s in range(STEPS):
                        split_down(k, s)
                        if s + 1 < STEPS:
                            split_up(k, s + 1)
                        if s >= 2:
                            dve.wait_ge(down_done, (k // 2) * (STEPS - 1) + s - 1)
                        banks.evacuated(dve, ("g", k, s))
                        ps = banks.read(dve, ("u", k, s))
                        tt(parts_of(hid_high[:, s % 2, :]), silu_g[:, s % 2, :], ps[:, :], ALU.mult)
                        banks.free(tt(hid[:, s % 2, :], silu_g[:, s % 2, :], ps[:, :], ALU.mult), ("u", k, s))
                        banks.evacuated(dve, ("u", k, s))
                        tt(parts_of(hid[:, s % 2, :]), hid[:, s % 2, :], parts_of.value(hid_high[:, s % 2, :]), ALU.subtract
                           ).then_inc(hid_split, 1)
                    for m in range(MT):
                        for n in range(2):
                            key = ("y", k, 2 * m + n)
                            ps = banks.read(dve, key)
                            xs = x_tok[:, m, n * 512:(n + 1) * 512]
                            banks.free(stt(xs, ps[:, :], 0.5, xs, ALU.mult, ALU.add), key)
                    for n in range(4):
                        banks.evacuated(dve, ("y", k, n))
                    dve.nop().then_inc(x_ready, 1)

                norm(0, r_ffn1)
                ts(mus[:, 0, :], cols[:, r_mu:r_mu + CT], -1.0, 1.0, ALU.mult, ALU.add)
                ts(mus[:, 1, :], cols[:, r_mu:r_mu + CT], 0.5, None, ALU.mult)
                v.memset(ones[:, :], 1.0)
                step(v.memset(edge[:, :, :, 0:S + 2:S + 1], 0.0))
                ffn(0)
                norm(1, r_mix)

                dve.wait_ge(params_landed, l * n_params + n_params)
                dve.wait_ge(tables_landed, 4 * 16)
                lprod = sq[:, 0:2 * HD].rearrange("p (a d) -> p a d", a=2)
                step(tt(lprod, lamv[:, 0::2, :], lamv[:, 1::2, :], ALU.mult))
                red(lam[:, 0:2], lprod, AX, ALU.add).then_inc(lam_asked, 1)
                dve.wait_ge(lam_exp, 1)
                step(tt(lam[:, 4:5], lam[:, 3:4], lam[:, 2:3], ALU.subtract))
                step(tt(lam[:, 4:5], lam[:, 4:5], lamc[:, 0:1], ALU.subtract))
                for c in range(2):
                    for m in range(MT):
                        banks.evacuated(dve, ("at", c, m))
                sq3 = sq.rearrange("p (m c) -> p m c", m=MT)
                for m in range(MT):
                    last = tt(sq3[:, m], at_tok[:, m, 0:2 * RW], at_tok[:, m, 0:2 * RW], ALU.mult)
                step(last)
                step(red(small[:, 120:152], sq.rearrange("p (h d) -> p h d", d=HD), AX, ALU.add))
                variance(small[:, 0:32], small[:, 120:152], 1.0 / HD, 1e-6)
                root(32)
                for m in range(MT):
                    qk = at_tok[:, m, 0:2 * RW].rearrange("p (h d) -> p h d", d=HD)
                    step(tt(qk, qk, spread(small[:, 64 + 16 * m:80 + 16 * m], 2, HD), ALU.mult))
                    for n in range(2):
                        last = tt(qk[:, 8 * n:8 * n + 8], qk[:, 8 * n:8 * n + 8], spread(qkg[:, n, :], 1, 8),
                                  ALU.mult)
                last.then_inc(at_ready, 1)

                dst = [rkv[:, t, :] for t in range(12)] + [low[:, t, :] for t in range(3)]
                for g in range(8):
                    n = 1 if g == 7 else 2
                    if g >= 2:
                        dve.wait_ge(mixed_ready, g - 1)
                    banks.evacuated(dve, ("rw", g))
                    tt(nbr[:, g % 2, 0:n, :], edge[:, g % 2, 0:n, 0:S], edge[:, g % 2, 0:n, 2:S + 2], ALU.add
                       ).then_inc(neighbours_read, 1)
                    dve.wait_ge(neighbours_read, g + 1)
                    for t in range(n):
                        j = 2 * g + t
                        last = stt(dst[j], nbr[:, g % 2, t, :], mus[:, 1, j:j + 1], dst[j], ALU.mult, ALU.add)
                    last.then_inc(mixed_ready, 1)

                for s in range(2 * BH + 2):
                    if s < 2 * BH:
                        h, o = s // 2, 72 + 4 * (s % 4)
                        slope = 2.0 ** (-8.0 * (h + 1) / BH)
                        pr = prob[:, h % 2, s % 2, :, :]
                        ps = banks.read(dve, ("score", s))
                        banks.free(stt(pr, dist[:, :, :], -slope * HD ** 0.5, pair_of(ps), ALU.mult, ALU.add),
                                   ("score", s))
                        banks.evacuated(dve, ("score", s))
                        step(red(small[:, 88:90], pr, AX, ALU.max))
                        ts(small[:, o:o + 2], small[:, 88:90], -HD ** -0.5, None, ALU.mult).then_inc(max_ready, 1)
                        dve.wait_ge(max_ready, s + 1)
                    if s % 2 and s > 1:
                        h = s // 2 - 1
                        o = 72 + 8 * (h % 2)
                        dve.wait_ge(exp_done, 2 * h + 2)
                        if h >= 2:
                            banks.read(dve, ("combT", h - 2))
                        v.reciprocal(small[:, 92:94], small[:, o + 2:o + 4])
                        step(v.reciprocal(small[:, 94:96], small[:, o + 6:o + 8]))
                        step(ts(small[:, 94:96], small[:, 94:96], lam[:, 4:5], None, ALU.mult))
                        for m in range(MT):
                            last = ts(prob[:, h % 2, 1, m, :], prob[:, h % 2, 1, m, :], small[:, 94 + m:95 + m],
                                      None, ALU.mult)
                        step(last)
                        for m in range(MT):
                            last = stt(comb[:, h % 2, m, :], prob[:, h % 2, 0, m, :], small[:, 92 + m:93 + m],
                                       prob[:, h % 2, 1, m, :], ALU.mult, ALU.add)
                        last.then_inc(comb_ready, 1)
                        dve.wait_ge(comb_ready, h + 1)
                for m in range(MT):
                    ps = banks.read(dve, ("o", m))
                    banks.free(v.tensor_copy(ob[:, m, :], ps[:, :]), ("o", m))
                    banks.evacuated(dve, ("o", m))
                ob2 = ob.rearrange("p m c -> p (m c)")
                step(tt(sq[:, 0:1024], ob2, ob2, ALU.mult))
                step(red(small[:, 120:128], sq[:, 0:1024].rearrange("p (h d) -> p h d", d=2 * HD), AX, ALU.add))
                variance(small[:, 0:8], small[:, 120:128], 1.0 / (2 * HD), 1e-6)
                root(8)
                step(ts(small[:, 64:72], small[:, 64:72], lamc[:, 1:2], None, ALU.mult))
                obh = ob2.rearrange("p (h d) -> p h d", d=2 * HD)
                step(tt(obh, obh, spread(small[:, 64:72], 2, 2 * HD), ALU.mult))
                tt(obh, obh, spread(subg[:, :], 1, 8), ALU.mult).then_inc(ob_ready, 1)
                dve.wait_ge(ob_ready, 1)

                r3, k3 = rkv[:, 0:RT, :], rkv[:, RT:2 * RT, :]
                sqt = sq[:, 0:1024].rearrange("p (t s) -> p t s", s=S)
                dve.wait_ge(mixed_ready, 8)
                step(tt(kk, k3, spread(cols[:, r_kk:r_kk + RT], 2, S), ALU.mult))
                tt(sqt, kk, kk, ALU.mult).then_inc(kk_squared, 1)
                for g in range(2):
                    banks.evacuated(dve, ("kkss", g))
                step(ts(sqt, sqt, 1e-12, None, ALU.max))
                step(v.reciprocal(sqt, sqt))
                step(tt(kk, kk, sqt, ALU.mult))

                for d in range(2):
                    for g in range(2):
                        banks.evacuated(dve, ("dec", d, g))
                        banks.evacuated(dve, ("rate", d, g))
                    if d:
                        for m in range(MT):
                            banks.evacuated(dve, ("Y", 0, m))
                    for n in range(RT * NCH):
                        w = sw[:, n * CH:(n + 1) * CH]
                        c = cs[:, n * CH:(n + 1) * CH]
                        if d:
                            w, c = w[:, ::-1], c[:, ::-1]
                        last = v.tensor_tensor_scan(c, ones[:, :], w, 0.0, ALU.mult, ALU.add)
                    step(last)
                    tt(ce, cs, sw, ALU.subtract).then_inc(cum_ready, 1)
                    ic3 = ic.rearrange("p (t s) -> p t s", s=S)
                    sw3 = sw.rearrange("p (t s) -> p t s", s=S)
                    dve.wait_ge(cum_ready, d + 1)
                    kd = SA0.rearrange("p m c -> p (m c)").rearrange("p (t s) -> p t s", s=S)
                    step(stt(kd, ic3, -1.0, spread(cols[:, r_ka:r_ka + RT], 2, S), ALU.add, ALU.mult))
                    step(stt(kd, kd, 1.0, k3, ALU.add, ALU.mult))
                    step(tt(sw3, r3, spread(cols[:, r_rk:r_rk + RT], 2, S), ALU.mult))
                    tt(sw3, sw3, kd, ALU.mult).then_inc(bonus_ready, 1)
                    step(tt(ic3, ic3, kk, ALU.mult))
                    dve.wait_ge(exps_ready, d + 1)
                    ends = slice(CH - 1, S, CH) if d == 0 else slice(0, S, CH)
                    step(v.tensor_copy(dcol.rearrange("p (t c) -> p t c", c=NCH), AR[:, :, 1, ends]))
                    tt(AR[:, :, 1, :], AR[:, :, 1, :], r3, ALU.mult)
                    stt(AR[:, :, 0, :], AR[:, :, 0, :], -1.0, kk, ALU.mult, ALU.mult)
                    step(tt(Kt, Bt, kd, ALU.mult))
                    tt(Bt, Bt, ic3, ALU.mult).then_inc(ABKR_ready, 1)
                    dve.wait_ge(ABKR_ready, d + 1)
                    banks.evacuated(dve, ("bonus", d))

                    for duo in range(2):
                        for q in range(2):
                            p = 2 * duo + q
                            for hh in range(2):
                                for name, low_, high in (("UR", U, MRB), ("KR", L2T, MRK)):
                                    key = (name, d, duo, q, hh)
                                    ps = banks.read(dve, key)[:, :].rearrange("p (m r t) -> p m r t", m=MT, r=2)
                                    tt(low_[:, q, 2 * hh:2 * hh + 2, :], ps[:, :, 0, :], mask(d, MT), ALU.mult)
                                    banks.free(tt(high[:, p, 2 * hh:2 * hh + 2, :], ps[:, :, 1, :],
                                                  mask(2 + d, MT), ALU.mult), key)
                                key = ("L", d, duo, q, hh)
                                ps = banks.read(dve, key)[:, 0:S].rearrange("p (m t) -> p m t", m=MT)
                                banks.free(tt(X[:, q, 2 * hh:2 * hh + 2, :], ps, mask(4 + d, MT), ALU.mult), key)
                            banks.evacuated(dve, ("UR", d, duo, q, 1))
                            banks.evacuated(dve, ("L", d, duo, q, 1))
                            idn = spread(ident[:, :], 1, 4)
                            step(tt(XT[:, q], U[:, q], mask(6, 4), ALU.mult))
                            step(tt(X[:, q], X[:, q], idn, ALU.add))
                            step(tt(XT[:, q], XT[:, q], idn, ALU.add))
                        for lv in range(LEVELS):
                            for q in range(2):
                                if lv:
                                    banks.read(dve, ("W", d, duo, q, lv - 1))
                                tt(Z[:, q], U[:, q], mask(7 + lv, 4), ALU.mult).then_inc(z_ready, 1)
                                if lv:
                                    for name, inverse in (("dX", X), ("dXT", XT)):
                                        key = (name, d, duo, q, lv - 1)
                                        ps = banks.read(dve, key)
                                        banks.free(tt(inverse[:, q], ps[:, :].rearrange("p (u t) -> p u t", u=4),
                                                      inverse[:, q], ALU.add), key)
                            for q in range(2):
                                if lv:
                                    banks.evacuated(dve, ("dXT", d, duo, q, lv - 1))
                        for q in range(2):
                            key = ("dXT", d, duo, q, LEVELS - 1)
                            ps = banks.read(dve, key)
                            banks.free(tt(XT[:, q], ps[:, :].rearrange("p (u t) -> p u t", u=4), XT[:, q], ALU.add),
                                       key)
                            banks.evacuated(dve, key)
                            dve.nop().then_inc(inv_ready, 1)

                    for duo in range(2):
                        for q in range(2):
                            banks.evacuated(dve, ("SA0", d, duo, q))
                            banks.evacuated(dve, ("XAT", d, duo, q))
                    dc = dcol.rearrange("p (t c) -> p t c", c=NCH)
                    for n, c in enumerate(scan_order[d]):
                        o, m = (c % 2) * CH, c // 2
                        part = slice(o, o + CH)
                        if n == 0:
                            v.tensor_copy(SA[part, m, :], SA0[part, m, :]).then_inc(sa_ready, 1)
                        else:
                            key = ("SA", d, n)
                            ps = banks.read(dve, key)
                            banks.free(tt(SA[part, m, :], ps[part, :], SA0[part, m, :], ALU.add), key)
                            banks.evacuated(dve, key)
                            dve.nop().then_inc(sa_ready, 1)
                        if n < NCH - 1:
                            nxt = scan_order[d][n + 1]
                            key = ("state", d, n)
                            ps = banks.read(dve, key)[:, :].rearrange("p (q v) -> p q v", q=RT)
                            S1 = state[:, nxt]
                            decay = spread(dc[:, :, c], 2, P)
                            if n:
                                banks.free(tt(S1, ps, state[:, c], ALU.add), key)
                                banks.evacuated(dve, key)
                                step(tt(S1, S1, decay, ALU.mult))
                            else:
                                banks.free(tt(S1, ps, decay, ALU.mult), key)
                                banks.evacuated(dve, key)
                            tt(S1, S1, spread(heads1[:, :], 1, RT), ALU.mult).then_inc(state_ready, 1)
                            dve.wait_ge(state_ready, 3 * d + n + 1)
                    for m in range(MT):
                        key = ("Y", d, m)
                        ps = banks.read(dve, key)
                        if d == 0:
                            last = v.tensor_copy(Y[:, m, :], ps[:, :])
                        else:
                            last = tt(Y[:, m, :], ps[:, :], Y[:, m, :], ALU.add)
                        banks.free(last, key)
                        banks.evacuated(dve, key)

                y1 = Y.rearrange("p m c -> p (m c)")
                yh = y1.rearrange("p (h d) -> p h d", d=HD)
                t1 = ytmp.rearrange("p (h d) -> p h d", d=HD)
                t2 = ytmp2.rearrange("p (h d) -> p h d", d=HD)
                step(red(small[:, 120:136], yh, AX, ALU.add))
                step(ts(small[:, 120:136], small[:, 120:136], 1.0 / HD, None, ALU.mult))
                step(tt(t1, yh, spread(small[:, 120:136], 2, HD), ALU.subtract))
                step(tt(t2, t1, t1, ALU.mult))
                step(red(small[:, 136:152], t2, AX, ALU.add))
                variance(small[:, 0:16], small[:, 136:152], 1.0 / HD, 64e-5)
                root(16)
                step(tt(t1, t1, spread(small[:, 64:80], 2, HD), ALU.mult))
                ym = ytmp.rearrange("p (m c) -> p m c", m=MT)
                step(tt(ym, ym, spread(lnx[:, 0, :], 1, MT), ALU.mult))
                step(tt(ym, ym, spread(lnx[:, 1, :], 1, MT), ALU.add))
                step(tt(small[:, 152:168].rearrange("p (m h) -> p m h", m=MT), bonus[:, 0], bonus[:, 1], ALU.add))
                step(tt(t2, Vtok.rearrange("p m (h d) -> p (m h) d", d=HD), spread(small[:, 152:168], 2, HD),
                        ALU.mult))
                step(tt(ytmp, ytmp, ytmp2, ALU.add))
                for m in range(MT):
                    ps = banks.read(dve, ("gate", m))
                    banks.free(tt(ym[:, m], ps[:, :], ym[:, m], ALU.mult), ("gate", m))
                for m in range(MT):
                    banks.evacuated(dve, ("gate", m))
                dve.nop().then_inc(oa_ready, 1)

                for g in range(8):
                    banks.evacuated(dve, ("gates", g))
                for t in range(DT):
                    ps = banks.read(dve, ("branch", t))
                    o = 512 * (t % 2)
                    if t >= 2:
                        dve.wait_ge(merged, t - 1)
                    tt(btmp[:, o:o + S], ps[:, 0:S], gates[:, t, :], ALU.mult)
                    banks.free(tt(btmp[:, o + S:o + 2 * S], ps[:, S:2 * S], gates[:, DT + t, :], ALU.mult),
                               ("branch", t))
                    banks.evacuated(dve, ("branch", t))
                    tt(yT[:, t, :], btmp[:, o:o + S], btmp[:, o + S:o + 2 * S], ALU.add).then_inc(merged, 1)
                dve.wait_ge(merged, DT)
                for n in range(2):
                    for m in range(MT):
                        key = ("out", n, m)
                        ps = banks.read(dve, key)
                        xs = x_tok[:, m, n * 512:(n + 1) * 512]
                        banks.free(tt(xs, ps[:, :], xs, ALU.add), key)
                for n in range(2):
                    for m in range(MT):
                        banks.evacuated(dve, ("out", n, m))
                dve.nop().then_inc(x_ready, 1)
                norm(2, r_ffn2)
                ffn(2)
                leave(dve, l)


def program(nc, a, out):
    with ExitStack() as ctx:
        def sb(name, shape):
            return ctx.enter_context(nc.sbuf_tensor(name, shape, F32))

        x_tok = sb("x_tok", [P, MT, D])
        consts = {
            "ident": sb("ident", [P, P]),
            "cos": sb("cos", [P, MT, HD // 2]),
            "sin": sb("sin", [P, MT, HD // 2]),
            "jlt": sb("jlt", [P, NG * NG]),
            "landed": ctx.enter_context(nc.semaphore("constants_landed")),
            "x_landed": ctx.enter_context(nc.semaphore("x_landed")),
            "count": 4 * 16,
        }
        stored = ctx.enter_context(nc.semaphore("out_stored"))
        x_v = a["x"][0].rearrange("(m p) d -> p m d", p=P)
        with nc.Block() as block:
            @block.sync
            def _(sp):
                for m in range(MT):
                    sp.dma_start(x_tok[:, m, :], x_v[:, m, :]).then_inc(consts["x_landed"], 16)
                for name in ("ident", "cos", "sin", "jlt"):
                    sp.dma_start(consts[name][:, :] if name in ("ident", "jlt") else consts[name][:, :, :],
                                 a["const_" + name]).then_inc(consts["landed"], 16)

        first_block(nc, a, x_tok, consts)
        second_block(nc, a, x_tok, consts)

        with nc.Block() as block:
            @block.sync
            def _(sp):
                sp.dma_start(out[0].rearrange("(m p) d -> p m d", p=P), x_tok[:, :, :]).then_inc(stored, 16)
                sp.wait_ge(stored, 16)


def shape_constants():
    t = np.arange(S)
    cols_, rows_ = 64, S // 64
    place = [(t // cols_ - rows_ // 2).astype(np.float32), (t % cols_ - cols_ // 2).astype(np.float32)]
    freq = (10000.0 ** (-np.arange(HD // 4, dtype=np.float32) / (HD // 4))).astype(np.float32)
    angle = np.concatenate([p[:, None] * freq for p in place], -1).astype(np.float32)

    def by_token(x):
        return np.ascontiguousarray(x.reshape(MT, P, -1).transpose(1, 0, 2), np.float32)

    g = np.arange(NG)
    earlier = np.tile((g[None, :] < g[:, None]).astype(np.float32).reshape(1, NG * NG), (P, 1))
    j, c = np.arange(P)[:, None], np.arange(P)[None, :]
    same = j // CH == c // CH
    pair = j // 2 == c // 2
    masks = [same & (j < c), same & (j > c), same & (j <= c), same & (j >= c), pair & (j > c), pair & (j < c)]
    masks += [(j // (2 * b) == c // (2 * b)) & (j // b != c // b) for b in (1, 2, 4, 8, 16, 32)]
    head_of = np.zeros((P, RT, 2 * RT), np.float32)
    for r in range(RT):
        head_of[:, r, 2 * r:2 * r + 2] = np.arange(P)[:, None] // HD == np.arange(2)[None, :]
    lam = np.zeros((DEPTH, P, 2), np.float32)
    for l in range(DEPTH):
        start = 0.8 - 0.6 * math.exp(-0.3 * l)
        lam[l] = start, 1.0 - start
    return {
        "const_ident": np.eye(P, dtype=np.float32),
        "const_cos": by_token(np.cos(angle)),
        "const_sin": by_token(np.sin(angle)),
        "const_jlt": earlier,
        "const_masks": np.ascontiguousarray(np.stack(masks, 1), np.float32),
        "const_dist": by_token(np.abs(t[:, None] - t[None, :]).astype(np.float32)),
        "const_heads": same.astype(np.float32),
        "const_headsel": head_of,
        "const_lam": lam,
    }


def kernel(**inputs):
    import concourse.bacc as _bacc
    from concourse.bass_utils import run_bass_kernel_spmd as _run

    nc = _bacc.Bacc("TRN2", target_bir_lowering=False, num_devices=1)
    arrays = {"in_" + name: np.ascontiguousarray(value) for name, value in inputs.items()}
    arrays.update(shape_constants())
    tensors = {name[3:] if name.startswith("in_") else name:
               nc.dram_tensor(name, value.shape, F32, kind="ExternalInput").ap() for name, value in arrays.items()}
    tensors["w_scratch"] = nc.dram_tensor("w_scratch", (E, S), F32, kind="Internal").ap()
    out = nc.dram_tensor("out", (1, S, D), F32, kind="ExternalOutput").ap()
    program(nc, tensors, out)
    result = _run(nc, [arrays], core_ids=[0])
    return result.results[0]["out"]
```
